# Optimizing a Trainium2 kernel written in Bass

```python
import math
import jax
import jax.numpy as jnp
from jax import lax
import numpy as np

D_MODEL = 1024
BATCH = 1
SEQ = 512
DEPTH = 2
DEC_BATCH = 8
DEC_SEQ = 8
PAST_LEN = 512
PAGE_SIZE = 128

N_MIXERS = 2
N_ATTN_LAYERS = (DEPTH + 1) // 2
N_RNN_LAYERS = DEPTH // 2
N_HEADS = 16
HEAD_DIM = D_MODEL // N_HEADS
Q_BLOCK = 128
D_RNN = 1408
N_RNN_BLOCKS = 16
RNN_BLOCK = D_RNN // N_RNN_BLOCKS
RNN_CONV_W = 4
LRU_C = 8.0
D_FF = 3 * D_MODEL
FFN_CONV_W = 3
ALPHA = (2.0 * DEPTH) ** 0.25
BETA = (8.0 * DEPTH) ** -0.25
LN_EPS = 1e-5
FORGET_BIAS_INIT = 2.0

kernel_name = 'fox_rglru_convffn_deepnorm_step'

def layer_norm(x, g, b):
    xf = x.astype(jnp.float32)
    mu = jnp.mean(xf, axis=-1, keepdims=True)
    var = jnp.mean(jnp.square(xf - mu), axis=-1, keepdims=True)
    y = (xf - mu) * lax.rsqrt(var + LN_EPS) * g.astype(jnp.float32) + b.astype(jnp.float32)
    return y.astype(x.dtype)

def causal_dwconv(x_hist, w, b):
    width = w.shape[0]
    t = x_hist.shape[1] - (width - 1)
    out = b
    for j in range(width):
        out = out + x_hist[:, j:j + t] * w[j]
    return out

def fox_project(x, w_in, b_f):
    proj = jnp.einsum('btd,de->bte', x, w_in)
    q, k, v, f = jnp.split(proj, [D_MODEL, 2 * D_MODEL, 3 * D_MODEL], axis=-1)
    shp = x.shape[:2] + (N_HEADS, HEAD_DIM)
    logf = jax.nn.log_sigmoid((f + b_f).astype(jnp.float32))
    return q.reshape(shp), k.reshape(shp), v.reshape(shp), logf

def fox_attend(q, k, v, cum_q, cum_k, q_pos, k_pos):
    s = jnp.einsum('bqhd,bkhd->bhqk', q, k).astype(jnp.float32) * (HEAD_DIM ** -0.5)
    s = s + jnp.transpose(cum_q, (0, 2, 1))[..., :, None] - jnp.transpose(cum_k, (0, 2, 1))[..., None, :]
    mask = k_pos[None, :] <= q_pos[:, None]
    s = jnp.where(mask, s, -jnp.inf)
    p = jax.nn.softmax(s, axis=-1).astype(v.dtype)
    return jnp.einsum('bhqk,bkhd->bqhd', p, v)

def fox_prompt(x, w_in, b_f, w_o):
    b, t = x.shape[:2]
    q, k, v, logf = fox_project(x, w_in, b_f)
    cum = jnp.cumsum(logf, axis=1)
    k_pos = jnp.arange(t)

    def block(i):
        start = i * Q_BLOCK
        qb = lax.dynamic_slice_in_dim(q, start, Q_BLOCK, axis=1)
        cb = lax.dynamic_slice_in_dim(cum, start, Q_BLOCK, axis=1)
        return fox_attend(qb, k, v, cb, cum, start + jnp.arange(Q_BLOCK), k_pos)

    o = lax.map(block, jnp.arange(t // Q_BLOCK))
    o = jnp.moveaxis(o, 0, 1).reshape(b, t, D_MODEL)
    return jnp.einsum('btd,de->bte', o, w_o), k, v, logf

def fox_sample(x, cache_k, cache_v, cache_logf, page_table, layer, w_in, b_f, w_o):
    db, ds = x.shape[:2]
    past = page_table.shape[1] * PAGE_SIZE
    q, k, v, logf = fox_project(x, w_in, b_f)
    k_past = cache_k[page_table, :, layer].reshape(db, past, N_HEADS, HEAD_DIM)
    v_past = cache_v[page_table, :, layer].reshape(db, past, N_HEADS, HEAD_DIM)
    lf_past = cache_logf[page_table, :, layer].reshape(db, past, N_HEADS)
    k_all = jnp.concatenate([k_past.astype(k.dtype), k], axis=1)
    v_all = jnp.concatenate([v_past.astype(v.dtype), v], axis=1)
    cum = jnp.cumsum(jnp.concatenate([lf_past.astype(jnp.float32), logf], axis=1), axis=1)
    o = fox_attend(q, k_all, v_all, cum[:, past:], cum, past + jnp.arange(ds), jnp.arange(past + ds))
    return jnp.einsum('btd,de->bte', o.reshape(db, ds, D_MODEL), w_o), k, v, logf

def rglru_block(x, conv_hist, h0, w_in, conv_w, conv_b, w_a, b_a, w_i, b_i, lam, w_out):
    proj = jnp.einsum('btd,de->bte', x, w_in)
    y_branch, x_branch = jnp.split(proj, 2, axis=-1)
    gate = jax.nn.gelu(y_branch, approximate=True)
    xh = jnp.concatenate([conv_hist.astype(x_branch.dtype), x_branch], axis=1)
    new_hist = xh[:, xh.shape[1] - (RNN_CONV_W - 1):]
    xc = causal_dwconv(xh, conv_w, conv_b)
    xb = xc.reshape(xc.shape[:2] + (N_RNN_BLOCKS, RNN_BLOCK))
    r = jax.nn.sigmoid((jnp.einsum('btnk,nkj->btnj', xb, w_a).reshape(xc.shape) + b_a).astype(jnp.float32))
    i = jax.nn.sigmoid((jnp.einsum('btnk,nkj->btnj', xb, w_i).reshape(xc.shape) + b_i).astype(jnp.float32))
    log_a = -LRU_C * r * jax.nn.softplus(-lam.astype(jnp.float32))
    a = jnp.exp(log_a)
    u = jnp.sqrt(-jnp.expm1(2.0 * log_a)) * i * xc.astype(jnp.float32)

    def step(h, au):
        a_t, u_t = au
        h = a_t * h + u_t
        return h, h

    h_last, hs = lax.scan(step, h0.astype(jnp.float32), (jnp.swapaxes(a, 0, 1), jnp.swapaxes(u, 0, 1)))
    hs = jnp.swapaxes(hs, 0, 1).astype(x.dtype)
    out = jnp.einsum('btr,rd->btd', hs * gate, w_out)
    return out, h_last, new_hist

def conv_ffn(x, g_hist, w_in, conv_w, conv_b, w_out):
    proj = jnp.einsum('btd,de->bte', x, w_in)
    g, u = jnp.split(proj, 2, axis=-1)
    gh = jnp.concatenate([g_hist.astype(g.dtype), g], axis=1)
    new_hist = gh[:, gh.shape[1] - (FFN_CONV_W - 1):]
    h = jax.nn.gelu(causal_dwconv(gh, conv_w, conv_b), approximate=True) * u
    return jnp.einsum('btf,fd->btd', h, w_out), new_hist

def setup_inputs(seed: int = 0) -> dict:
    key = jax.random.key(seed)
    ks = jax.random.split(key, 32)
    f32 = jnp.float32
    n_pages = PAST_LEN // PAGE_SIZE
    n_used = DEC_BATCH * n_pages
    n_pool = n_used + max(1, n_used // 4)

    def nrm(k, shape, scale):
        return jax.random.normal(k, shape, f32) * scale

    x_prompt = nrm(ks[0], (BATCH, SEQ, D_MODEL), 1.0)
    x_sample = nrm(ks[1], (DEC_BATCH, DEC_SEQ, D_MODEL), 1.0)
    cache_k = nrm(ks[2], (n_pool, PAGE_SIZE, N_ATTN_LAYERS, N_HEADS, HEAD_DIM), 1.0)
    cache_v = nrm(ks[3], (n_pool, PAGE_SIZE, N_ATTN_LAYERS, N_HEADS, HEAD_DIM), BETA)
    cache_logf = jax.nn.log_sigmoid(FORGET_BIAS_INIT + nrm(ks[4], (n_pool, PAGE_SIZE, N_ATTN_LAYERS, N_HEADS), 1.0))
    page_table = jax.random.permutation(ks[5], n_pool)[:n_used].reshape(DEC_BATCH, n_pages).astype(jnp.int32)
    state_rglru_h = nrm(ks[6], (N_RNN_LAYERS, DEC_BATCH, D_RNN), 0.5)
    state_rglru_conv = nrm(ks[7], (N_RNN_LAYERS, DEC_BATCH, RNN_CONV_W - 1, D_RNN), 1.0)
    state_ffn_conv = nrm(ks[8], (DEPTH, DEC_BATCH, FFN_CONV_W - 1, D_FF), 1.0)
    ln_g = 1.0 + nrm(ks[9], (DEPTH, 2, D_MODEL), 0.02)
    ln_b = nrm(ks[10], (DEPTH, 2, D_MODEL), 0.02)
    w_qk = nrm(ks[11], (N_ATTN_LAYERS, D_MODEL, 2 * D_MODEL), D_MODEL ** -0.5)
    w_v = nrm(ks[12], (N_ATTN_LAYERS, D_MODEL, D_MODEL), D_MODEL ** -0.5 * BETA)
    w_f = nrm(ks[13], (N_ATTN_LAYERS, D_MODEL, N_HEADS), D_MODEL ** -0.5)
    w_attn_in = jnp.concatenate([w_qk, w_v, w_f], axis=-1)
    b_forget = FORGET_BIAS_INIT + nrm(ks[14], (N_ATTN_LAYERS, N_HEADS), 0.1)
    w_attn_out = nrm(ks[15], (N_ATTN_LAYERS, D_MODEL, D_MODEL), D_MODEL ** -0.5 * BETA)
    w_rnn_in = nrm(ks[16], (N_RNN_LAYERS, D_MODEL, 2 * D_RNN), D_MODEL ** -0.5)
    rnn_conv_w = nrm(ks[17], (N_RNN_LAYERS, RNN_CONV_W, D_RNN), RNN_CONV_W ** -0.5)
    rnn_conv_b = nrm(ks[18], (N_RNN_LAYERS, D_RNN), 0.01)
    w_rg_a = nrm(ks[19], (N_RNN_LAYERS, N_RNN_BLOCKS, RNN_BLOCK, RNN_BLOCK), RNN_BLOCK ** -0.5)
    b_rg_a = nrm(ks[20], (N_RNN_LAYERS, D_RNN), 0.01)
    w_rg_i = nrm(ks[21], (N_RNN_LAYERS, N_RNN_BLOCKS, RNN_BLOCK, RNN_BLOCK), RNN_BLOCK ** -0.5)
    b_rg_i = nrm(ks[22], (N_RNN_LAYERS, D_RNN), 0.01)
    a_c = jax.random.uniform(ks[23], (N_RNN_LAYERS, D_RNN), f32, 0.9, 0.999)
    base = a_c ** (1.0 / LRU_C)
    rg_lambda = jnp.log(base) - jnp.log1p(-base)
    w_rnn_out = nrm(ks[24], (N_RNN_LAYERS, D_RNN, D_MODEL), D_RNN ** -0.5 * BETA)
    w_ffn_in = nrm(ks[25], (DEPTH, D_MODEL, 2 * D_FF), D_MODEL ** -0.5)
    ffn_conv_w = nrm(ks[26], (DEPTH, FFN_CONV_W, D_FF), FFN_CONV_W ** -0.5)
    ffn_conv_b = nrm(ks[27], (DEPTH, D_FF), 0.01)
    w_ffn_out = nrm(ks[28], (DEPTH, D_FF, D_MODEL), D_FF ** -0.5 * BETA)
    return {
        'x_prompt': x_prompt, 'x_sample': x_sample,
        'cache_k': cache_k, 'cache_v': cache_v, 'cache_logf': cache_logf,
        'page_table': page_table,
        'state_rglru_h': state_rglru_h, 'state_rglru_conv': state_rglru_conv,
        'state_ffn_conv': state_ffn_conv,
        'ln_g': ln_g, 'ln_b': ln_b,
        'w_attn_in': w_attn_in, 'b_forget': b_forget, 'w_attn_out': w_attn_out,
        'w_rnn_in': w_rnn_in, 'rnn_conv_w': rnn_conv_w, 'rnn_conv_b': rnn_conv_b,
        'w_rg_a': w_rg_a, 'b_rg_a': b_rg_a, 'w_rg_i': w_rg_i, 'b_rg_i': b_rg_i,
        'rg_lambda': rg_lambda, 'w_rnn_out': w_rnn_out,
        'w_ffn_in': w_ffn_in, 'ffn_conv_w': ffn_conv_w, 'ffn_conv_b': ffn_conv_b,
        'w_ffn_out': w_ffn_out,
    }

def reference(x_prompt, x_sample, cache_k, cache_v, cache_logf, page_table,
              state_rglru_h, state_rglru_conv, state_ffn_conv,
              ln_g, ln_b, w_attn_in, b_forget, w_attn_out,
              w_rnn_in, rnn_conv_w, rnn_conv_b, w_rg_a, b_rg_a, w_rg_i, b_rg_i,
              rg_lambda, w_rnn_out, w_ffn_in, ffn_conv_w, ffn_conv_b, w_ffn_out):
    xp, xs = x_prompt, x_sample
    bp = xp.shape[0]
    kp_l, vp_l, fp_l, ks_l, vs_l, fs_l = [], [], [], [], [], []
    hp_l, hs_l, rcp_l, rcs_l, gcp_l, gcs_l = [], [], [], [], [], []
    for i in range(DEPTH):
        if i % N_MIXERS == 0:
            a = i // N_MIXERS
            op, kp, vp, lfp = fox_prompt(xp, w_attn_in[a], b_forget[a], w_attn_out[a])
            osm, ksm, vsm, lfs = fox_sample(xs, cache_k, cache_v, cache_logf, page_table, a,
                                            w_attn_in[a], b_forget[a], w_attn_out[a])
            kp_l.append(kp); vp_l.append(vp); fp_l.append(lfp)
            ks_l.append(ksm); vs_l.append(vsm); fs_l.append(lfs)
        else:
            r = i // N_MIXERS
            rnn_w = (w_rnn_in[r], rnn_conv_w[r], rnn_conv_b[r], w_rg_a[r], b_rg_a[r],
                     w_rg_i[r], b_rg_i[r], rg_lambda[r], w_rnn_out[r])
            op, hp, rcp = rglru_block(xp, jnp.zeros((bp, RNN_CONV_W - 1, D_RNN), xp.dtype),
                                      jnp.zeros((bp, D_RNN), jnp.float32), *rnn_w)
            osm, hsm, rcs = rglru_block(xs, state_rglru_conv[r], state_rglru_h[r], *rnn_w)
            hp_l.append(hp); hs_l.append(hsm); rcp_l.append(rcp); rcs_l.append(rcs)
        xp = layer_norm(ALPHA * xp + op, ln_g[i, 0], ln_b[i, 0])
        xs = layer_norm(ALPHA * xs + osm, ln_g[i, 0], ln_b[i, 0])
        fp, gcp = conv_ffn(xp, jnp.zeros((bp, FFN_CONV_W - 1, D_FF), xp.dtype),
                           w_ffn_in[i], ffn_conv_w[i], ffn_conv_b[i], w_ffn_out[i])
        fsm, gcs = conv_ffn(xs, state_ffn_conv[i], w_ffn_in[i], ffn_conv_w[i], ffn_conv_b[i], w_ffn_out[i])
        gcp_l.append(gcp); gcs_l.append(gcs)
        xp = layer_norm(ALPHA * xp + fp, ln_g[i, 1], ln_b[i, 1])
        xs = layer_norm(ALPHA * xs + fsm, ln_g[i, 1], ln_b[i, 1])
    k_prompt = jnp.stack(kp_l, axis=2)
    v_prompt = jnp.stack(vp_l, axis=2)
    logf_prompt = jnp.stack(fp_l, axis=2)
    k_sample = jnp.stack(ks_l, axis=2)
    v_sample = jnp.stack(vs_l, axis=2)
    logf_sample = jnp.stack(fs_l, axis=2)
    h_prompt = jnp.stack(hp_l, axis=0)
    h_sample = jnp.stack(hs_l, axis=0)
    rconv_prompt = jnp.stack(rcp_l, axis=0)
    rconv_sample = jnp.stack(rcs_l, axis=0)
    fconv_prompt = jnp.stack(gcp_l, axis=0)
    fconv_sample = jnp.stack(gcs_l, axis=0)
    return (xp, xs, k_prompt, v_prompt, logf_prompt, k_sample, v_sample, logf_sample,
            h_prompt, h_sample, rconv_prompt, rconv_sample, fconv_prompt, fconv_sample)


_drawn_inputs = setup_inputs


def setup_inputs(seed=0):
    import zlib

    import numpy as np

    out = dict(_drawn_inputs(seed))
    spreads = {}
    factors = {'cache_logf': 5.169, 'b_rg_a': 8.0, 'b_rg_i': 8.0, 'ffn_conv_b': 8.0}
    for name, (base, spread) in spreads.items():
        noise = np.random.default_rng([zlib.crc32(name.encode()), seed]).standard_normal(out[name].shape)
        drawn = base * np.exp(spread * noise) if base else spread * noise
        out[name] = jnp.asarray(drawn.astype(out[name].dtype))
    for name, factor in factors.items():
        out[name] = (out[name] * factor).astype(out[name].dtype)
    return out
```

```python
import concourse.bass as bass
from concourse import mybir
from contextlib import ExitStack

P = 128
D = 1024
KD = D // P
TP, NB, TQ = 512, 8, 8
TS = NB * TQ
T = TP + TS
HT = T // 2
NQ = TP // P
NH, HD = 16, 64
NPAIR = NH // 2
NPG = 4
PAST = NPG * P
FF = 3 * D
NF = FF // P
GF = 4
NG = NF // GF
R = 1408
NR = R // P
RB = 88
ALPHA = 4.0 ** 0.25
EPS = 1e-5
NEG = -3.0e38
SW = PAST + TS
GHW = 2 + TP + NB * (2 + TQ)
CVW = GHW - 2
XRW = 3 + TP + NB * (3 + TQ)
CXW = XRW - 3
RING = 3
SLOT = KD * P

N_QKV = 0
N_AO = N_QKV + 3 * NPAIR
N_F0 = N_AO + KD
N_RI = N_F0 + 12 * NG
N_RO = N_RI + 2 * NR
N_F1 = N_RO + 12
N_END = N_F1 + 12 * NG
M_AO = 3 * NPAIR
M_F0 = M_AO + KD
M_RI = M_F0 + 16 * NG
M_F1 = M_RI + 2 * NR
Z_AO = 0
Z_F0 = KD
Z_RO = Z_F0 + NG * KD
Z_F1 = Z_RO + KD

C_LNG, C_LNB = 0, 32
C_RCB, C_RBA, C_RBI, C_LAM = 64, 75, 86, 97
C_RCW = 128
C_FCB = C_RCW + 4 * NR
C_FCW = (256, 384)


class At:

    def __init__(self, first, step=0, turn=None):
        self.first, self.step, self.turn = first, step, turn

    def __add__(self, k):
        return At(self.first + k, self.step, self.turn)

    def times(self, k, plus=0):
        return At(self.first * k + plus, self.step * k, self.turn)

    @property
    def v(self):
        return self.first if self.turn is None else self.turn * self.step + self.first

    def slot(self, r):
        assert self.turn is None or self.step % r == 0
        return self.first % r

    def round(self, r):
        return At(self.first // r, self.step // r, self.turn)


def wait(engine, sem, value):
    if isinstance(value, At):
        value = value.v
    if isinstance(value, int) and value <= 0:
        return
    engine.wait_ge(sem, value)


def build(nc, a):
    f32, f32r, i32 = mybir.dt.float32, mybir.dt.float32r, mybir.dt.int32
    ALU, ACT, AX = mybir.AluOpType, mybir.ActivationFunctionType, mybir.AxisListType
    ds = bass.ds
    ctx = ExitStack()
    with ctx:
        sems = {}

        def S(name):
            if name not in sems:
                sems[name] = ctx.enter_context(nc.semaphore(name))
            return sems[name]

        base = 16512
        top = [base]

        def sb(name, shape, dt=f32, at=None):
            size = 4
            for n in shape[1:]:
                size *= n
            size = (size + 31) // 32 * 32
            if at is None:
                off = top[0]
                top[0] += size
            else:
                off = at[0]
                at[0] += size
            assert off + size <= 229376, (name, off + size)
            return nc.alloc_sbuf_tensor_at(name, shape, dt, offset=off)

        ident = sb("ident", [P, P])
        over_d = sb("over_d", [P, P])
        prm = sb("prm", [P, 512])
        hist_f = sb("hist_f", [P, NF, 32])
        hist_r = sb("hist_r", [P, NR, 32])
        cols = sb("cols", [P, 8])
        lru_c = sb("lru_c", [P, NR])
        half_b = sb("half_b", [P, 2 * NR])
        x_f = sb("x_f", [P, KD, T])
        w_raw = sb("w_raw", [P, RING, SLOT])
        w_hi = sb("w_hi", [P, RING, SLOT], f32r)
        w_lo = sb("w_lo", [P, RING, SLOT], f32r)
        xhl_at = [top[0]]
        x_hi = sb("x_hi", [P, KD, T], f32r)
        x_lo = sb("x_lo", [P, KD, T], f32r)
        phase = top[0]

        at = [phase]
        o_hi = sb("o_hi", [P, KD, T], f32r, at)
        o_lo = sb("o_lo", [P, KD, T], f32r, at)
        v_new = sb("v_new", [P, D], f32, at)
        qT_s = sb("qT_s", [P, NPAIR, TS], f32, at)
        kT_s = sb("kT_s", [P, NPAIR, TS], f32, at)
        lf_pg = sb("lf_pg", [P, NPG, NB, NH], f32, at)
        lf_s = sb("lf_s", [P, PAST + TQ], f32, at)
        head_of = sb("head_of", [P, NH, TQ], f32, at)
        batch_of = sb("batch_of", [P, NB], f32, at)
        new_mask = sb("new_mask", [P, NB * 72], f32, at)
        causal_w = sb("causal_w", [P, NH, TQ], f32, at)
        ones_s = sb("ones_s", [P, PAST + TQ], f32, at)
        pages = sb("pages", [1, NB * NPG], i32, at)
        bf_col = sb("bf_col", [NH, 1], f32, at)
        pair_at = at[0]
        q_sb = sb("q_sb", [P, 2, T], f32, at)
        k_sb = sb("k_sb", [P, 2, T], f32, at)
        v_sb = sb("v_sb", [P, T], f32, at)
        v_tok = sb("v_tok", [P, 2, NQ, P], f32, at)
        k_tok = sb("k_tok", [P, NQ, P], f32, at)
        k_new = sb("k_new", [TS, P], f32, at)
        ncb = sb("ncb", [P, 2, TP], f32, at)
        ncbm = sb("ncbm", [P, 2, TP], f32, at)
        mask4 = sb("mask4", [P, NQ, P], f32, at)
        cumq = sb("cumq", [P, NQ, NH], f32, at)
        lf_tok = sb("lf_tok", [P, NQ + 1, NH], f32, at)
        sc = sb("sc", [P, 2, TP], f32, at)
        pr = sb("pr", [P, 2, TP], f32, at)
        prT = sb("prT", [P, NQ, TP], f32, at)
        sm = sb("sm", [P, 3, 2], f32, at)
        at0 = [pair_at]
        x_in = sb("x_in", [P, NQ + 1, D], f32, at0)
        assert at0[0] <= 229376
        at1 = [phase]
        prow = sb("prow", [P, 4, P], f32, at1)
        frow = sb("frow", [32, FF], f32, at1)
        rrow = sb("rrow", [32, R], f32, at1)
        wf = sb("wf", [P, KD, NH], f32, at1)
        fz = sb("fz", [NH, 7, T], f32, at1)
        assert at1[0] <= phase + 2 * KD * T * 4
        k_pg = sb("k_pg", [P, 2, NPG, D], f32, xhl_at)
        at2 = [pair_at]
        v_pg = sb("v_pg", [P, 2, NPG, D], f32, at2)
        kT = sb("kT", [P, 2, PAST], f32, xhl_at)
        assert xhl_at[0] <= phase
        qz = sb("qz", [P, 2, KD * 144], f32, at2)
        e_b = sb("e_b", [P, 2, P], f32, at2)
        nc_s = sb("nc_s", [P, PAST + TQ], f32, at2)
        cq_w = sb("cq_w", [P, NH, TQ], f32, at2)
        cq_s = sb("cq_s", [P, NB], f32, at2)
        ss = sb("ss", [P, 2, SW], f32, at2)
        ps_ = sb("ps_", [P, 2, SW], f32, at2)
        psT = sb("psT", [P, NPG + 1, P], f32, at2)
        sms = sb("sms", [P, 3, 2], f32, at2)

        def norm_space(at, tag):
            return sb("ln_sq" + tag, [P, 2, T], f32, at), sb("ln_rstd" + tag, [P, 2, T], f32, at)

        atf = [phase]
        gh = sb("gh", [P, 2, GHW], f32, atf)
        cv = sb("cv", [P, CVW], f32, atf)
        gl = sb("gl", [P, GHW], f32, atf)
        hf = sb("hf", [P, T], f32, atf)
        h_hi = sb("h_hi", [P, 2, GF, T], f32r, atf)
        h_lo = sb("h_lo", [P, 2, GF, T], f32r, atf)
        f_st = sb("f_st", [P, NF, 2 + 2 * NB], f32, atf)
        f_rows = sb("f_rows", [2 + 2 * NB, FF], f32, atf)
        ln_f = norm_space(atf, "f")

        atr = [phase]
        r_hi = sb("r_hi", [P, NR, T], f32r, atr)
        r_lo = sb("r_lo", [P, NR, T], f32r, atr)
        r_end = atr[0]
        gate = sb("gate", [P, 3, T], f32, atr)
        xr = sb("xr", [P, 3, XRW], f32, atr)
        cx = sb("cx", [P, XRW], f32, atr)
        xc = sb("xc", [P, 3, T], f32, atr)
        tr = sb("tr", [P, T], f32, atr)
        ti = sb("ti", [P, T], f32, atr)
        om = sb("om", [P, T], f32, atr)
        sq = sb("sq", [P, T], f32, atr)
        aa = sb("aa", [P, T], f32, atr)
        uu = sb("uu", [P, T], f32, atr)
        rgw = sb("rgw", [P, 3, 3, 2, P], f32, atr)
        r_st = sb("r_st", [P, NR, 36], f32, atr)
        r_rows = sb("r_rows", [36, R], f32, [r_end])
        ln_r = norm_space([r_end + 8192], "r")
        y_tok = sb("y_tok", [P, 2, D], f32, [phase])

        ps = ctx.enter_context(nc.psum_tensor("ps", [P, 8, 512], f32))
        block = ctx.enter_context(nc.Block())

        def acc(m):
            b = 2 * m.slot(2)
            return ps[:, b:b + 2, 0:HT]

        def halves(x):
            return x.rearrange("p (a t) -> p a t", a=2)

        def bank_pair(b):
            return ps[:, b:b + 2, 0:HT]

        def prompt_parts(b):
            return [(ps[:, b, 0:HT], 0, HT), (ps[:, b + 1, 0:TP - HT], HT, TP)]

        def strided(x, first, step):
            return x[:, first:first + NB * step].rearrange("p (b c) -> p b c", c=step)[:, :, 0:TQ]

        xp = a["x_prompt"].rearrange("a (t p) d -> p (a t) d", p=P)
        xs = a["x_sample"].rearrange("a b d -> (a b) d")
        w_qkv = a["w_attn_in"].rearrange("a (k p) e -> p (a k) e", p=P)
        w_ao = a["w_attn_out"].rearrange("a (k p) e -> p (a k) e", p=P)
        w_ri = a["w_rnn_in"].rearrange("a (k p) e -> p (a k) e", p=P)
        w_ro = a["w_rnn_out"].rearrange("a (k p) e -> p (a k) e", p=P)
        w_fi = a["w_ffn_in"].rearrange("l (k p) e -> l p k e", p=P)
        w_fo = a["w_ffn_out"].rearrange("l (k p) e -> l p k e", p=P)
        ck = a["cache_k"].rearrange("n p a h d -> n p (a h d)")
        cvv = a["cache_v"].rearrange("n p a h d -> n p (a h d)")
        clf = a["cache_logf"].rearrange("n p a h -> n p (a h)")
        kp_o = a["k_prompt"].rearrange("a (t p) l h d -> p (a t) (l h d)", p=P)
        vp_o = a["v_prompt"].rearrange("a (t p) l h d -> p (a t) (l h d)", p=P)
        ks_o = a["k_sample"].rearrange("b q l h d -> (b q) (l h d)")
        vs_o = a["v_sample"].rearrange("b q l h d -> (b q) (l h d)")
        lp_o = a["logf_prompt"].rearrange("a (t p) l h -> p (a t) (l h)", p=P)
        ls_o = a["logf_sample"].rearrange("b q l h -> (b q) (l h)")
        yp_o = a["y_prompt"].rearrange("a (t p) d -> (a t) p d", p=P)
        ys_o = a["y_sample"].rearrange("a b d -> (a b) d")
        ncum_d = nc.dram_tensor("ncum_scratch", [NH, TP], f32, kind="Internal").ap()

        def load(sp, n, dst_cols, src):
            s = n.slot(RING)
            wait(sp, S("w_lo_ready"), n + (1 - RING))
            dst = w_raw[:, s, 0:dst_cols]
            k = src.shape[1]
            sp.dma_start(dst.rearrange("p (k e) -> p k e", k=k), src).then_inc(S(f"w_raw{s}"), 16)

        def split_hi(act, n, m_done, width=SLOT):
            s = n.slot(RING)
            wait(act, S(f"w_raw{s}"), n.round(RING).times(16, 16))
            if m_done is not None:
                wait(act, *m_done)
            nc.scalar.copy(w_hi[:, s, 0:width], w_raw[:, s, 0:width]).then_inc(S("w_hi_ready"), 1)

        def split_lo(dve, n, width=SLOT):
            s = n.slot(RING)
            wait(dve, S("w_hi_ready"), n + 1)
            nc.vector.tensor_tensor(w_lo[:, s, 0:width], w_raw[:, s, 0:width],
                                    w_hi[:, s, 0:width].bitcast(f32), ALU.subtract).then_inc(S("w_lo_ready"), 1)

        def width_of(n):
            first = n.first
            return 3 * 2 * P if N_RO <= first < N_F1 and (first - N_RO) % 3 == 2 else SLOT

        def products(pe, n, out, terms, half, first=True, last=True):
            s = n.slot(RING)
            for i, (t, hi, lo) in enumerate(terms):
                w_h, w_l = w_hi[:, s, t * P:(t + 1) * P], w_lo[:, s, t * P:(t + 1) * P]
                r = slice(half * HT, (half + 1) * HT)
                nc.tensor.matmul(out, w_h, hi[:, r], start=first and i == 0, stop=False)
                nc.tensor.matmul(out, w_h, lo[:, r], start=False, stop=False)
                done = nc.tensor.matmul(out, w_l, hi[:, r], start=False, stop=last and i == len(terms) - 1)
            return done

        def x_terms():
            return [(k, x_hi[:, k, :], x_lo[:, k, :]) for k in range(KD)]

        def unit_half(pe, n, m, half, terms):
            b = 2 * m.slot(2) + half
            return products(pe, n, ps[:, b, 0:HT], terms, half)

        @block.sync
        def _(sp):
            sp.dma_start(x_in[:, 0:NQ, :], xp).then_inc(S("x_in"), 16)
            sp.dma_start(x_in[0:TS, NQ, :], xs).then_inc(S("x_in"), 16)
            sp.dma_start(wf[:], w_qkv[:, :, 3 * D:3 * D + NH]).then_inc(S("wf_in"), 16)
            sp.dma_start(bf_col[:], a["b_forget"].rearrange("a h -> h a")).then_inc(S("wf_in"), 16)

            def qkv(j, n):
                for c in range(3):
                    load(sp, n + c, SLOT, w_qkv[:, :, ds((j.times(P) + c * D).v, P)])

            qkv(At(0), At(N_QKV))

            def rows(blk, r0, n, src):
                sp.dma_start(prow[r0:r0 + n, blk, :], src).then_inc(S("prm_in"), 16)

            rows(0, C_LNG, 32, a["ln_g"].rearrange("l s (k p) -> (l s k) p", p=P))
            rows(0, C_LNB, 32, a["ln_b"].rearrange("l s (k p) -> (l s k) p", p=P))
            rows(0, C_RCB, NR, a["rnn_conv_b"].rearrange("l (k p) -> (l k) p", p=P))
            rows(0, C_RBA, NR, a["b_rg_a"].rearrange("l (k p) -> (l k) p", p=P))
            rows(0, C_RBI, NR, a["b_rg_i"].rearrange("l (k p) -> (l k) p", p=P))
            rows(0, C_LAM, NR, a["rg_lambda"].rearrange("l (k p) -> (l k) p", p=P))
            rows(1, 0, 4 * NR, a["rnn_conv_w"].rearrange("l w (k p) -> (l w k) p", p=P))
            rows(1, 4 * NR, 2 * NF, a["ffn_conv_b"].rearrange("l (k p) -> (l k) p", p=P))
            for l in range(2):
                rows(2 + l, 0, 3 * NF, a["ffn_conv_w"][l].rearrange("w (k p) -> (w k) p", p=P))
            sp.dma_start(frow[:], a["state_ffn_conv"].rearrange("l b w f -> (l b w) f")).then_inc(S("prm_in"), 16)
            sp.dma_start(rrow[0:24, :], a["state_rglru_conv"].rearrange("l b w f -> (l b w) f")).then_inc(S("prm_in"), 16)
            sp.dma_start(rrow[24:32, :], a["state_rglru_h"].rearrange("l b f -> (l b) f")).then_inc(S("prm_in"), 16)

            with sp.Fori(0, NPAIR - 1) as i:
                qkv(At(1, 1, i), At(3, 3, i))
            for j in range(RING):
                load(sp, At(N_AO + j), SLOT, w_ao[:, :, P * j:P * (j + 1)])

            sp.wait_ge(S("pages_in"), 16)

            def page_loads(b):
                s = b.slot(2)
                if b.first < 2 and b.turn is None:
                    sp.wait_ge(S("acc_full"), M_AO)
                    sp.wait_ge(S("o_lo_ready"), NPAIR)
                    sp.wait_ge(S("kv_stored"), 64 * NPAIR)
                    sp.wait_ge(S("qk_kept"), 2 * NPAIR)
                else:
                    sp.wait_ge(S("s_full"), (b + (-1)).v)
                    sp.wait_ge(S("pv_s_done"), (b + (-1)).v)
                for t in range(NPG):
                    pg = sp.value_load(pages[0:1, ds(b.times(NPG, t).v, 1)], min_val=0, max_val=39)
                    sp.dma_start(k_pg[:, s, t, :], ck[ds(pg, 1)].rearrange("n p e -> (n p) e")).then_inc(S(f"k_pg{s}"), 16)
                    sp.dma_start(v_pg[:, s, t, :], cvv[ds(pg, 1)].rearrange("n p e -> (n p) e")).then_inc(S(f"v_pg{s}"), 16)

            page_loads(At(0))
            page_loads(At(1))
            with sp.Fori(0, NB // 2 - 1) as i:
                page_loads(At(2, 2, i))
                page_loads(At(3, 2, i))

            for j in range(RING, KD):
                load(sp, At(N_AO + j), SLOT, w_ao[:, :, P * j:P * (j + 1)])

            def ffn(l, n0):
                def pair(F, n):
                    load(sp, n, SLOT, w_fi[l, :, :, ds(F.times(P).v, P)])
                    load(sp, n + 1, SLOT, w_fi[l, :, :, ds(F.times(P, FF).v, P)])

                def group(g, more):
                    n = g.times(12, n0 + 2)
                    for f in range(1, GF):
                        pair(g.times(GF, f), n + 2 * (f - 1))
                    if more:
                        pair(g.times(GF, GF), n + 6)
                    for c in range(4):
                        load(sp, n + ((8 if more else 6) + c), SLOT,
                             w_fo[l, :, ds(g.times(GF).v, GF), 2 * P * c:2 * P * (c + 1)])

                pair(At(0), At(n0))
                with sp.Fori(0, NG - 1) as i:
                    group(At(0, 1, i), True)
                group(At(NG - 1), False)

            ffn(0, N_F0)

            def rnn_in(j, n):
                load(sp, n, SLOT, w_ri[:, :, ds(j.times(P).v, P)])
                load(sp, n + 1, SLOT, w_ri[:, :, ds(j.times(P, R).v, P)])

            rnn_in(At(0), At(N_RI))
            rnn_in(At(1), At(N_RI + 2))
            with sp.Fori(0, 3) as i:
                for u in range(3):
                    rnn_in(At(2 + u, 3, i), At(N_RI + 4 + 2 * u, 6, i))
            for q in range(4):
                for c in range(3):
                    n = At(N_RO + 3 * q + c)
                    load(sp, n, width_of(n), w_ro[:, 4 * c:min(4 * c + 4, NR), 2 * P * q:2 * P * (q + 1)])
            ffn(1, N_F1)

        def scale_residual(pool, k):
            for j in range(KD):
                pool.wait_ge(S("x_lo_ready"), KD * k + j + 1)
                nc.gpsimd.tensor_scalar(x_f[:, j, :], x_f[:, j, :], ALPHA, 1.0, ALU.mult, ALU.mult
                                        ).then_inc(S("x_scaled"), 1)

        def ffn_pool(pool, l):
            nc.gpsimd.memset(gh[:, :, 0:2], 0.0).then_inc(S("gh_zero"), 1)

            def tile(F):
                Fg = F + NF * l
                s = F.slot(2)
                seq = gh[:, s, 2 + TP:GHW].rearrange("p (b c) -> p b c", c=2 + TQ)
                wait(pool, S("cv_tap"), Fg.times(3, -3))
                nc.gpsimd.tensor_copy(seq[:, :, 0:2],
                                      hist_f[:, ds(F.v, 1), 16 * l:16 * l + 16].rearrange("p o (b c) -> p (o b) c", c=2)
                                      ).then_inc(S("gh_hist"), 1)
                wait(pool, S("gh_ready"), Fg + 1)
                nc.gpsimd.tensor_copy(f_st[:, ds(F.v, 1), 0:2], gh[:, s, TP:TP + 2].rearrange("p (o c) -> p o c", o=1))
                nc.gpsimd.tensor_copy(f_st[:, ds(F.v, 1), 2:18].rearrange("p o (b c) -> p (o b) c", c=2),
                                      seq[:, :, TQ:TQ + 2]).then_inc(S("gh_kept"), 1)

            tile(At(0))
            tile(At(1))
            with pool.Fori(0, NF // 2 - 1) as i:
                tile(At(2, 2, i))
                tile(At(3, 2, i))
            pool.wait_ge(S("rows_ready"), (6, 15)[l])
            pool.dma_start(a["fconv_prompt"][l].rearrange("b w f -> (b w) f"), f_rows[0:2, :]).then_inc(S("rows_stored"), 16)
            pool.dma_start(a["fconv_sample"][l].rearrange("b w f -> (b w) f"), f_rows[2:18, :]).then_inc(S("rows_stored"), 16)

        @block.gpsimd
        def _(pool):
            link_n = [0]

            def link(ins):
                link_n[0] += 1
                ins.then_inc(S("pool_step"), 1)
                pool.wait_ge(S("pool_step"), link_n[0])

            link(nc.gpsimd.memset(ident[:], 0.0))
            nc.gpsimd.affine_select(out=ident[:], in_=ident[:], compare_op=ALU.not_equal, fill=1.0, base=0,
                                    pattern=[[-1, P]], channel_multiplier=1).then_inc(S("ident_ready"), 1)
            pool.dma_start(pages[:], a["page_table"].rearrange("b (o t) -> o (b t)", o=1)).then_inc(S("pages_in"), 16)
            nc.gpsimd.memset(cols[:, 0:1], EPS)
            nc.gpsimd.memset(cols[:, 1:2], 2.0 ** -116)
            nc.gpsimd.memset(ones_s[:], 1.0)
            link(nc.gpsimd.memset(over_d[:], 1.0 / D))
            link(nc.gpsimd.memset(head_of[:], 0.0))
            for b in range(NB):
                link(nc.gpsimd.affine_select(out=head_of[:], in_=head_of[:], compare_op=ALU.not_equal, fill=1.0,
                                             base=-NH * b, pattern=[[-1, NH], [0, TQ]], channel_multiplier=1))
            link(nc.gpsimd.memset(batch_of[:], 1.0))
            link(nc.gpsimd.affine_select(out=batch_of[:], in_=batch_of[:], compare_op=ALU.is_ge, fill=0.0, base=0,
                                         pattern=[[-NH, NB]], channel_multiplier=1))
            link(nc.gpsimd.affine_select(out=batch_of[:], in_=batch_of[:], compare_op=ALU.is_ge, fill=0.0,
                                         base=NH - 1, pattern=[[NH, NB]], channel_multiplier=-1))
            link(nc.gpsimd.memset(causal_w[:], 0.0))
            link(nc.gpsimd.affine_select(out=causal_w[:], in_=causal_w[:], compare_op=ALU.is_ge, fill=NEG, base=0,
                                         pattern=[[-TQ, NH], [-1, TQ]], channel_multiplier=1))
            link(nc.gpsimd.affine_select(out=causal_w[:], in_=causal_w[:], compare_op=ALU.is_ge, fill=NEG,
                                         base=TQ - 1, pattern=[[TQ, NH], [0, TQ]], channel_multiplier=-1))
            nc.gpsimd.memset(v_new[:], 0.0)
            nc.gpsimd.memset(new_mask[:], NEG).then_inc(S("masks_ready"), 1)
            pool.wait_ge(S("x_staged"), KD)
            link(nc.gpsimd.memset(mask4[:], 0.0))
            link(nc.gpsimd.affine_select(out=mask4[:], in_=mask4[:], compare_op=ALU.is_ge, fill=NEG, base=0,
                                         pattern=[[0, NQ], [-1, P]], channel_multiplier=1))
            pool.wait_ge(S("f_full"), 1)
            scale_residual(pool, 0)
            pool.wait_ge(S("ncum_ready"), 1)
            pool.dma_start(ncum_d, fz[:, 6, 0:TP]).then_inc(S("ncum_stored"), 16)
            for b in range(NB):
                pool.dma_start(lf_s[NH * b:NH * (b + 1), PAST:PAST + TQ],
                               fz[:, 5, TP + TQ * b:TP + TQ * (b + 1)]).then_inc(S("lf_new_in"), 16)
            pool.wait_ge(S("lf_tok_ready"), 1)
            pool.dma_start(lp_o, lf_tok[:, 0:NQ, :]).then_inc(S("lf_stored"), 16)
            pool.dma_start(ls_o, lf_tok[0:TS, NQ, :]).then_inc(S("lf_stored"), 16)
            pool.wait_ge(S("ncum_stored"), 16)
            pool.wait_ge(S("pages_in"), 16)

            def pair(j):
                s = j.slot(2)
                wait(pool, S("q_ready"), j + 1)
                nc.gpsimd.tensor_copy(qT_s[:, ds(j.v, 1), :], q_sb[:, s, TP:T]).then_inc(S("qk_kept"), 1)
                wait(pool, S("k_ready"), j + 1)
                nc.gpsimd.tensor_copy(kT_s[:, ds(j.v, 1), :], k_sb[:, s, TP:T]).then_inc(S("qk_kept"), 1)
                for t in range(NPG):
                    pg = pool.value_load(pages[0:1, ds(j.times(NPG, t).v, 1)], min_val=0, max_val=39)
                    pool.dma_start(lf_pg[:, t, ds(j.v, 1), :], clf[ds(pg, 1)].rearrange("n p h -> (n p) h")
                                   ).then_inc(S("lf_pg_in"), 16)
                wait(pool, S("k_new_ready"), j + 1)
                wait(pool, S("v_new_ready"), j + 1)
                pool.dma_start(kp_o[:, :, ds(j.times(P).v, P)], k_tok[:]).then_inc(S("kv_stored"), 16)
                pool.dma_start(ks_o[:, ds(j.times(P).v, P)], k_new[:]).then_inc(S("kv_stored"), 16)
                pool.dma_start(vp_o[:, :, ds(j.times(P).v, P)], v_tok[:, s]).then_inc(S("kv_stored"), 16)
                pool.dma_start(vs_o[:, ds(j.times(P).v, P)], v_new[0:TS, ds(j.times(P).v, P)]).then_inc(S("kv_stored"), 16)
                for hh in range(2):
                    wait(pool, S("biased"), j.times(8, 4 * hh + 4 - 8))
                    pool.dma_start(ncb[:, hh, :], ncum_d[ds(j.times(2, hh).v, 1), :].broadcast_to([P, TP])
                                   ).then_inc(S("ncb_in"), 16)
                    wait(pool, S("ncb_in"), j.times(32, 16 * hh + 16))
                    nc.gpsimd.tensor_tensor(ncbm[:, hh, :], ncb[:, hh, :],
                                            mask4[:].rearrange("p t k -> p (t k)"), ALU.add
                                            ).then_inc(S("ncb_ready"), 1)

            pair(At(0))
            pair(At(1))
            with pool.Fori(0, NPAIR // 2 - 1) as i:
                pair(At(2, 2, i))
                pair(At(3, 2, i))

            pool.wait_ge(S("o_lo_ready"), NPAIR)
            pool.wait_ge(S("kv_stored"), 64 * NPAIR)
            nc.gpsimd.memset(psT[:], 0.0).then_inc(S("psT_zero"), 1)
            nc.gpsimd.memset(qz[:], 0.0).then_inc(S("qz_zero"), 1)
            pool.wait_ge(S("qz_zero"), 1)

            def sample(b):
                s = b.slot(2)
                v = qz[:, s, :].rearrange("p (j c) -> p j c", c=144)
                wait(pool, S("s_full"), b + (-1))
                for hh in range(2):
                    nc.gpsimd.tensor_copy(v[64 * hh:64 * hh + 64, :, TQ * hh:TQ * hh + TQ],
                                          qT_s[64 * hh:64 * hh + 64, :, ds(b.times(TQ).v, TQ)]
                                          ).then_inc(S("qz_ready"), 1)

            sample(At(0))
            with pool.Fori(0, NB // 2 - 1) as i:
                sample(At(1, 2, i))
                sample(At(2, 2, i))
            sample(At(NB - 1))

            scale_residual(pool, 1)
            ffn_pool(pool, 0)
            scale_residual(pool, 2)

            pool.wait_ge(S("rows_stored"), 32)
            nc.gpsimd.memset(xr[:, :, 0:3], 0.0).then_inc(S("xr_zero"), 1)
            nc.gpsimd.memset(xc[:, 2, :], 0.0).then_inc(S("xc_zero"), 1)
            pieces = [0, 0, 0]

            def gate_weights(j):
                s = j % 3
                wait(pool, S("rg_full"), j - 2)
                nc.gpsimd.memset(rgw[:, s], 0.0).then_inc(S("rgw_zero"), 1)
                pool.wait_ge(S("rgw_zero"), j + 1)
                for i in range(max(j - 1, 0), min(j + 2, NR)):
                    for blk in range(NH):
                        r0, r1 = max(RB * blk, P * i), min(RB * blk + RB, P * i + P)
                        c0, c1 = max(RB * blk, P * j), min(RB * blk + RB, P * j + P)
                        if r0 >= r1 or c0 >= c1:
                            continue
                        for q, w in enumerate(("w_rg_a", "w_rg_i")):
                            pool.dma_start(rgw[r0 - P * i:r1 - P * i, s, i - j + 1, q, c0 - P * j:c1 - P * j],
                                           a[w][0, blk, r0 - RB * blk:r1 - RB * blk, c0 - RB * blk:c1 - RB * blk]
                                           ).then_inc(S(f"rgw_in{s}"), 16)
                            pieces[s] += 1

            def gate_weights_in(j):
                pool.wait_ge(S(f"rgw_in{j % 3}"), 16 * pieces[j % 3])
                nc.gpsimd.memset(cols[:, 2 + j % 3:3 + j % 3], 0.0).then_inc(S("rgw_ready"), 1)

            def conv_pool(j):
                s = j % 3
                hist = xr[:, s, 3 + TP:XRW].rearrange("p (b c) -> p b c", c=3 + TQ)
                wait(pool, S("cx_tap"), 5 * (j - 2))
                nc.gpsimd.tensor_copy(hist[:, :, 0:3], hist_r[:, j, 0:24].rearrange("p (b c) -> p b c", c=3)
                                      ).then_inc(S("xr_hist"), 1)
                pool.wait_ge(S("xr_ready"), j + 1)
                nc.gpsimd.tensor_copy(r_st[:, j, 0:3], xr[:, s, TP:TP + 3])
                nc.gpsimd.tensor_copy(r_st[:, j, 3:27].rearrange("p (b c) -> p b c", c=3),
                                      hist[:, :, TQ:TQ + 3]).then_inc(S("xr_kept"), 1)

            for j in range(NR):
                gate_weights(j)
                conv_pool(j)
                gate_weights_in(j)

            pool.wait_ge(S("rows_ready"), 9)
            pool.dma_start(a["rconv_prompt"].rearrange("l b w f -> (l b w) f"), r_rows[0:3, :]).then_inc(S("rows_stored"), 16)
            pool.dma_start(a["rconv_sample"].rearrange("l b w f -> (l b w) f"), r_rows[3:27, :]).then_inc(S("rows_stored"), 16)
            pool.dma_start(a["h_prompt"].rearrange("l b f -> (l b) f"), r_rows[27:28, :]).then_inc(S("rows_stored"), 16)
            pool.dma_start(a["h_sample"].rearrange("l b f -> (l b) f"), r_rows[28:36, :]).then_inc(S("rows_stored"), 16)
            scale_residual(pool, 3)
            pool.wait_ge(S("rows_stored"), 16 * 6)
            ffn_pool(pool, 1)

            for t in range(NQ + 1):
                pool.wait_ge(S("y_left"), t + 1)
                pool.wait_ge(S("y_right"), t + 1)
                if t < NQ:
                    pool.dma_start(yp_o[t], y_tok[:, t % 2, :]).then_inc(S(f"y_stored{t % 2}"), 16)
                else:
                    pool.dma_start(ys_o, y_tok[0:TS, t % 2, :]).then_inc(S(f"y_stored{t % 2}"), 16)
            pool.wait_ge(S("y_stored0"), 16 * 3)
            pool.wait_ge(S("y_stored1"), 16 * 2)
            pool.wait_ge(S("rows_stored"), 16 * 8)
            pool.wait_ge(S("kv_stored"), 64 * NPAIR)
            pool.wait_ge(S("lf_stored"), 32)

        T_ORDER = ["T0", "T1", "T2", "T3", "T4", "T5", "k0", "k1", "T6", "v0", "v1", "T7"]
        T_LAST = 4 + 12 * (NPAIR - 1)

        def t_use(what, j):
            if j is None:
                return At(T_LAST + int(what[1]))
            if j.turn is None and j.first == 0:
                return At(["k0", "k1", "v0", "v1"].index(what))
            return j.times(12, 4 - 12 + T_ORDER.index(what))

        LN_BANK = (4, 4, 0, 4)
        Z_END = (Z_AO, Z_F0 + KD * (NG - 1), Z_RO, Z_F1 + KD * (NG - 1))
        ROW_BANKS = {1: (2, 3, 6, 7, 4, 5), 2: (4, 5, 6), 3: (2, 3, 6, 7, 4, 5)}
        ROWS_BEFORE = {1: 0, 2: 6, 3: 9}

        @block.tensor
        def _(pe):
            def transpose(out, in_):
                k = in_.shape[0]
                return nc.tensor.transpose(out, in_, ident[0:k, 0:k])

            pe.wait_ge(S("ident_ready"), 1)
            pe.wait_ge(S("x_in"), 32)
            for j in range(KD):
                b = 4 + 2 * (j % 2)
                wait(pe, S("x_f_ready"), j - 1)
                for t in range(NQ):
                    transpose(ps[:, b, P * t:P * t + P], x_in[:, t, P * j:P * j + P])
                transpose(ps[:, b + 1, 0:TS], x_in[0:TS, NQ, P * j:P * j + P]).then_inc(S("x_staged"), 1)
            pe.wait_ge(S("wf_in"), 32)
            pe.wait_ge(S("x_f_ready"), KD)
            for half in range(2):
                for k in range(KD):
                    last = nc.tensor.matmul(ps[0:NH, 4 + half, 0:HT], wf[:, k, :], x_f[:, k, HT * half:HT * half + HT],
                                            start=k == 0, stop=k == KD - 1)
            last.then_inc(S("f_full"), 1)
            pe.wait_ge(S("x_lo_ready"), KD)

            def qkv_half(j, c, half):
                n = j.times(3, c)
                if half == 0:
                    wait(pe, S("w_lo_ready"), n + 1)
                    wait(pe, *((S("k_ready"), j), (S("v_ready"), j), (S("q_ready"), j + 1))[c])
                last = unit_half(pe, n, n, half, x_terms())
                if half:
                    last.then_inc(S("acc_full"), 1)

            def token_rows(j, what):
                src = (k_sb[:, j.slot(2), :] if what[0] == "k" else v_sb[:, :])
                wait(pe, S("k_ready" if what[0] == "k" else "v_ready"), j + 1)
                wait(pe, S("t_free"), t_use(what, j))
                if what[1] == "0":
                    for t in range(NQ):
                        last = transpose(ps[:, 6, P * t:P * t + P], src[:, P * t:P * t + P])
                else:
                    last = transpose(ps[:, 6, 0:P], src[:, T - P:T])
                last.then_inc(S("t_full"), 1)

            def scores(p, s):
                g, hh, qt = p.times(8, s), s // 4, s % 4
                wait(pe, S("biased"), g + (-1 if s else 0))
                r = slice(64 * hh, 64 * hh + 64)
                nc.tensor.matmul(ps[:, 4 + s % 2, 0:P * (qt + 1)], q_sb[r, p.slot(2), P * qt:P * qt + P],
                                 k_sb[r, p.slot(2), 0:P * (qt + 1)], start=True, stop=True
                                 ).then_inc(S("sc_full"), 1)

            def prob_rows(p, s, j):
                g, qt = p.times(8, s), s % 4
                wait(pe, S("pr_norm"), g + 1)
                wait(pe, S("t_free"), t_use(f"T{s}", j))
                for kt in range(qt + 1):
                    last = transpose(ps[:, 6, P * kt:P * kt + P], pr[:, s % 2, P * kt:P * kt + P])
                last.then_inc(S("t_full"), 1)

            def values(p, hh, j):
                wait(pe, S("t_free"), t_use(f"T{4 * hh + 3}", j) + 1)
                if hh == 0:
                    wait(pe, S("o_lo_ready"), p)
                r = slice(64 * hh, 64 * hh + 64)
                for kt in range(NQ):
                    last = nc.tensor.matmul(ps[r, 7, P * kt:TP], v_tok[:, p.slot(2), kt, r], prT[:, kt, P * kt:TP],
                                            start=kt == 0, stop=kt == NQ - 1)
                last.then_inc(S("pv_done"), 1)

            for c in range(3):
                qkv_half(At(0), c, 0)
                qkv_half(At(0), c, 1)
            pe.wait_ge(S("prm_in"), 16 * 13)
            for blk, n in enumerate((C_LAM + NR, 4 * NR + 2 * NF, 3 * NF, 3 * NF)):
                last = transpose(ps[:, 6, P * blk:P * blk + n], prow[0:n, blk, :])
            last.then_inc(S("prm_full"), 1)
            for F in range(16):
                last = transpose(ps[:, 7, 32 * F:32 * F + 32], frow[:, P * F:P * F + P])
            last.then_inc(S("prm_full"), 1)
            pe.wait_ge(S("prm_ready"), 1)
            for F in range(16, NF):
                last = transpose(ps[:, 6, 32 * F - 512:32 * F - 480], frow[:, P * F:P * F + P])
            last.then_inc(S("prm_full"), 1)
            pe.wait_ge(S("prm_ready"), 2)
            for j in range(NR):
                last = transpose(ps[:, 7, 32 * j:32 * j + 32], rrow[:, P * j:P * j + P])
            last.then_inc(S("prm_full"), 1)
            pe.wait_ge(S("prm_ready"), 4)
            pe.wait_ge(S("ncum_ready"), 1)
            for t in range(NQ):
                transpose(ps[:, 6, NH * t:NH * t + NH], fz[:, 6, P * t:P * t + P])
            for t in range(NQ + 1):
                w = min(P, T - P * t)
                last = transpose(ps[0:w, 6, 64 + NH * t:64 + NH * t + NH], fz[:, 5, P * t:P * t + w])
            last.then_inc(S("lf_full"), 1)
            pe.wait_ge(S("lf_tok_ready"), 1)
            for what in ("k0", "k1", "v0", "v1"):
                token_rows(At(0), what)

            def pair(j, p):
                scores(p, 0)
                qkv_half(j, 0, 0)
                scores(p, 1)
                prob_rows(p, 0, j)
                qkv_half(j, 0, 1)
                scores(p, 2)
                prob_rows(p, 1, j)
                qkv_half(j, 1, 0)
                scores(p, 3)
                prob_rows(p, 2, j)
                qkv_half(j, 1, 1)
                scores(p, 4)
                prob_rows(p, 3, j)
                qkv_half(j, 2, 0)
                values(p, 0, j)
                scores(p, 5)
                prob_rows(p, 4, j)
                qkv_half(j, 2, 1)
                scores(p, 6)
                prob_rows(p, 5, j)
                token_rows(j, "k0")
                token_rows(j, "k1")
                scores(p, 7)
                prob_rows(p, 6, j)
                token_rows(j, "v0")
                token_rows(j, "v1")
                prob_rows(p, 7, j)
                values(p, 1, j)

            with pe.Fori(0, NPAIR // 2 - 1) as i:
                pair(At(1, 2, i), At(0, 2, i))
                pair(At(2, 2, i), At(1, 2, i))
            pair(At(NPAIR - 1), At(NPAIR - 2))
            last_pair = At(NPAIR - 1)
            scores(last_pair, 0)
            for s in range(1, 8):
                scores(last_pair, s)
                prob_rows(last_pair, s - 1, None)
                if s == 5:
                    values(last_pair, 0, None)
            prob_rows(last_pair, 7, None)
            values(last_pair, 1, None)

            pe.wait_ge(S("lf_pg_in"), 16 * NB * NPG)
            pe.wait_ge(S("t_free"), T_LAST + 8)
            for t in range(NPG):
                last = transpose(ps[:, 6, P * t:P * t + P], lf_pg[:, t, :, :].rearrange("p b h -> p (b h)"))
            last.then_inc(S("t_full"), 1)
            pe.wait_ge(S("cq_w_ready"), 1)
            pe.wait_ge(S("o_lo_ready"), NPAIR)
            nc.tensor.matmul(ps[:, 7, 0:NB], cq_w[:].rearrange("p h q -> p (h q)"), batch_of[:], start=True, stop=True
                             ).then_inc(S("cq_full"), 1)

            def s_scores(b):
                s = b.slot(2)
                bk = 2 * s
                wait(pe, S(f"k_pg{s}"), b.round(2).times(64, 64))
                wait(pe, S("qz_ready"), b.times(2, 2))
                wait(pe, S("e_b_ready"), b + 1)
                wait(pe, S("s_biased"), b + (-1))

                def k_columns(j):
                    ready = S("kT_even" if j % 2 == 0 else "kT_odd")
                    wait(pe, ready, b.times(4, j // 2))
                    for t in range(NPG):
                        last = transpose(ps[:, 4 + j % 2, P * t:P * t + P], k_pg[:, s, t, P * j:P * j + P])
                    last.then_inc(S("kT_full"), 1)

                def add(j):
                    wait(pe, S("kT_even" if j % 2 == 0 else "kT_odd"), b.times(4, j // 2 + 1))
                    q = qz[:, s, P * j:P * j + P]
                    nc.tensor.matmul(ps[:, bk, 0:PAST], q, kT[:, j % 2, :], start=j == 0, stop=False)
                    nc.tensor.matmul(ps[:, bk + 1, 0:TS], q, kT_s[:, j, :], start=j == 0, stop=False
                                     ).then_inc(S("kT_used"), 1)

                k_columns(0)
                for j in range(1, KD):
                    k_columns(j)
                    add(j - 1)
                add(KD - 1)
                nc.tensor.matmul(ps[:, bk, 0:PAST], e_b[:, s, :], nc_s[:, 0:PAST], start=False, stop=True)
                new = nc_s[:, PAST:PAST + TQ].rearrange("p (o k) -> p o k", o=1).broadcast_to([P, NB, TQ])
                nc.tensor.matmul(ps[:, bk + 1, 0:TS].rearrange("p (b k) -> p b k", b=NB), e_b[:, s, :], new,
                                 start=False, stop=True).then_inc(S("s_full"), 1)

            def s_values(b):
                s = b.slot(2)
                wait(pe, S("ps_norm"), b + 1)
                wait(pe, S("psT_ready"), b)
                wait(pe, S("os_lo"), b.times(2))
                for t in range(NPG):
                    transpose(ps[:, 6, P * t:P * t + P], ps_[:, s, P * t:P * t + P])
                transpose(ps[0:TS, 7, P:2 * P], ps_[:, s, PAST:SW]).then_inc(S("psT_full"), 1)
                wait(pe, S("psT_ready"), b + 1)
                wait(pe, S(f"v_pg{s}"), b.round(2).times(64, 64))
                for j in range(KD):
                    for t in range(NPG + 1):
                        v = v_pg[:, s, t, P * j:P * j + P] if t < NPG else v_new[:, P * j:P * j + P]
                        last = nc.tensor.matmul(ps[:, 7, 16 * j:16 * j + 16], v, psT[:, t, 16 * j:16 * j + 16],
                                                start=t == 0, stop=t == NPG)
                last.then_inc(S("pv_s_done"), 1)

            pe.wait_ge(S("cq_s_ready"), 1)
            pe.wait_ge(S("psT_zero"), 1)
            pe.wait_ge(S("q_ready"), NPAIR)
            pe.wait_ge(S("k_ready"), NPAIR)
            pe.wait_ge(S("v_ready"), NPAIR)
            pe.wait_ge(S("qk_kept"), 2 * NPAIR)
            s_scores(At(0))
            with pe.Fori(0, NB // 2 - 1) as i:
                s_scores(At(1, 2, i))
                s_values(At(0, 2, i))
                s_scores(At(2, 2, i))
                s_values(At(1, 2, i))
            s_scores(At(NB - 1))
            s_values(At(NB - 2))
            s_values(At(NB - 1))

            pe.wait_ge(S("os_lo"), 2 * NB)
            pe.wait_ge(S("s_biased"), NB)
            for j in range(KD):
                n = At(N_AO + j)
                wait(pe, S("w_lo_ready"), n + 1)
                wait(pe, S("z_added"), Z_AO + j - 1)
                for half in range(2):
                    last = unit_half(pe, n, At(M_AO + j), half, [(k, o_hi[:, k, :], o_lo[:, k, :]) for k in range(KD)])
                last.then_inc(S("acc_full"), 1)

            def norm(k):
                b = LN_BANK[k]
                if k == 2:
                    pe.wait_ge(S("z_added"), Z_RO + 6)
                for j in range(KD):
                    pe.wait_ge(S("z_added"), Z_END[k] + j + 1)
                    for half in range(2):
                        last = nc.tensor.matmul(ps[:, b + half, 0:HT], over_d[:], x_f[:, j, HT * half:HT * half + HT],
                                                start=j == 0, stop=j == KD - 1)
                last.then_inc(S("ln_mean"), 1)
                sq_t = (ln_f, ln_f, ln_r, ln_f)[k][0]
                for j in range(KD):
                    pe.wait_ge(S("ln_sq_ready"), KD * k + j + 1)
                    for half in range(2):
                        last = nc.tensor.matmul(ps[:, b + 2 + half, 0:HT], over_d[:],
                                                sq_t[:, j % 2, HT * half:HT * half + HT],
                                                start=j == 0, stop=j == KD - 1)
                    last.then_inc(S("ln_sq_used"), 1)
                if k == 0:
                    return
                pe.wait_ge(S("ln_centred"), KD * (k + 1))
                pe.wait_ge(S("ln_std"), k + 1)
                if k == 2:
                    pe.wait_ge(S("z_added"), Z_RO + KD)
                    pe.wait_ge(S("xr_kept"), NR)
                    pe.wait_ge(S("h_kept"), NR)
                else:
                    pe.wait_ge(S("gh_kept"), NF * (1 if k == 1 else 2))
                src, n, w = (r_st, NR, 36) if k == 2 else (f_st, NF, 18)
                for i, bank in enumerate(ROW_BANKS[k]):
                    for c in range(4 * i, min(4 * i + 4, n)):
                        last = transpose(ps[0:w, bank, P * (c % 4):P * (c % 4) + P], src[:, c, :])
                    last.then_inc(S("rows_full"), 1)

            norm(0)

            def ffn(l, n0, m0, z0):
                def inner(F, n, m, n_waits=()):
                    Fg = F + NF * l
                    for c in range(2):
                        wait(pe, S("w_lo_ready"), n + c + 1)
                        wait(pe, S("gh_ready" if c == 0 else "h_ready"), Fg)
                        for sem, value in n_waits:
                            wait(pe, sem, value)
                        for half in range(2):
                            last = unit_half(pe, n + c, m + c, half, x_terms())
                        last.then_inc(S("acc_full"), 1)

                def outer(g, par, n, m):
                    wait(pe, S("h_lo_ready"), g.times(GF, NF * l + GF))
                    for c in range(4):
                        wait(pe, S("w_lo_ready"), n + c + 1)
                        for d in (2 * c, 2 * c + 1):
                            if d < 2:
                                nxt = g.times(GF, NF * l + GF)
                                more = not (g.turn is None and g.first == NG - 1)
                                wait(pe, S("gh_ready" if d == 0 else "h_ready"), nxt + (1 if more else 0))
                            else:
                                wait(pe, S("z_added"), g.times(KD, z0 + d - 1))
                            for half in range(2):
                                terms = [(2 * f + d % 2, h_hi[:, par, f, :], h_lo[:, par, f, :]) for f in range(GF)]
                                last = unit_half(pe, n + c, m + d, half, terms)
                            last.then_inc(S("acc_full"), 1)

                def group(g, par, more):
                    n, m = g.times(12, n0 + 2), g.times(16, m0 + 2)
                    for f in range(1, GF):
                        out_before = [(S("z_added"), g.times(KD, z0))] if f == 1 else []
                        inner(g.times(GF, f), n + 2 * (f - 1), m + 2 * (f - 1), out_before)
                    if more:
                        inner(g.times(GF, GF), n + 6, m + 6)
                    k = 8 if more else 6
                    outer(g, par, n + k, m + k)

                inner(At(0), At(n0), At(m0), [(S("z_added"), z0), (S("x_lo_ready"), KD * (2 if l == 0 else 4))])
                with pe.Fori(0, NG // 2 - 1) as i:
                    group(At(0, 2, i), 0, True)
                    group(At(1, 2, i), 1, True)
                group(At(NG - 2), 0, True)
                group(At(NG - 1), 1, False)

            ffn(0, N_F0, M_F0, Z_F0)
            norm(1)

            def in_proj(j, c):
                n, m = j.times(2, N_RI + c), j.times(2, M_RI + c)
                wait(pe, S("w_lo_ready"), n + 1)
                wait(pe, S("gate_ready" if c == 0 else "xr_ready"), j)
                for half in range(2):
                    last = unit_half(pe, n, m, half, x_terms())
                last.then_inc(S("acc_full"), 1)

            def gates(j, sources, u):
                wait(pe, S("rgw_ready"), j + 1)
                wait(pe, S("cx_tap"), min(5 * (j.first + 2), 5 * NR) if j.turn is None else j.times(5, 10))
                wait(pe, S("rg_read"), j)
                for q in range(2):
                    for half in range(2):
                        for i in sources:
                            last = nc.tensor.matmul(ps[:, 4 + 2 * q + half, 0:HT], rgw[:, u, i + 1, q, :],
                                                    xc[:, (u + i) % 3, HT * half:HT * half + HT],
                                                    start=i == sources[0], stop=i == sources[-1])
                last.then_inc(S("rg_full"), 1)

            pe.wait_ge(S("x_lo_ready"), 3 * KD)
            pe.wait_ge(S("rows_ready"), 6)
            pe.wait_ge(S("xc_zero"), 1)
            for j in range(2):
                in_proj(At(j), 0)
                in_proj(At(j), 1)
            with pe.Fori(0, 3) as i:
                for u in range(3):
                    j = At(2 + u, 3, i)
                    in_proj(j, 0)
                    gates(At(u, 3, i), (-1, 0, 1), u)
                    in_proj(j, 1)
            gates(At(NR - 2), (-1, 0, 1), (NR - 2) % 3)
            gates(At(NR - 1), (-1, 0), (NR - 1) % 3)

            pe.wait_ge(S("r_lo_ready"), NR)
            pe.wait_ge(S("rg_read"), NR)
            for q in range(4):
                wait(pe, S("z_added"), Z_RO + 2 * (q - 1) if q >= 2 else 0)
                for c in range(3):
                    n = At(N_RO + 3 * q + c)
                    wait(pe, S("w_lo_ready"), n + 1)
                    tiles = range(4 * c, min(4 * c + 4, NR))
                    for d in range(2):
                        for half in range(2):
                            terms = [(2 * (k - 4 * c) + d, r_hi[:, k, :], r_lo[:, k, :]) for k in tiles]
                            last = products(pe, n, ps[:, 4 * (q % 2) + 2 * d + half, 0:HT], terms, half,
                                            first=c == 0, last=c == 2)
                    last.then_inc(S("ro_full"), 1)
            norm(2)
            pe.wait_ge(S("rows_ready"), 9)
            ffn(1, N_F1, M_F1, Z_F1)
            norm(3)

            pe.wait_ge(S("x_f_ready"), 5 * KD)
            pe.wait_ge(S("rows_ready"), 15)
            for t in range(NQ + 1):
                w = min(P, T - P * t)
                wait(pe, S("y_left"), t - 1)
                wait(pe, S("y_right"), t - 1)
                for j in range(KD):
                    last = transpose(ps[0:w, 2 * (t % 2) + j // 4, P * (j % 4):P * (j % 4) + P], x_f[:, j, P * t:P * t + w])
                last.then_inc(S("y_full"), 1)

        @block.scalar
        def _(act):
            def hi_next(n, done):
                if n.turn is not None or n.first + RING < N_END:
                    split_hi(act, n + RING, done, width_of(n + RING))

            for j in range(KD):
                act.wait_ge(S("x_f_ready"), j + 1)
                nc.scalar.copy(x_hi[:, j, :], x_f[:, j, :]).then_inc(S("x_hi_ready"), 1)
            for n in range(RING):
                split_hi(act, At(n), None)
            act.wait_ge(S("f_logits"), 1)
            nc.scalar.activation(fz[:, 0, :], fz[:, 1, :], ACT.Abs).then_inc(S("f_abs"), 1)
            act.wait_ge(S("f_abs"), 1)
            nc.scalar.activation(fz[:, 0, :], fz[:, 0, :], ACT.Exp, scale=-1.0).then_inc(S("f_exp"), 1)

            def q_out(j):
                wait(act, S("acc_full"), j.times(3, 1))
                wait(act, S("qk_kept"), j.times(2, -2))
                nc.scalar.mul(halves(q_sb[:, j.slot(2), :]), acc(j.times(3)), HD ** -0.5).then_inc(S("q_ready"), 1)
                hi_next(j.times(3), (S("acc_full"), j.times(3, 1)))

            def v_out(j):
                wait(act, S("acc_full"), j.times(3, 3))
                nc.scalar.copy(halves(v_sb[:]), acc(j.times(3, 2))).then_inc(S("v_ready"), 1)
                hi_next(j.times(3, 2), (S("acc_full"), j.times(3, 3)))

            def v_rows(j):
                wait(act, S("t_full"), t_use("v0", j) + 1)
                wait(act, S("kv_stored"), j.times(64))
                nc.scalar.copy(v_tok[:, j.slot(2)].rearrange("p t e -> p (t e)"), ps[:, 6, 0:TP]).then_inc(S("t_free"), 1)
                wait(act, S("t_full"), t_use("v1", j) + 1)
                nc.scalar.copy(v_new[0:TS, ds(j.times(P).v, P)], ps[P - TS:P, 6, 0:P]).then_inc(S("t_free"), 1)

            def v_rows_known(j):
                wait(act, S("t_free"), t_use("v1", j) + 1)
                nc.scalar.copy(cols[:, 5:6], cols[:, 0:1]).then_inc(S("v_new_ready"), 1)

            def exps(p, s):
                g, w = p.times(8, s), P * (s % 4 + 1)
                wait(act, S("row_max"), g + 1)
                nc.scalar.activation(pr[:, s % 2, 0:w], sc[:, s % 2, 0:w], ACT.Exp, bias=sm[:, 0, s % 2:s % 2 + 1],
                                     accum_out=sm[:, 1, s % 2:s % 2 + 1]).then_inc(S("probs"), 1)

            def prob_columns(p, s, j):
                qt = s % 4
                wait(act, S("t_full"), t_use(f"T{s}", j) + 1)
                wait(act, S("pv_done"), p.times(2, s // 4))
                nc.scalar.copy(prT[:, 0:qt + 1, P * qt:P * qt + P],
                               ps[:, 6, 0:P * (qt + 1)].rearrange("p (t k) -> p t k", k=P)).then_inc(S("t_free"), 1)

            def o_out(p):
                wait(act, S("pv_done"), p.times(2, 2))
                nc.scalar.copy(o_hi[:, ds(p.v, 1), 0:TP].rearrange("p o t -> p (o t)"), ps[:, 7, 0:TP]).then_inc(S("o_hi_ready"), 1)

            act.wait_ge(S("masks_ready"), 1)
            q_out(At(0))
            wait(act, S("acc_full"), 2)
            hi_next(At(1), (S("acc_full"), 2))
            v_out(At(0))
            for i, (dst, bank, w) in enumerate(((prm[:], 6, 512), (hist_f[:, 0:16, :], 7, 512),
                                                (hist_f[:, 16:NF, :], 6, 256), (hist_r[:], 7, 32 * NR))):
                act.wait_ge(S("prm_full"), i + 1)
                src = ps[:, bank, 0:w]
                if i == 0:
                    for blk, n in enumerate((C_LAM + NR, 4 * NR + 2 * NF, 3 * NF, 3 * NF)):
                        last = nc.scalar.copy(prm[:, P * blk:P * blk + n], ps[:, 6, P * blk:P * blk + n])
                    last.then_inc(S("prm_ready"), 1)
                else:
                    nc.scalar.copy(dst, src.rearrange("p (c w) -> p c w", w=32)).then_inc(S("prm_ready"), 1)
            lam = prm[:, C_LAM:C_LAM + NR]
            act.wait_ge(S("prm_ready"), 4)
            nc.scalar.activation(lru_c[:], lam, ACT.Abs).then_inc(S("lam_abs"), 1)
            act.wait_ge(S("lam_abs"), 1)
            nc.scalar.activation(lru_c[:], lru_c[:], ACT.Exp, scale=-1.0).then_inc(S("lam_exp"), 1)
            act.wait_ge(S("lf_full"), 1)
            nc.scalar.mul(cumq[:], ps[:, 6, 0:64].rearrange("p (t h) -> p t h", h=NH), -1.0)
            nc.scalar.copy(lf_tok[:, 0:NQ, :], ps[:, 6, 64:64 + NH * NQ].rearrange("p (t h) -> p t h", h=NH))
            nc.scalar.copy(lf_tok[0:TS, NQ, :], ps[0:TS, 6, 64 + NH * NQ:64 + NH * (NQ + 1)]).then_inc(S("lf_tok_ready"), 1)
            v_rows(At(0))
            v_rows_known(At(0))
            act.wait_ge(S("ncum_stored"), 16)
            act.wait_ge(S("lf_new_in"), 16 * NB)

            def pair(j, p):
                exps(p, 0)
                exps(p, 1)
                prob_columns(p, 0, j)
                q_out(j)
                exps(p, 2)
                prob_columns(p, 1, j)
                exps(p, 3)
                prob_columns(p, 2, j)
                wait(act, S("acc_full"), j.times(3, 2))
                hi_next(j.times(3, 1), (S("acc_full"), j.times(3, 2)))
                exps(p, 4)
                prob_columns(p, 3, j)
                exps(p, 5)
                prob_columns(p, 4, j)
                v_out(j)
                exps(p, 6)
                prob_columns(p, 5, j)
                exps(p, 7)
                prob_columns(p, 6, j)
                v_rows(j)
                v_rows_known(j)
                prob_columns(p, 7, j)
                o_out(p)

            with act.Fori(0, NPAIR // 2 - 1) as i:
                pair(At(1, 2, i), At(0, 2, i))
                pair(At(2, 2, i), At(1, 2, i))
            pair(At(NPAIR - 1), At(NPAIR - 2))
            p = At(NPAIR - 1)
            exps(p, 0)
            for s in range(1, 8):
                exps(p, s)
                prob_columns(p, s - 1, None)
            prob_columns(p, 7, None)
            o_out(p)

            act.wait_ge(S("cq_full"), 1)
            nc.scalar.mul(cq_s[:], ps[:, 7, 0:NB], -1.0).then_inc(S("cq_s_ready"), 1)

            def kT_even(b):
                for j in range(0, KD, 2):
                    wait(act, S("kT_full"), b.times(KD, j + 1))
                    wait(act, S("kT_used"), b.times(KD, j - 1))
                    nc.scalar.copy(kT[:, 0, :], ps[:, 4, 0:PAST]).then_inc(S("kT_even"), 1)

            def s_exp(b):
                s = b.slot(2)
                wait(act, S("s_max"), b + 1)
                nc.scalar.activation(ps_[:, s, :], ss[:, s, :], ACT.Exp, bias=sms[:, 0, s:s + 1],
                                     accum_out=sms[:, 1, s:s + 1]).then_inc(S("s_probs"), 1)

            def s_columns(b):
                wait(act, S("psT_full"), b + 1)
                wait(act, S("pv_s_done"), b)
                nc.scalar.copy(psT[:, 0:NPG, :].rearrange("p t c -> p (t c)"), ps[:, 6, 0:PAST])
                nc.scalar.copy(psT[0:TS, NPG, :], ps[0:TS, 7, P:2 * P]).then_inc(S("psT_ready"), 1)

            def s_out(b):
                wait(act, S("pv_s_done"), b + 1)
                for hh in range(2):
                    r = slice(64 * hh, 64 * hh + 64)
                    nc.scalar.copy(o_hi[r, :, ds(b.times(TQ, TP).v, TQ)],
                                   ps[r, 7, 0:P].rearrange("p (j c) -> p j c", c=16)[:, :, TQ * hh:TQ * hh + TQ]
                                   ).then_inc(S("os_hi"), 1)

            act.wait_ge(S("psT_zero"), 1)
            kT_even(At(0))
            s_exp(At(0))

            def sample(b, c):
                kT_even(b)
                s_columns(c)
                s_exp(b)
                s_out(c)

            with act.Fori(0, NB // 2 - 1) as i:
                sample(At(1, 2, i), At(0, 2, i))
                sample(At(2, 2, i), At(1, 2, i))
            sample(At(NB - 1), At(NB - 2))
            s_columns(At(NB - 1))
            s_out(At(NB - 1))
            for j in range(KD):
                hi_next(At(N_AO + j), (S("acc_full"), M_AO + j + 1))

            def norm(k):
                b = LN_BANK[k]
                sq_t, rs = (ln_f, ln_f, ln_r, ln_f)[k]
                for j in range(KD):
                    act.wait_ge(S("ln_centred"), KD * k + j + 1)
                    wait(act, S("ln_sq_used"), KD * k + j - 1)
                    nc.scalar.activation(sq_t[:, j % 2, :], x_f[:, j, :], ACT.Square).then_inc(S("ln_sq_ready"), 1)
                act.wait_ge(S("ln_sq_used"), KD * (k + 1))
                nc.scalar.activation(halves(rs[:, 0, :]), bank_pair(b + 2), ACT.Sqrt, bias=cols[:, 0:1]
                                     ).then_inc(S("ln_std"), 1)
                for j in range(KD):
                    g = prm[:, C_LNG + KD * k + j:C_LNG + KD * k + j + 1]
                    h = prm[:, C_LNB + KD * k + j:C_LNB + KD * k + j + 1]
                    act.wait_ge(S("ln_scaled"), KD * k + j + 1)
                    if k < 3:
                        nc.scalar.activation(x_hi[:, j, :], x_f[:, j, :], ACT.Identity, bias=h, scale=g
                                             ).then_inc(S("x_hi_ready"), 1)
                    nc.scalar.activation(x_f[:, j, :], x_f[:, j, :], ACT.Identity, bias=h, scale=g
                                         ).then_inc(S("x_f_ready"), 1)
                if k == 0:
                    return
                dst, w, n = (r_rows, 36, R) if k == 2 else (f_rows, 18, FF)
                for i, bank in enumerate(ROW_BANKS[k]):
                    act.wait_ge(S("rows_full"), ROWS_BEFORE[k] + i + 1)
                    c0, c1 = 512 * i, min(512 * i + 512, n)
                    nc.scalar.copy(dst[:, c0:c1], ps[0:w, bank, 0:c1 - c0]).then_inc(S("rows_ready"), 1)

            norm(0)

            def ffn(l, n0, m0):
                def tile(F, n, m, par, f):
                    Fg = F + NF * l
                    s = F.slot(2)
                    wait(act, S("acc_full"), m + 1)
                    wait(act, S("cv_tap"), Fg.times(3, -3))
                    wait(act, S("gh_kept"), Fg + (-1))
                    for src, t0, t1 in prompt_parts(2 * m.slot(2)):
                        nc.scalar.copy(gh[:, s, 2 + t0:2 + t1], src)
                    seq = gh[:, s, 2 + TP:GHW].rearrange("p (b c) -> p b c", c=2 + TQ)
                    src = ps[:, 2 * m.slot(2) + 1, TP - HT:HT].rearrange("p (b q) -> p b q", q=TQ)
                    nc.scalar.copy(seq[:, :, 2:2 + TQ], src).then_inc(S("gh_ready"), 1)
                    hi_next(n, (S("acc_full"), m + 1))
                    wait(act, S("cv_tap"), Fg.times(3, 3))
                    wait(act, S("h_ready"), Fg)
                    nc.scalar.activation(gl[:, 0:CVW], cv[:], ACT.Gelu_apprx_tanh).then_inc(S("gelu_ready"), 1)
                    wait(act, S("acc_full"), m + 2)
                    hi_next(n + 1, (S("acc_full"), m + 2))
                    wait(act, S("h_ready"), Fg + 1)
                    nc.scalar.copy(h_hi[:, par, f, :], hf[:]).then_inc(S("h_hi_ready"), 1)

                def group(g, par, more):
                    n, m = g.times(12, n0 + 2), g.times(16, m0 + 2)
                    for f in range(1, GF):
                        tile(g.times(GF, f), n + 2 * (f - 1), m + 2 * (f - 1), par, f)
                    if more:
                        tile(g.times(GF, GF), n + 6, m + 6, 1 - par, 0)
                    k = 8 if more else 6
                    for c in range(4):
                        hi_next(n + (k + c), (S("acc_full"), m + (k + 2 * c + 2)))

                act.wait_ge(S("x_lo_ready"), KD * (2 if l == 0 else 4))
                tile(At(0), At(n0), At(m0), 0, 0)
                with act.Fori(0, NG // 2 - 1) as i:
                    group(At(0, 2, i), 0, True)
                    group(At(1, 2, i), 1, True)
                group(At(NG - 2), 0, True)
                group(At(NG - 1), 1, False)

            ffn(0, N_F0, M_F0)
            norm(1)

            def y_out(j, u):
                m = j.times(2, M_RI)
                wait(act, S("acc_full"), m + 1)
                wait(act, S("r_ready"), j + (-2))
                nc.scalar.activation(halves(gate[:, u, :]), acc(m), ACT.Gelu_apprx_tanh).then_inc(S("gate_ready"), 1)
                hi_next(j.times(2, N_RI), (S("acc_full"), m + 1))

            def x_out(j):
                m, s = j.times(2, M_RI + 1), j.slot(3)
                wait(act, S("acc_full"), m + 1)
                wait(act, S("cx_tap"), j.times(5, -10))
                wait(act, S("xr_kept"), j + (-2))
                for src, t0, t1 in prompt_parts(2 * m.slot(2)):
                    nc.scalar.copy(xr[:, s, 3 + t0:3 + t1], src)
                seq = xr[:, s, 3 + TP:XRW].rearrange("p (b c) -> p b c", c=3 + TQ)
                src = ps[:, 2 * m.slot(2) + 1, TP - HT:HT].rearrange("p (b q) -> p b q", q=TQ)
                nc.scalar.copy(seq[:, :, 3:3 + TQ], src).then_inc(S("xr_ready"), 1)
                hi_next(j.times(2, N_RI + 1), (S("acc_full"), m + 1))

            def gates(j):
                wait(act, S("rg_full"), j + 1)
                wait(act, S("r_ready"), j)
                col = lambda t, c: t[:, ds((j + c).v, 1)]
                nc.scalar.activation(halves(tr[:]), bank_pair(4), ACT.Tanh, bias=col(half_b, 0), scale=0.5
                                     ).then_inc(S("tr_half"), 1)
                nc.scalar.activation(halves(ti[:]), bank_pair(6), ACT.Tanh, bias=col(half_b, NR), scale=0.5
                                     ).then_inc(S("rg_read"), 1)
                wait(act, S("tr_half"), j + 1)
                nc.scalar.activation(tr[:], tr[:], ACT.Tanh, bias=col(lru_c, 0), scale=col(lru_c, 0)
                                     ).then_inc(S("tr_ready"), 1)
                wait(act, S("tr_ready"), j + 1)
                nc.scalar.activation(om[:], tr[:], ACT.Identity, bias=1.0, scale=-1.0).then_inc(S("om_ready"), 1)
                nc.scalar.activation(sq[:], tr[:], ACT.Sqrt, bias=cols[:, 1:2], scale=-1.0).then_inc(S("sq_ready"), 1)

            def r_out(j):
                wait(act, S("r_ready"), j + 1)
                nc.scalar.copy(r_hi[:, ds(j.v, 1), :].rearrange("p o t -> p (o t)"), uu[:]).then_inc(S("r_hi_ready"), 1)

            act.wait_ge(S("rows_stored"), 32)
            act.wait_ge(S("half_b_ready"), 1)
            for j in range(2):
                y_out(At(j), j)
                x_out(At(j))
            with act.Fori(0, 3) as i:
                for u in range(3):
                    j = At(2 + u, 3, i)
                    y_out(j, (2 + u) % 3)
                    gates(At(u, 3, i))
                    x_out(j)
                    r_out(At(u, 3, i))
            for j in (NR - 2, NR - 1):
                gates(At(j))
                r_out(At(j))
            for q in range(4):
                for c in range(3):
                    hi_next(At(N_RO + 3 * q + c), (S("ro_full"), 3 * q + c + 1))
            norm(2)
            act.wait_ge(S("rows_stored"), 16 * 6)
            ffn(1, N_F1, M_F1)
            norm(3)
            for t in range(NQ + 1):
                w = min(P, T - P * t)
                act.wait_ge(S("y_full"), t + 1)
                if t == 0:
                    act.wait_ge(S("rows_stored"), 16 * 8)
                wait(act, S(f"y_stored{t % 2}"), 16 * (t // 2))
                nc.scalar.copy(y_tok[0:w, t % 2, 0:512], ps[0:w, 2 * (t % 2), 0:512]).then_inc(S("y_left"), 1)

        @block.vector
        def _(dve):
            link_n = [0]

            def link(ins):
                link_n[0] += 1
                ins.then_inc(S("dve_step"), 1)
                dve.wait_ge(S("dve_step"), link_n[0])

            def lo_next(n):
                if n.turn is not None or n.first + RING < N_END:
                    split_lo(dve, n + RING, width_of(n + RING))

            V = nc.vector

            def x_lo_tile(k, j):
                dve.wait_ge(S("x_hi_ready"), KD * k + j + 1)
                dve.wait_ge(S("x_f_ready"), KD * k + j + 1)
                V.tensor_tensor(x_lo[:, j, :], x_f[:, j, :], x_hi[:, j, :].bitcast(f32), ALU.subtract
                                ).then_inc(S("x_lo_ready"), 1)

            for j in range(KD):
                b = 4 + 2 * (j % 2)
                dve.wait_ge(S("x_staged"), j + 1)
                V.tensor_copy(x_f[:, j, 0:TP], ps[:, b, 0:TP])
                V.tensor_copy(x_f[:, j, TP:T], ps[:, b + 1, 0:TS]).then_inc(S("x_f_ready"), 1)
                if j:
                    x_lo_tile(0, j - 1)
            x_lo_tile(0, KD - 1)
            for n in range(RING):
                split_lo(dve, At(n))

            def log1p_half(s, r, s2, e):
                link(V.tensor_scalar(r, e, 2.0, None, ALU.add))
                link(V.reciprocal(r, r))
                link(V.tensor_tensor(s, e, r, ALU.mult))
                link(V.tensor_tensor(s2, s, s, ALU.mult))
                link(V.tensor_scalar(r, s2, 1.0 / 17, None, ALU.mult))
                for k in (15, 13, 11, 9, 7, 5, 3):
                    link(V.scalar_tensor_tensor(out=r, in0=r, scalar=1.0 / k, in1=s2, op0=ALU.add, op1=ALU.mult))
                link(V.scalar_tensor_tensor(out=r, in0=r, scalar=1.0, in1=s, op0=ALU.add, op1=ALU.mult))

            dve.wait_ge(S("f_full"), 1)
            dve.wait_ge(S("wf_in"), 32)
            V.tensor_scalar(halves(fz[:, 1, :]), ps[0:NH, 4:6, 0:HT], bf_col[:], None, ALU.add
                            ).then_inc(S("f_logits"), 1)
            dve.wait_ge(S("f_exp"), 1)
            link(V.tensor_scalar(fz[:, 1, :], fz[:, 1, :], 0.0, None, ALU.min))
            log1p_half(fz[:, 3, :], fz[:, 2, :], fz[:, 4, :], fz[:, 0, :])
            link(V.scalar_tensor_tensor(out=fz[:, 5, :], in0=fz[:, 2, :], scalar=-2.0, in1=fz[:, 1, :],
                                        op0=ALU.mult, op1=ALU.add))
            dve.wait_ge(S("masks_ready"), 1)
            V.tensor_tensor_scan(out=fz[:, 6, 0:TP], data0=ones_s[0:NH, 0:TP], data1=fz[:, 5, 0:TP], initial=0.0,
                                 op0=ALU.mult, op1=ALU.subtract).then_inc(S("ncum_ready"), 1)

            def k_out(j):
                wait(dve, S("acc_full"), j.times(3, 2))
                wait(dve, S("qk_kept"), j.times(2, -2))
                V.tensor_copy(halves(k_sb[:, j.slot(2), :]), acc(j.times(3, 1))).then_inc(S("k_ready"), 1)
                lo_next(j.times(3, 1))

            def k_rows(j):
                wait(dve, S("t_full"), t_use("k0", j) + 1)
                wait(dve, S("kv_stored"), j.times(64))
                V.tensor_copy(k_tok[:].rearrange("p t e -> p (t e)"), ps[:, 6, 0:TP]).then_inc(S("t_free"), 1)
                wait(dve, S("t_full"), t_use("k1", j) + 1)
                V.tensor_copy(k_new[:], ps[P - TS:P, 6, 0:P]).then_inc(S("t_free"), 1)

            def k_rows_known(j):
                wait(dve, S("t_free"), t_use("k1", j) + 1)
                V.tensor_copy(cols[:, 6:7], cols[:, 0:1]).then_inc(S("k_new_ready"), 1)

            def bias(p, s):
                g, hh, qt = p.times(8, s), s // 4, s % 4
                q = cumq[:, qt, ds(p.times(2, hh).v, 1)]
                bank, off = ps[:, 4 + s % 2, :], P * qt
                wait(dve, S("sc_full"), g + 1)
                wait(dve, S("ncb_ready"), p.times(2, hh + 1))
                wait(dve, S("probs"), g + (-1 if s else 0))
                if qt:
                    V.scalar_tensor_tensor(out=sc[:, s % 2, 0:off], in0=bank[:, 0:off], scalar=q,
                                           in1=ncb[:, hh, 0:off], op0=ALU.add, op1=ALU.add)
                V.scalar_tensor_tensor(out=sc[:, s % 2, off:off + P], in0=bank[:, off:off + P], scalar=q,
                                       in1=ncbm[:, hh, off:off + P], op0=ALU.add, op1=ALU.add).then_inc(S("biased"), 1)
                wait(dve, S("biased"), g + 1)
                V.tensor_reduce(out=sm[:, 0, s % 2:s % 2 + 1], in_=sc[:, s % 2, 0:off + P], axis=AX.X, op=ALU.max,
                                negate=True).then_inc(S("row_max"), 1)

            def normalize(p, s):
                g, w = p.times(8, s), P * (s % 4 + 1)
                wait(dve, S("probs"), g + 1)
                V.reciprocal(sm[:, 2, s % 2:s % 2 + 1], sm[:, 1, s % 2:s % 2 + 1]).then_inc(S("row_inv"), 1)
                wait(dve, S("row_inv"), g + 1)
                V.tensor_scalar(pr[:, s % 2, 0:w], pr[:, s % 2, 0:w], sm[:, 2, s % 2:s % 2 + 1], None, ALU.mult
                                ).then_inc(S("pr_norm"), 1)

            def o_out(p):
                wait(dve, S("o_hi_ready"), p + 1)
                r = "p o t -> p (o t)"
                V.tensor_tensor(o_lo[:, ds(p.v, 1), 0:TP].rearrange(r), ps[:, 7, 0:TP],
                                o_hi[:, ds(p.v, 1), 0:TP].rearrange(r).bitcast(f32), ALU.subtract
                                ).then_inc(S("o_lo_ready"), 1)

            lo_next(At(0))
            k_out(At(0))
            lo_next(At(2))
            dve.wait_ge(S("lam_exp"), 1)
            w = [sc[:, 0, 64 * i:64 * i + NR] for i in range(3)]
            log1p_half(w[0], w[1], w[2], lru_c[:])
            lam = prm[:, C_LAM:C_LAM + NR]
            link(V.tensor_scalar(w[0], lam, -1.0, 0.0, ALU.mult, ALU.max))
            link(V.scalar_tensor_tensor(out=w[1], in0=w[1], scalar=2.0, in1=w[0], op0=ALU.mult, op1=ALU.add))
            link(V.tensor_scalar(lru_c[:], w[1], -2.0, None, ALU.mult))
            V.tensor_scalar(half_b[:], prm[:, C_RBA:C_RBA + 2 * NR], 0.5, None, ALU.mult).then_inc(S("half_b_ready"), 1)
            link(V.tensor_reduce(out=sc[:, 1, 0:TQ], in_=causal_w[:].rearrange("p h k -> p k h"), axis=AX.X, op=ALU.max))
            link(V.tensor_copy(new_mask[:].rearrange("p (b c) -> p b c", c=72)[:, :, 0:TQ],
                               sc[:, 1, 0:TQ].rearrange("p (o k) -> p o k", o=1).broadcast_to([P, NB, TQ])))
            k_rows(At(0))
            k_rows_known(At(0))

            def pair(j, p):
                bias(p, 0)
                bias(p, 1)
                normalize(p, 0)
                lo_next(j.times(3))
                bias(p, 2)
                normalize(p, 1)
                bias(p, 3)
                normalize(p, 2)
                k_out(j)
                bias(p, 4)
                normalize(p, 3)
                bias(p, 5)
                normalize(p, 4)
                lo_next(j.times(3, 2))
                bias(p, 6)
                normalize(p, 5)
                k_rows(j)
                k_rows_known(j)
                bias(p, 7)
                normalize(p, 6)
                normalize(p, 7)
                o_out(p)

            with dve.Fori(0, NPAIR // 2 - 1) as i:
                pair(At(1, 2, i), At(0, 2, i))
                pair(At(2, 2, i), At(1, 2, i))
            pair(At(NPAIR - 1), At(NPAIR - 2))
            p = At(NPAIR - 1)
            bias(p, 0)
            for s in range(1, 8):
                bias(p, s)
                normalize(p, s - 1)
            normalize(p, 7)
            o_out(p)

            dve.wait_ge(S("t_full"), T_LAST + 9)
            dve.wait_ge(S("lf_new_in"), 16 * NB)
            link(V.tensor_copy(lf_s[:, 0:PAST], ps[:, 6, 0:PAST]))
            link(V.tensor_tensor_scan(out=nc_s[:], data0=ones_s[:], data1=lf_s[:], initial=0.0,
                                      op0=ALU.mult, op1=ALU.subtract))
            V.tensor_tensor(cq_w[:], head_of[:],
                            nc_s[:, PAST:PAST + TQ].rearrange("p (o k) -> p o k", o=1).broadcast_to([P, NH, TQ]),
                            ALU.mult).then_inc(S("cq_w_ready"), 1)
            dve.wait_ge(S("cq_s_ready"), 1)

            def e_batch(b):
                wait(dve, S("s_full"), b + (-1))
                V.tensor_scalar(e_b[:, b.slot(2), :], head_of[:].rearrange("p h q -> p (h q)"),
                                batch_of[:, ds(b.v, 1)], None, ALU.mult).then_inc(S("e_b_ready"), 1)

            def kT_odd(b):
                for j in range(1, KD, 2):
                    wait(dve, S("kT_full"), b.times(KD, j + 1))
                    wait(dve, S("kT_used"), b.times(KD, j - 1))
                    V.tensor_copy(kT[:, 1, :], ps[:, 5, 0:PAST]).then_inc(S("kT_odd"), 1)

            def s_bias(b):
                s = b.slot(2)
                q = cq_s[:, ds(b.v, 1)]
                wait(dve, S("s_full"), b + 1)
                wait(dve, S("s_probs"), b + (-1))
                V.tensor_scalar(ss[:, s, 0:PAST], ps[:, 2 * s, 0:PAST], q, None, ALU.add)
                V.scalar_tensor_tensor(out=ss[:, s, PAST:SW], in0=ps[:, 2 * s + 1, 0:TS], scalar=q,
                                       in1=new_mask[:, ds(b.times(TS).v, TS)], op0=ALU.add, op1=ALU.add
                                       ).then_inc(S("s_biased"), 1)
                wait(dve, S("s_biased"), b + 1)
                V.tensor_reduce(out=sms[:, 0, s:s + 1], in_=ss[:, s, :], axis=AX.X, op=ALU.max, negate=True
                                ).then_inc(S("s_max"), 1)

            def s_normalize(b):
                s = b.slot(2)
                wait(dve, S("s_probs"), b + 1)
                V.reciprocal(sms[:, 2, s:s + 1], sms[:, 1, s:s + 1]).then_inc(S("s_inv"), 1)
                wait(dve, S("s_inv"), b + 1)
                V.tensor_scalar(ps_[:, s, :], ps_[:, s, :], sms[:, 2, s:s + 1], None, ALU.mult).then_inc(S("ps_norm"), 1)

            def s_out(b):
                for hh in range(2):
                    r = slice(64 * hh, 64 * hh + 64)
                    wait(dve, S("os_hi"), b.times(2, hh + 1))
                    o = ds(b.times(TQ, TP).v, TQ)
                    V.tensor_tensor(o_lo[r, :, o],
                                    ps[r, 7, 0:P].rearrange("p (j c) -> p j c", c=16)[:, :, TQ * hh:TQ * hh + TQ],
                                    o_hi[r, :, o].bitcast(f32), ALU.subtract).then_inc(S("os_lo"), 1)

            e_batch(At(0))
            kT_odd(At(0))
            s_bias(At(0))
            s_normalize(At(0))

            def sample(b, c):
                e_batch(b)
                kT_odd(b)
                s_bias(b)
                s_normalize(b)
                s_out(c)

            with dve.Fori(0, NB // 2 - 1) as i:
                sample(At(1, 2, i), At(0, 2, i))
                sample(At(2, 2, i), At(1, 2, i))
            sample(At(NB - 1), At(NB - 2))
            s_out(At(NB - 1))

            def add_z(sem, full, src, j, z):
                wait(dve, sem, full)
                wait(dve, S("z_added"), z + (1 - KD))
                V.tensor_tensor(halves(x_f[:, j, :]), halves(x_f[:, j, :]), src, ALU.add).then_inc(S("z_added"), 1)

            dve.wait_ge(S("x_scaled"), KD)
            for j in range(KD):
                m = At(M_AO + j)
                add_z(S("acc_full"), m + 1, acc(m), j, At(Z_AO + j))
                lo_next(At(N_AO + j))

            def norm(k):
                b = LN_BANK[k]
                rs = (ln_f, ln_f, ln_r, ln_f)[k][1]
                dve.wait_ge(S("ln_mean"), k + 1)
                for j in range(KD):
                    V.tensor_tensor(halves(x_f[:, j, :]), halves(x_f[:, j, :]), bank_pair(b), ALU.subtract
                                    ).then_inc(S("ln_centred"), 1)
                dve.wait_ge(S("ln_std"), k + 1)
                V.reciprocal(rs[:, 1, :], rs[:, 0, :]).then_inc(S("ln_rstd"), 1)
                dve.wait_ge(S("ln_rstd"), k + 1)
                for j in range(KD):
                    V.tensor_tensor(x_f[:, j, :], x_f[:, j, :], rs[:, 1, :], ALU.mult).then_inc(S("ln_scaled"), 1)
                if k < 3:
                    for j in range(KD):
                        x_lo_tile(k + 1, j)

            norm(0)

            def ffn(l, n0, m0, z0):
                def tile(F, n, m, par, f):
                    Fg = F + NF * l
                    s = F.slot(2)
                    lo_next(n)
                    col = lambda c: prm[:, ds((F + c).v, 1)]
                    wait(dve, S("gh_ready"), Fg + 1)
                    wait(dve, S("gh_hist"), Fg + 1)
                    wait(dve, S("gelu_ready"), Fg)
                    V.tensor_scalar(cv[:], gh[:, s, 0:CVW], col(C_FCW[l]), col(C_FCB + NF * l), ALU.mult, ALU.add
                                    ).then_inc(S("cv_tap"), 1)
                    for t in (1, 2):
                        wait(dve, S("cv_tap"), Fg.times(3, t))
                        V.scalar_tensor_tensor(out=cv[:], in0=gh[:, s, t:t + CVW], scalar=col(C_FCW[l] + NF * t),
                                               in1=cv[:], op0=ALU.mult, op1=ALU.add).then_inc(S("cv_tap"), 1)
                    lo_next(n + 1)
                    wait(dve, S("acc_full"), m + 2)
                    wait(dve, S("gelu_ready"), Fg + 1)
                    wait(dve, S("h_hi_ready"), Fg)
                    for src, t0, t1 in prompt_parts(2 * (m + 1).slot(2)):
                        V.tensor_tensor(hf[:, t0:t1], gl[:, t0:t1], src, ALU.mult)
                    src = ps[:, 2 * (m + 1).slot(2) + 1, TP - HT:HT].rearrange("p (b q) -> p b q", q=TQ)
                    V.tensor_tensor(hf[:, TP:T].rearrange("p (b q) -> p b q", q=TQ), strided(gl, TP + 2, 2 + TQ), src,
                                    ALU.mult).then_inc(S("h_ready"), 1)
                    wait(dve, S("h_hi_ready"), Fg + 1)
                    V.tensor_tensor(h_lo[:, par, f, :], hf[:], h_hi[:, par, f, :].bitcast(f32), ALU.subtract
                                    ).then_inc(S("h_lo_ready"), 1)

                def group(g, par, more):
                    n, m = g.times(12, n0 + 2), g.times(16, m0 + 2)
                    for f in range(1, GF):
                        tile(g.times(GF, f), n + 2 * (f - 1), m + 2 * (f - 1), par, f)
                    if more:
                        tile(g.times(GF, GF), n + 6, m + 6, 1 - par, 0)
                    k = 8 if more else 6
                    for c in range(4):
                        lo_next(n + (k + c))
                        for d in (2 * c, 2 * c + 1):
                            add_z(S("acc_full"), m + (k + d + 1), acc(m + (k + d)), d, g.times(KD, z0 + d))

                dve.wait_ge(S("gh_zero"), l + 1)
                tile(At(0), At(n0), At(m0), 0, 0)
                dve.wait_ge(S("x_scaled"), KD * (2 if l == 0 else 4))
                with dve.Fori(0, NG // 2 - 1) as i:
                    group(At(0, 2, i), 0, True)
                    group(At(1, 2, i), 1, True)
                group(At(NG - 2), 0, True)
                group(At(NG - 1), 1, False)

            ffn(0, N_F0, M_F0, Z_F0)
            norm(1)

            def convolve(j):
                s, u = j.slot(3), j.slot(3)
                col = lambda c: prm[:, ds((j + c).v, 1)]
                wait(dve, S("xr_ready"), j + 1)
                wait(dve, S("xr_hist"), j + 1)
                wait(dve, S("cx_tap"), j.times(5))
                V.tensor_scalar(cx[:, 0:CXW], xr[:, s, 0:CXW], col(C_RCW), col(C_RCB), ALU.mult, ALU.add).then_inc(S("cx_tap"), 1)
                for t in (1, 2):
                    wait(dve, S("cx_tap"), j.times(5, t))
                    V.scalar_tensor_tensor(out=cx[:, 0:CXW], in0=xr[:, s, t:t + CXW], scalar=col(C_RCW + NR * t), in1=cx[:, 0:CXW],
                                           op0=ALU.mult, op1=ALU.add).then_inc(S("cx_tap"), 1)
                wait(dve, S("cx_tap"), j.times(5, 3))
                c3 = col(C_RCW + 3 * NR)
                V.scalar_tensor_tensor(out=xc[:, u, 0:TP], in0=xr[:, s, 3:3 + TP], scalar=c3, in1=cx[:, 0:TP],
                                       op0=ALU.mult, op1=ALU.add).then_inc(S("cx_tap"), 1)
                seq = xr[:, s, 3 + TP:XRW].rearrange("p (b c) -> p b c", c=3 + TQ)
                V.scalar_tensor_tensor(out=xc[:, u, TP:T].rearrange("p (b q) -> p b q", q=TQ), in0=seq[:, :, 3:3 + TQ],
                                       scalar=c3, in1=strided(cx, TP + 3, 3 + TQ), op0=ALU.mult, op1=ALU.add
                                       ).then_inc(S("cx_tap"), 1)

            STEPS = 9

            def recur(j, u):
                def step(k, ins):
                    ins.then_inc(S("r_step"), 1)
                    wait(dve, S("r_step"), j.times(STEPS, k))

                first = lambda x: x[:, TP:T].rearrange("p (b q) -> p b q", q=TQ)[:, :, 0]
                wait(dve, S("om_ready"), j + 1)
                step(1, V.reciprocal(om[:], om[:]))
                step(2, V.scalar_tensor_tensor(out=aa[:], in0=tr[:], scalar=1.0, in1=om[:], op0=ALU.add, op1=ALU.mult))
                wait(dve, S("r_lo_ready"), j)
                step(3, V.scalar_tensor_tensor(out=uu[:], in0=ti[:], scalar=1.0, in1=xc[:, u, :], op0=ALU.add, op1=ALU.mult))
                wait(dve, S("sq_ready"), j + 1)
                step(4, V.tensor_tensor(sq[:], sq[:], om[:], ALU.mult))
                step(5, V.tensor_tensor(uu[:], uu[:], sq[:], ALU.mult))
                h0 = hist_r[:, ds(j.v, 1), 24:32].rearrange("p o b -> p (o b)")
                step(6, V.tensor_tensor(sq[:, 0:NB], first(aa), h0, ALU.mult))
                step(7, V.tensor_tensor(first(uu), first(uu), sq[:, 0:NB], ALU.add))
                step(8, V.memset(first(aa), 0.0))
                step(9, V.tensor_tensor_scan(out=om[:], data0=aa[:], data1=uu[:], initial=0.0, op0=ALU.mult, op1=ALU.add))
                V.tensor_copy(r_st[:, ds(j.v, 1), 27:28].rearrange("p o c -> p (o c)"), om[:, TP - 1:TP])
                V.tensor_copy(r_st[:, ds(j.v, 1), 28:36].rearrange("p o c -> p (o c)"),
                              om[:, TP:T].rearrange("p (b q) -> p b q", q=TQ)[:, :, TQ - 1]).then_inc(S("h_kept"), 1)
                V.tensor_tensor(uu[:], om[:], gate[:, u, :], ALU.mult).then_inc(S("r_ready"), 1)

            def r_low(j):
                r = "p o t -> p (o t)"
                wait(dve, S("r_hi_ready"), j + 1)
                V.tensor_tensor(r_lo[:, ds(j.v, 1), :].rearrange(r), uu[:],
                                r_hi[:, ds(j.v, 1), :].rearrange(r).bitcast(f32), ALU.subtract).then_inc(S("r_lo_ready"), 1)

            dve.wait_ge(S("rows_stored"), 32)
            dve.wait_ge(S("xr_zero"), 1)
            for j in range(2):
                lo_next(At(N_RI + 2 * j))
                convolve(At(j))
                lo_next(At(N_RI + 2 * j + 1))
            with dve.Fori(0, 3) as i:
                for u in range(3):
                    j = At(2 + u, 3, i)
                    lo_next(j.times(2, N_RI))
                    recur(At(u, 3, i), u)
                    convolve(j)
                    lo_next(j.times(2, N_RI + 1))
                    r_low(At(u, 3, i))
            for j in (NR - 2, NR - 1):
                recur(At(j), j % 3)
                r_low(At(j))
            dve.wait_ge(S("x_scaled"), 3 * KD)
            for q in range(4):
                for c in range(3):
                    lo_next(At(N_RO + 3 * q + c))
                for d in range(2):
                    add_z(S("ro_full"), 3 * q + 3, bank_pair(4 * (q % 2) + 2 * d), 2 * q + d, At(Z_RO + 2 * q + d))
            norm(2)
            dve.wait_ge(S("rows_stored"), 16 * 6)
            ffn(1, N_F1, M_F1, Z_F1)
            norm(3)
            for t in range(NQ + 1):
                w = min(P, T - P * t)
                dve.wait_ge(S("y_full"), t + 1)
                if t == 0:
                    dve.wait_ge(S("rows_stored"), 16 * 8)
                wait(dve, S(f"y_stored{t % 2}"), 16 * (t // 2))
                V.tensor_copy(y_tok[0:w, t % 2, 512:D], ps[0:w, 2 * (t % 2) + 1, 0:512]).then_inc(S("y_right"), 1)


INPUTS = ["x_prompt", "x_sample", "cache_k", "cache_v", "cache_logf", "page_table", "state_rglru_h",
          "state_rglru_conv", "state_ffn_conv", "ln_g", "ln_b", "w_attn_in", "b_forget", "w_attn_out", "w_rnn_in",
          "rnn_conv_w", "rnn_conv_b", "w_rg_a", "b_rg_a", "w_rg_i", "b_rg_i", "rg_lambda", "w_rnn_out",
          "w_ffn_in", "ffn_conv_w", "ffn_conv_b", "w_ffn_out"]
OUTPUTS = [("y_prompt", (1, TP, D)), ("y_sample", (NB, TQ, D)), ("k_prompt", (1, TP, 1, NH, HD)),
           ("v_prompt", (1, TP, 1, NH, HD)), ("logf_prompt", (1, TP, 1, NH)), ("k_sample", (NB, TQ, 1, NH, HD)),
           ("v_sample", (NB, TQ, 1, NH, HD)), ("logf_sample", (NB, TQ, 1, NH)), ("h_prompt", (1, 1, R)),
           ("h_sample", (1, NB, R)), ("rconv_prompt", (1, 1, 3, R)), ("rconv_sample", (1, NB, 3, R)),
           ("fconv_prompt", (2, 1, 2, FF)), ("fconv_sample", (2, NB, 2, FF))]


def kernel(**inputs):
    import numpy as np
    import concourse.bacc as bacc
    from concourse.bass_utils import run_bass_kernel_spmd

    nc = bacc.Bacc("TRN2", target_bir_lowering=False, num_devices=1)
    arrays, args = {}, {}
    for name in INPUTS:
        arr = np.ascontiguousarray(inputs[name])
        arrays["in_" + name] = arr
        args[name] = nc.dram_tensor("in_" + name, arr.shape, mybir.dt.from_np(arr.dtype), kind="ExternalInput").ap()
    for name, shape in OUTPUTS:
        args[name] = nc.dram_tensor("out_" + name, shape, mybir.dt.float32, kind="ExternalOutput").ap()
    build(nc, args)
    r = run_bass_kernel_spmd(nc, [arrays], core_ids=[0])
    return tuple(r.results[0]["out_" + name] for name, _ in OUTPUTS)
```

```python
import concourse.bass as bass
from concourse import mybir
from contextlib import ExitStack

P = 128
D = 1024
KD = D // P
TP, NB, TQ = 512, 8, 8
TS = NB * TQ
T = TP + TS
HT = T // 2
NQ = TP // P
NH, HD = 16, 64
NPAIR = NH // 2
NPG = 4
PAST = NPG * P
FF = 3 * D
NF = FF // P
GF = 4
NG = NF // GF
R = 1408
NR = R // P
RB = 88
ALPHA = 4.0 ** 0.25
EPS = 1e-5
NEG = -3.0e38
SW = PAST + TS
GHW = 2 + TP + NB * (2 + TQ)
CVW = GHW - 2
XRW = 3 + TP + NB * (3 + TQ)
CXW = XRW - 3
RING = 3
SLOT = KD * P

N_QKV = 0
N_AO = N_QKV + 3 * NPAIR
N_F0 = N_AO + KD
N_RI = N_F0 + 12 * NG
N_RO = N_RI + 2 * NR
N_F1 = N_RO + 12
N_END = N_F1 + 12 * NG
M_AO = 3 * NPAIR
M_F0 = M_AO + KD
M_RI = M_F0 + 16 * NG
M_F1 = M_RI + 2 * NR
Z_AO = 0
Z_F0 = KD
Z_RO = Z_F0 + NG * KD
Z_F1 = Z_RO + KD

C_LNG, C_LNB = 0, 32
C_RCB, C_RBA, C_RBI, C_LAM = 64, 75, 86, 97
C_RCW = 128
C_FCB = C_RCW + 4 * NR
C_FCW = (256, 384)


class At:

    def __init__(self, first, step=0, turn=None):
        self.first, self.step, self.turn = first, step, turn

    def __add__(self, k):
        return At(self.first + k, self.step, self.turn)

    def times(self, k, plus=0):
        return At(self.first * k + plus, self.step * k, self.turn)

    @property
    def v(self):
        return self.first if self.turn is None else self.turn * self.step + self.first

    def slot(self, r):
        assert self.turn is None or self.step % r == 0
        return self.first % r

    def round(self, r):
        return At(self.first // r, self.step // r, self.turn)


def wait(engine, sem, value):
    if isinstance(value, At):
        value = value.v
    if isinstance(value, int) and value <= 0:
        return
    engine.wait_ge(sem, value)


def build(nc, a):
    f32, f32r, i32 = mybir.dt.float32, mybir.dt.float32r, mybir.dt.int32
    ALU, ACT, AX = mybir.AluOpType, mybir.ActivationFunctionType, mybir.AxisListType
    ds = bass.ds
    ctx = ExitStack()
    with ctx:
        sems = {}

        def S(name):
            if name not in sems:
                sems[name] = ctx.enter_context(nc.semaphore(name))
            return sems[name]

        base = 16512
        top = [base]

        def sb(name, shape, dt=f32, at=None):
            size = 4
            for n in shape[1:]:
                size *= n
            size = (size + 31) // 32 * 32
            if at is None:
                off = top[0]
                top[0] += size
            else:
                off = at[0]
                at[0] += size
            assert off + size <= 229376, (name, off + size)
            return nc.alloc_sbuf_tensor_at(name, shape, dt, offset=off)

        ident = sb("ident", [P, P])
        over_d = sb("over_d", [P, P])
        prm = sb("prm", [P, 512])
        hist_f = sb("hist_f", [P, NF, 32])
        hist_r = sb("hist_r", [P, NR, 32])
        cols = sb("cols", [P, 8])
        lru_c = sb("lru_c", [P, NR])
        half_b = sb("half_b", [P, 2 * NR])
        x_f = sb("x_f", [P, KD, T])
        w_raw = sb("w_raw", [P, RING, SLOT])
        w_hi = sb("w_hi", [P, RING, SLOT], f32r)
        w_lo = sb("w_lo", [P, RING, SLOT], f32r)
        xhl_at = [top[0]]
        x_hi = sb("x_hi", [P, KD, T], f32r)
        x_lo = sb("x_lo", [P, KD, T], f32r)
        phase = top[0]

        at = [phase]
        o_hi = sb("o_hi", [P, KD, T], f32r, at)
        o_lo = sb("o_lo", [P, KD, T], f32r, at)
        v_new = sb("v_new", [P, D], f32, at)
        qT_s = sb("qT_s", [P, NPAIR, TS], f32, at)
        kT_s = sb("kT_s", [P, NPAIR, TS], f32, at)
        lf_pg = sb("lf_pg", [P, NPG, NB, NH], f32, at)
        lf_s = sb("lf_s", [P, PAST + TQ], f32, at)
        own_head = sb("own_head", [P, NH], f32, at)
        head_of = sb("head_of", [P, NH, TQ], f32, at)
        batch_of = sb("batch_of", [P, NB], f32, at)
        new_mask = sb("new_mask", [P, NB * 72], f32, at)
        causal_w = sb("causal_w", [P, NH, TQ], f32, at)
        ones_s = sb("ones_s", [P, PAST + TQ], f32, at)
        pages = sb("pages", [1, NB * NPG], i32, at)
        bf_col = sb("bf_col", [NH, 1], f32, at)
        pair_at = at[0]
        q_sb = sb("q_sb", [P, 2, T], f32, at)
        k_sb = sb("k_sb", [P, 2, T], f32, at)
        v_sb = sb("v_sb", [P, T], f32, at)
        v_tok = sb("v_tok", [P, 2, NQ, P], f32, at)
        k_tok = sb("k_tok", [P, NQ, P], f32, at)
        k_new = sb("k_new", [TS, P], f32, at)
        ncb = sb("ncb", [P, 2, TP], f32, at)
        ncbm = sb("ncbm", [P, 2, TP], f32, at)
        mask4 = sb("mask4", [P, NQ, P], f32, at)
        cumq = sb("cumq", [P, NQ, NH], f32, at)
        lf_tok = sb("lf_tok", [P, NQ + 1, NH], f32, at)
        sc = sb("sc", [P, 2, TP], f32, at)
        pr = sb("pr", [P, 2, TP], f32, at)
        prT = sb("prT", [P, NQ, TP], f32, at)
        sm = sb("sm", [P, 3, 2], f32, at)
        at0 = [pair_at]
        x_in = sb("x_in", [P, NQ + 1, D], f32, at0)
        assert at0[0] <= 229376
        at1 = [phase]
        prow = sb("prow", [P, 4, P], f32, at1)
        frow = sb("frow", [32, FF], f32, at1)
        rrow = sb("rrow", [32, R], f32, at1)
        wf = sb("wf", [P, KD, NH], f32, at1)
        fz = sb("fz", [NH, 7, T], f32, at1)
        assert at1[0] <= phase + 2 * KD * T * 4
        k_pg = sb("k_pg", [P, 2, NPG, D], f32, xhl_at)
        at2 = [pair_at]
        v_pg = sb("v_pg", [P, 2, NPG, D], f32, at2)
        kT = sb("kT", [P, 2, PAST], f32, xhl_at)
        assert xhl_at[0] <= phase
        qz = sb("qz", [P, 2, KD * 144], f32, at2)
        e_b = sb("e_b", [P, 2, P], f32, at2)
        nc_s = sb("nc_s", [P, PAST + TQ], f32, at2)
        cq_w = sb("cq_w", [P, NH, TQ], f32, at2)
        cq_s = sb("cq_s", [P, NB], f32, at2)
        ss = sb("ss", [P, 2, SW], f32, at2)
        psT = sb("psT", [P, NPG + 1, P], f32, at2)
        sms = sb("sms", [P, 3, 2], f32, at2)
        o_own = sb("o_own", [P, D], f32, at2)
        q_of = sb("q_of", [P, TQ], f32, at2)

        def norm_space(at, tag):
            return sb("ln_sq" + tag, [P, 2, T], f32, at), sb("ln_rstd" + tag, [P, 2, T], f32, at)

        atf = [phase]
        gh = sb("gh", [P, 2, GHW], f32, atf)
        cv = sb("cv", [P, CVW], f32, atf)
        gl = sb("gl", [P, GHW], f32, atf)
        hf = sb("hf", [P, T], f32, atf)
        h_hi = sb("h_hi", [P, 2, GF, T], f32r, atf)
        h_lo = sb("h_lo", [P, 2, GF, T], f32r, atf)
        f_st = sb("f_st", [P, NF, 2 + 2 * NB], f32, atf)
        f_rows = sb("f_rows", [2 + 2 * NB, FF], f32, atf)
        ln_f = norm_space(atf, "f")

        atr = [phase]
        r_hi = sb("r_hi", [P, NR, T], f32r, atr)
        r_lo = sb("r_lo", [P, NR, T], f32r, atr)
        r_end = atr[0]
        gate = sb("gate", [P, 3, T], f32, atr)
        xr = sb("xr", [P, 3, XRW], f32, atr)
        cx = sb("cx", [P, XRW], f32, atr)
        xc = sb("xc", [P, 3, T], f32, atr)
        tr = sb("tr", [P, T], f32, atr)
        ti = sb("ti", [P, T], f32, atr)
        om = sb("om", [P, T], f32, atr)
        sq = sb("sq", [P, T], f32, atr)
        aa = sb("aa", [P, T], f32, atr)
        uu = sb("uu", [P, T], f32, atr)
        rgw = sb("rgw", [P, 3, 3, 2, P], f32, atr)
        r_st = sb("r_st", [P, NR, 36], f32, atr)
        r_rows = sb("r_rows", [36, R], f32, [r_end])
        ln_r = norm_space([r_end + 8192], "r")
        y_tok = sb("y_tok", [P, 2, D], f32, [phase])

        ps = ctx.enter_context(nc.psum_tensor("ps", [P, 8, 512], f32))
        block = ctx.enter_context(nc.Block())

        def acc(m):
            b = 2 * m.slot(2)
            return ps[:, b:b + 2, 0:HT]

        def halves(x):
            return x.rearrange("p (a t) -> p a t", a=2)

        def bank_pair(b):
            return ps[:, b:b + 2, 0:HT]

        def prompt_parts(b):
            return [(ps[:, b, 0:HT], 0, HT), (ps[:, b + 1, 0:TP - HT], HT, TP)]

        def strided(x, first, step):
            return x[:, first:first + NB * step].rearrange("p (b c) -> p b c", c=step)[:, :, 0:TQ]

        xp = a["x_prompt"].rearrange("a (t p) d -> p (a t) d", p=P)
        xs = a["x_sample"].rearrange("a b d -> (a b) d")
        w_qkv = a["w_attn_in"].rearrange("a (k p) e -> p (a k) e", p=P)
        w_ao = a["w_attn_out"].rearrange("a (k p) e -> p (a k) e", p=P)
        w_ri = a["w_rnn_in"].rearrange("a (k p) e -> p (a k) e", p=P)
        w_ro = a["w_rnn_out"].rearrange("a (k p) e -> p (a k) e", p=P)
        w_fi = a["w_ffn_in"].rearrange("l (k p) e -> l p k e", p=P)
        w_fo = a["w_ffn_out"].rearrange("l (k p) e -> l p k e", p=P)
        ck = a["cache_k"].rearrange("n p a h d -> n p (a h d)")
        cvv = a["cache_v"].rearrange("n p a h d -> n p (a h d)")
        clf = a["cache_logf"].rearrange("n p a h -> n p (a h)")
        kp_o = a["k_prompt"].rearrange("a (t p) l h d -> p (a t) (l h d)", p=P)
        vp_o = a["v_prompt"].rearrange("a (t p) l h d -> p (a t) (l h d)", p=P)
        ks_o = a["k_sample"].rearrange("b q l h d -> (b q) (l h d)")
        vs_o = a["v_sample"].rearrange("b q l h d -> (b q) (l h d)")
        lp_o = a["logf_prompt"].rearrange("a (t p) l h -> p (a t) (l h)", p=P)
        ls_o = a["logf_sample"].rearrange("b q l h -> (b q) (l h)")
        yp_o = a["y_prompt"].rearrange("a (t p) d -> (a t) p d", p=P)
        ys_o = a["y_sample"].rearrange("a b d -> (a b) d")
        ncum_d = nc.dram_tensor("ncum_scratch", [NH, TP], f32, kind="Internal").ap()

        def load(sp, n, dst_cols, src):
            s = n.slot(RING)
            wait(sp, S("w_lo_ready"), n + (1 - RING))
            dst = w_raw[:, s, 0:dst_cols]
            k = src.shape[1]
            sp.dma_start(dst.rearrange("p (k e) -> p k e", k=k), src).then_inc(S(f"w_raw{s}"), 16)

        def split_hi(act, n, m_done, width=SLOT):
            s = n.slot(RING)
            wait(act, S(f"w_raw{s}"), n.round(RING).times(16, 16))
            if m_done is not None:
                wait(act, *m_done)
            nc.scalar.copy(w_hi[:, s, 0:width], w_raw[:, s, 0:width]).then_inc(S("w_hi_ready"), 1)

        def split_lo(dve, n, width=SLOT):
            s = n.slot(RING)
            wait(dve, S("w_hi_ready"), n + 1)
            nc.vector.tensor_tensor(w_lo[:, s, 0:width], w_raw[:, s, 0:width],
                                    w_hi[:, s, 0:width].bitcast(f32), ALU.subtract).then_inc(S("w_lo_ready"), 1)

        def width_of(n):
            first = n.first
            return 3 * 2 * P if N_RO <= first < N_F1 and (first - N_RO) % 3 == 2 else SLOT

        def products(pe, n, out, terms, half, first=True, last=True):
            s = n.slot(RING)
            for i, (t, hi, lo) in enumerate(terms):
                w_h, w_l = w_hi[:, s, t * P:(t + 1) * P], w_lo[:, s, t * P:(t + 1) * P]
                r = slice(half * HT, (half + 1) * HT)
                nc.tensor.matmul(out, w_h, hi[:, r], start=first and i == 0, stop=False)
                nc.tensor.matmul(out, w_h, lo[:, r], start=False, stop=False)
                done = nc.tensor.matmul(out, w_l, hi[:, r], start=False, stop=last and i == len(terms) - 1)
            return done

        def x_terms():
            return [(k, x_hi[:, k, :], x_lo[:, k, :]) for k in range(KD)]

        def unit_half(pe, n, m, half, terms):
            b = 2 * m.slot(2) + half
            return products(pe, n, ps[:, b, 0:HT], terms, half)

        @block.sync
        def _(sp):
            sp.dma_start(x_in[:, 0:NQ, :], xp).then_inc(S("x_in"), 16)
            sp.dma_start(x_in[0:TS, NQ, :], xs).then_inc(S("x_in"), 16)
            sp.dma_start(wf[:], w_qkv[:, :, 3 * D:3 * D + NH]).then_inc(S("wf_in"), 16)
            sp.dma_start(bf_col[:], a["b_forget"].rearrange("a h -> h a")).then_inc(S("wf_in"), 16)

            def qkv(j, n):
                for c, first in enumerate((D, 2 * D, 0)):
                    load(sp, n + c, SLOT, w_qkv[:, :, ds(j.times(P, first).v, P)])

            qkv(At(0), At(N_QKV))

            def rows(blk, r0, n, src):
                sp.dma_start(prow[r0:r0 + n, blk, :], src).then_inc(S("prm_in"), 16)

            rows(0, C_LNG, 32, a["ln_g"].rearrange("l s (k p) -> (l s k) p", p=P))
            rows(0, C_LNB, 32, a["ln_b"].rearrange("l s (k p) -> (l s k) p", p=P))
            rows(0, C_RCB, NR, a["rnn_conv_b"].rearrange("l (k p) -> (l k) p", p=P))
            rows(0, C_RBA, NR, a["b_rg_a"].rearrange("l (k p) -> (l k) p", p=P))
            rows(0, C_RBI, NR, a["b_rg_i"].rearrange("l (k p) -> (l k) p", p=P))
            rows(0, C_LAM, NR, a["rg_lambda"].rearrange("l (k p) -> (l k) p", p=P))
            rows(1, 0, 4 * NR, a["rnn_conv_w"].rearrange("l w (k p) -> (l w k) p", p=P))
            rows(1, 4 * NR, 2 * NF, a["ffn_conv_b"].rearrange("l (k p) -> (l k) p", p=P))
            for l in range(2):
                rows(2 + l, 0, 3 * NF, a["ffn_conv_w"][l].rearrange("w (k p) -> (w k) p", p=P))
            sp.dma_start(frow[:], a["state_ffn_conv"].rearrange("l b w f -> (l b w) f")).then_inc(S("prm_in"), 16)
            sp.dma_start(rrow[0:24, :], a["state_rglru_conv"].rearrange("l b w f -> (l b w) f")).then_inc(S("prm_in"), 16)
            sp.dma_start(rrow[24:32, :], a["state_rglru_h"].rearrange("l b f -> (l b) f")).then_inc(S("prm_in"), 16)

            with sp.Fori(0, NPAIR - 1) as i:
                qkv(At(1, 1, i), At(3, 3, i))
            for j in range(RING):
                load(sp, At(N_AO + j), SLOT, w_ao[:, :, P * j:P * (j + 1)])

            sp.wait_ge(S("pages_in"), 16)

            def page_loads(b):
                k_loads(b)
                v_loads(b)

            def numbers(b):
                return [sp.value_load(pages[0:1, ds(b.times(NPG, t).v, 1)], min_val=0, max_val=39) for t in range(NPG)]

            def k_loads(b):
                s, pgs = b.slot(2), numbers(b)
                wait(sp, S("s_full"), b + (-1))
                for t, pg in enumerate(pgs):
                    sp.dma_start(k_pg[:, s, t, :], ck[ds(pg, 1)].rearrange("n p e -> (n p) e")).then_inc(S(f"k_pg{s}"), 16)

            def v_loads(b):
                s, pgs = b.slot(2), numbers(b)
                wait(sp, S("pv_s_done"), b + (-1))
                for t, pg in enumerate(pgs):
                    sp.dma_start(v_pg[:, s, t, :], cvv[ds(pg, 1)].rearrange("n p e -> (n p) e")).then_inc(S(f"v_pg{s}"), 16)

            sp.wait_ge(S("acc_full"), M_AO)
            for b in range(2):
                k_loads(At(b))
            sp.wait_ge(S("o_lo_ready"), NPAIR)
            sp.wait_ge(S("kv_stored"), 64 * NPAIR)
            sp.wait_ge(S("qk_kept"), 2 * NPAIR)
            for b in range(2):
                v_loads(At(b))
            with sp.Fori(0, NB // 2 - 1) as i:
                page_loads(At(2, 2, i))
                page_loads(At(3, 2, i))

            for j in range(RING, KD):
                load(sp, At(N_AO + j), SLOT, w_ao[:, :, P * j:P * (j + 1)])

            def ffn(l, n0):
                def pair(F, n):
                    load(sp, n, SLOT, w_fi[l, :, :, ds(F.times(P).v, P)])
                    load(sp, n + 1, SLOT, w_fi[l, :, :, ds(F.times(P, FF).v, P)])

                def group(g, more):
                    n = g.times(12, n0 + 2)
                    for f in range(1, GF):
                        pair(g.times(GF, f), n + 2 * (f - 1))
                    if more:
                        pair(g.times(GF, GF), n + 6)
                    for c in range(4):
                        load(sp, n + ((8 if more else 6) + c), SLOT,
                             w_fo[l, :, ds(g.times(GF).v, GF), 2 * P * c:2 * P * (c + 1)])

                pair(At(0), At(n0))
                with sp.Fori(0, NG - 1) as i:
                    group(At(0, 1, i), True)
                group(At(NG - 1), False)

            ffn(0, N_F0)

            def rnn_in(j, n):
                load(sp, n, SLOT, w_ri[:, :, ds(j.times(P).v, P)])
                load(sp, n + 1, SLOT, w_ri[:, :, ds(j.times(P, R).v, P)])

            rnn_in(At(0), At(N_RI))
            rnn_in(At(1), At(N_RI + 2))
            with sp.Fori(0, 3) as i:
                for u in range(3):
                    rnn_in(At(2 + u, 3, i), At(N_RI + 4 + 2 * u, 6, i))
            for q in range(4):
                for c in range(3):
                    n = At(N_RO + 3 * q + c)
                    load(sp, n, width_of(n), w_ro[:, 4 * c:min(4 * c + 4, NR), 2 * P * q:2 * P * (q + 1)])
            ffn(1, N_F1)

        def scale_residual(pool, k):
            for j in range(KD):
                pool.wait_ge(S("x_lo_ready"), KD * k + j + 1)
                if k == 0:
                    ins = nc.gpsimd.tensor_scalar(x_f[:, j, :], x_f[:, j, :], ALPHA, 1.0, ALU.mult, ALU.mult)
                else:
                    c = C_LNB + KD * (k - 1) + j
                    ins = nc.gpsimd.tensor_scalar(x_f[:, j, :], x_f[:, j, :], prm[:, c:c + 1], ALPHA, ALU.add, ALU.mult)
                ins.then_inc(S("x_scaled"), 1)

        def ffn_pool(pool, l):
            nc.gpsimd.memset(gh[:, :, 0:2], 0.0).then_inc(S("gh_zero"), 1)

            def tile(F):
                Fg = F + NF * l
                s = F.slot(2)
                seq = gh[:, s, 2 + TP:GHW].rearrange("p (b c) -> p b c", c=2 + TQ)
                wait(pool, S("cv_tap"), Fg.times(3, -3))
                nc.gpsimd.tensor_copy(seq[:, :, 0:2],
                                      hist_f[:, ds(F.v, 1), 16 * l:16 * l + 16].rearrange("p o (b c) -> p (o b) c", c=2)
                                      ).then_inc(S("gh_hist"), 1)
                wait(pool, S("gh_ready"), Fg + 1)
                nc.gpsimd.tensor_copy(f_st[:, ds(F.v, 1), 0:2], gh[:, s, TP:TP + 2].rearrange("p (o c) -> p o c", o=1))
                nc.gpsimd.tensor_copy(f_st[:, ds(F.v, 1), 2:18].rearrange("p o (b c) -> p (o b) c", c=2),
                                      seq[:, :, TQ:TQ + 2]).then_inc(S("gh_kept"), 1)

            tile(At(0))
            tile(At(1))
            with pool.Fori(0, NF // 2 - 1) as i:
                tile(At(2, 2, i))
                tile(At(3, 2, i))
            pool.wait_ge(S("rows_ready"), (6, 15)[l])
            pool.dma_start(a["fconv_prompt"][l].rearrange("b w f -> (b w) f"), f_rows[0:2, :]).then_inc(S("rows_stored"), 16)
            pool.dma_start(a["fconv_sample"][l].rearrange("b w f -> (b w) f"), f_rows[2:18, :]).then_inc(S("rows_stored"), 16)

        @block.gpsimd
        def _(pool):
            link_n = [0]

            def link(ins):
                link_n[0] += 1
                ins.then_inc(S("pool_step"), 1)
                pool.wait_ge(S("pool_step"), link_n[0])

            link(nc.gpsimd.memset(ident[:], 0.0))
            nc.gpsimd.affine_select(out=ident[:], in_=ident[:], compare_op=ALU.not_equal, fill=1.0, base=0,
                                    pattern=[[-1, P]], channel_multiplier=1).then_inc(S("ident_ready"), 1)
            pool.dma_start(pages[:], a["page_table"].rearrange("b (o t) -> o (b t)", o=1)).then_inc(S("pages_in"), 16)
            nc.gpsimd.memset(cols[:, 0:1], EPS)
            nc.gpsimd.memset(cols[:, 1:2], 2.0 ** -116)
            nc.gpsimd.memset(ones_s[:], 1.0)
            link(nc.gpsimd.memset(over_d[:], 1.0 / D))
            link(nc.gpsimd.memset(head_of[:], 0.0))
            for b in range(NB):
                link(nc.gpsimd.affine_select(out=head_of[:], in_=head_of[:], compare_op=ALU.not_equal, fill=1.0,
                                             base=-NH * b, pattern=[[-1, NH], [0, TQ]], channel_multiplier=1))
            link(nc.gpsimd.memset(batch_of[:], 1.0))
            link(nc.gpsimd.affine_select(out=batch_of[:], in_=batch_of[:], compare_op=ALU.is_ge, fill=0.0, base=0,
                                         pattern=[[-NH, NB]], channel_multiplier=1))
            link(nc.gpsimd.affine_select(out=batch_of[:], in_=batch_of[:], compare_op=ALU.is_ge, fill=0.0,
                                         base=NH - 1, pattern=[[NH, NB]], channel_multiplier=-1))
            link(nc.gpsimd.memset(causal_w[:], 0.0))
            link(nc.gpsimd.affine_select(out=causal_w[:], in_=causal_w[:], compare_op=ALU.is_ge, fill=NEG, base=0,
                                         pattern=[[-TQ, NH], [-1, TQ]], channel_multiplier=1))
            link(nc.gpsimd.affine_select(out=causal_w[:], in_=causal_w[:], compare_op=ALU.is_ge, fill=NEG,
                                         base=TQ - 1, pattern=[[TQ, NH], [0, TQ]], channel_multiplier=-1))
            link(nc.gpsimd.memset(own_head[:], 1.0))
            link(nc.gpsimd.affine_select(out=own_head[:], in_=own_head[:], compare_op=ALU.is_ge, fill=0.0, base=0,
                                         pattern=[[-TQ, NH]], channel_multiplier=1))
            link(nc.gpsimd.affine_select(out=own_head[:], in_=own_head[:], compare_op=ALU.is_ge, fill=0.0,
                                         base=TQ - 1, pattern=[[TQ, NH]], channel_multiplier=-1))
            nc.gpsimd.memset(v_new[:], 0.0)
            nc.gpsimd.memset(new_mask[:], NEG).then_inc(S("masks_ready"), 1)
            pool.wait_ge(S("x_staged"), KD)
            link(nc.gpsimd.memset(mask4[:], 0.0))
            link(nc.gpsimd.affine_select(out=mask4[:], in_=mask4[:], compare_op=ALU.is_ge, fill=NEG, base=0,
                                         pattern=[[0, NQ], [-1, P]], channel_multiplier=1))
            pool.wait_ge(S("f_full"), 1)
            scale_residual(pool, 0)
            pool.wait_ge(S("ncum_ready"), 1)
            pool.dma_start(ncum_d, fz[:, 6, 0:TP]).then_inc(S("ncum_stored"), 16)
            for b in range(NB):
                pool.dma_start(lf_s[NH * b:NH * (b + 1), PAST:PAST + TQ],
                               fz[:, 5, TP + TQ * b:TP + TQ * (b + 1)]).then_inc(S("lf_new_in"), 16)
            pool.wait_ge(S("lf_tok_ready"), 1)
            pool.dma_start(lp_o, lf_tok[:, 0:NQ, :]).then_inc(S("lf_stored"), 16)
            pool.dma_start(ls_o, lf_tok[0:TS, NQ, :]).then_inc(S("lf_stored"), 16)
            pool.wait_ge(S("ncum_stored"), 16)
            pool.wait_ge(S("pages_in"), 16)

            def pair(j):
                s = j.slot(2)
                def decay_rows(hh):
                    wait(pool, S("biased"), j.times(8, 4 * hh + 4 - 8))
                    pool.dma_start(ncb[:, hh, :], ncum_d[ds(j.times(2, hh).v, 1), :].broadcast_to([P, TP])
                                   ).then_inc(S("ncb_in"), 16)
                    wait(pool, S("ncb_in"), j.times(32, 16 * hh + 16))
                    nc.gpsimd.tensor_tensor(ncbm[:, hh, :], ncb[:, hh, :],
                                            mask4[:].rearrange("p t k -> p (t k)"), ALU.add
                                            ).then_inc(S("ncb_ready"), 1)

                wait(pool, S("k_ready"), j + 1)
                nc.gpsimd.tensor_copy(kT_s[:, ds(j.v, 1), :], k_sb[:, s, TP:T]).then_inc(S("qk_kept"), 1)
                decay_rows(0)
                for t in range(NPG):
                    pg = pool.value_load(pages[0:1, ds(j.times(NPG, t).v, 1)], min_val=0, max_val=39)
                    pool.dma_start(lf_pg[:, t, ds(j.v, 1), :], clf[ds(pg, 1)].rearrange("n p h -> (n p) h")
                                   ).then_inc(S("lf_pg_in"), 16)
                wait(pool, S("k_new_ready"), j + 1)
                wait(pool, S("v_new_ready"), j + 1)
                pool.dma_start(kp_o[:, :, ds(j.times(P).v, P)], k_tok[:]).then_inc(S("kv_stored"), 16)
                pool.dma_start(ks_o[:, ds(j.times(P).v, P)], k_new[:]).then_inc(S("kv_stored"), 16)
                pool.dma_start(vp_o[:, :, ds(j.times(P).v, P)], v_tok[:, s]).then_inc(S("kv_stored"), 16)
                pool.dma_start(vs_o[:, ds(j.times(P).v, P)], v_new[0:TS, ds(j.times(P).v, P)]).then_inc(S("kv_stored"), 16)
                decay_rows(1)
                wait(pool, S("q_ready"), j + 1)
                nc.gpsimd.tensor_copy(qT_s[:, ds(j.v, 1), :], q_sb[:, s, TP:T]).then_inc(S("qk_kept"), 1)

            pair(At(0))
            pair(At(1))
            with pool.Fori(0, NPAIR // 2 - 1) as i:
                pair(At(2, 2, i))
                pair(At(3, 2, i))

            pool.wait_ge(S("o_lo_ready"), NPAIR)
            pool.wait_ge(S("kv_stored"), 64 * NPAIR)
            nc.gpsimd.memset(psT[:], 0.0).then_inc(S("psT_zero"), 1)
            nc.gpsimd.memset(qz[:], 0.0).then_inc(S("qz_zero"), 1)
            pool.wait_ge(S("qz_zero"), 1)

            def sample(b):
                s = b.slot(2)
                v = qz[:, s, :].rearrange("p (j c) -> p j c", c=144)
                wait(pool, S("s_full"), b + (-1))
                for hh in range(2):
                    nc.gpsimd.tensor_copy(v[64 * hh:64 * hh + 64, :, TQ * hh:TQ * hh + TQ],
                                          qT_s[64 * hh:64 * hh + 64, :, ds(b.times(TQ).v, TQ)]
                                          ).then_inc(S("qz_ready"), 1)

            sample(At(0))
            with pool.Fori(0, NB // 2 - 1) as i:
                sample(At(1, 2, i))
                sample(At(2, 2, i))
            sample(At(NB - 1))

            scale_residual(pool, 1)
            ffn_pool(pool, 0)
            scale_residual(pool, 2)

            pool.wait_ge(S("rows_stored"), 32)
            nc.gpsimd.memset(xr[:, :, 0:3], 0.0).then_inc(S("xr_zero"), 1)
            nc.gpsimd.memset(xc[:, 2, :], 0.0).then_inc(S("xc_zero"), 1)
            pieces = [0, 0, 0]

            def gate_weights(j):
                s = j % 3
                wait(pool, S("rg_full"), j - 2)
                nc.gpsimd.memset(rgw[:, s], 0.0).then_inc(S("rgw_zero"), 1)
                pool.wait_ge(S("rgw_zero"), j + 1)
                for i in range(max(j - 1, 0), min(j + 2, NR)):
                    for blk in range(NH):
                        r0, r1 = max(RB * blk, P * i), min(RB * blk + RB, P * i + P)
                        c0, c1 = max(RB * blk, P * j), min(RB * blk + RB, P * j + P)
                        if r0 >= r1 or c0 >= c1:
                            continue
                        for q, w in enumerate(("w_rg_a", "w_rg_i")):
                            pool.dma_start(rgw[r0 - P * i:r1 - P * i, s, i - j + 1, q, c0 - P * j:c1 - P * j],
                                           a[w][0, blk, r0 - RB * blk:r1 - RB * blk, c0 - RB * blk:c1 - RB * blk]
                                           ).then_inc(S(f"rgw_in{s}"), 16)
                            pieces[s] += 1

            def gate_weights_in(j):
                pool.wait_ge(S(f"rgw_in{j % 3}"), 16 * pieces[j % 3])
                nc.gpsimd.memset(cols[:, 2 + j % 3:3 + j % 3], 0.0).then_inc(S("rgw_ready"), 1)

            def conv_pool(j):
                s = j % 3
                hist = xr[:, s, 3 + TP:XRW].rearrange("p (b c) -> p b c", c=3 + TQ)
                wait(pool, S("cx_tap"), 5 * (j - 2))
                nc.gpsimd.tensor_copy(hist[:, :, 0:3], hist_r[:, j, 0:24].rearrange("p (b c) -> p b c", c=3)
                                      ).then_inc(S("xr_hist"), 1)
                pool.wait_ge(S("xr_ready"), j + 1)
                nc.gpsimd.tensor_copy(r_st[:, j, 0:3], xr[:, s, TP:TP + 3])
                nc.gpsimd.tensor_copy(r_st[:, j, 3:27].rearrange("p (b c) -> p b c", c=3),
                                      hist[:, :, TQ:TQ + 3]).then_inc(S("xr_kept"), 1)

            for j in range(NR):
                gate_weights(j)
                conv_pool(j)
                gate_weights_in(j)

            pool.wait_ge(S("rows_ready"), 9)
            pool.dma_start(a["rconv_prompt"].rearrange("l b w f -> (l b w) f"), r_rows[0:3, :]).then_inc(S("rows_stored"), 16)
            pool.dma_start(a["rconv_sample"].rearrange("l b w f -> (l b w) f"), r_rows[3:27, :]).then_inc(S("rows_stored"), 16)
            pool.dma_start(a["h_prompt"].rearrange("l b f -> (l b) f"), r_rows[27:28, :]).then_inc(S("rows_stored"), 16)
            pool.dma_start(a["h_sample"].rearrange("l b f -> (l b) f"), r_rows[28:36, :]).then_inc(S("rows_stored"), 16)
            scale_residual(pool, 3)
            pool.wait_ge(S("rows_stored"), 16 * 6)
            ffn_pool(pool, 1)

            for t in range(NQ + 1):
                pool.wait_ge(S("y_left"), t + 1)
                pool.wait_ge(S("y_right"), t + 1)
                if t < NQ:
                    pool.dma_start(yp_o[t], y_tok[:, t % 2, :]).then_inc(S(f"y_stored{t % 2}"), 16)
                else:
                    pool.dma_start(ys_o, y_tok[0:TS, t % 2, :]).then_inc(S(f"y_stored{t % 2}"), 16)
            pool.wait_ge(S("y_stored0"), 16 * 3)
            pool.wait_ge(S("y_stored1"), 16 * 2)
            pool.wait_ge(S("rows_stored"), 16 * 8)
            pool.wait_ge(S("kv_stored"), 64 * NPAIR)
            pool.wait_ge(S("lf_stored"), 32)

        T_ORDER = ["T0", "T1", "T2", "k0", "T3", "k1", "T4", "v0", "T5", "v1", "T6", "T7"]
        T_LAST = 4 + 12 * (NPAIR - 1)

        def t_use(what, j):
            if j is None:
                return At(T_LAST + int(what[1]))
            if j.turn is None and j.first == 0:
                return At(["k0", "k1", "v0", "v1"].index(what))
            return j.times(12, 4 - 12 + T_ORDER.index(what))

        LN_BANK = (4, 4, 0, 4)
        Z_END = (Z_AO, Z_F0 + KD * (NG - 1), Z_RO, Z_F1 + KD * (NG - 1))
        ROW_BANKS = {1: (6, 7, 6, 7, 6, 7), 2: (4, 5, 6), 3: (6, 7, 6, 7, 6, 7)}
        ROWS_BEFORE = {1: 0, 2: 6, 3: 9}

        @block.tensor
        def _(pe):
            def transpose(out, in_):
                k = in_.shape[0]
                return nc.tensor.transpose(out, in_, ident[0:k, 0:k])

            pe.wait_ge(S("ident_ready"), 1)
            pe.wait_ge(S("x_in"), 32)
            for j in range(KD):
                b = 4 + 2 * (j % 2)
                wait(pe, S("x_f_ready"), j - 1)
                for t in range(NQ):
                    transpose(ps[:, b, P * t:P * t + P], x_in[:, t, P * j:P * j + P])
                transpose(ps[:, b + 1, 0:TS], x_in[0:TS, NQ, P * j:P * j + P]).then_inc(S("x_staged"), 1)
            pe.wait_ge(S("wf_in"), 32)
            pe.wait_ge(S("x_f_ready"), KD)
            for half in range(2):
                for k in range(KD):
                    last = nc.tensor.matmul(ps[0:NH, 4 + half, 0:HT], wf[:, k, :], x_f[:, k, HT * half:HT * half + HT],
                                            start=k == 0, stop=k == KD - 1)
            last.then_inc(S("f_full"), 1)
            pe.wait_ge(S("x_lo_ready"), KD)

            def qkv(j, first, count):
                for term in range(first, first + count):
                    c, half, k = term // (2 * KD), term // KD % 2, term % KD
                    n = j.times(3, c)
                    if term % (2 * KD) == 0:
                        wait(pe, S("w_lo_ready"), n + 1)
                        wait(pe, *((S("v_ready"), j), (S("q_ready"), j), (S("k_ready"), j + 1))[c])
                    last = products(pe, n, ps[:, 2 * n.slot(2) + half, 0:HT], x_terms()[k:k + 1], half,
                                    first=k == 0, last=k == KD - 1)
                    if term % (2 * KD) == 2 * KD - 1:
                        last.then_inc(S("acc_full"), 1)

            def token_rows(j, what):
                src = (k_sb[:, j.slot(2), :] if what[0] == "k" else v_sb[:, :])
                wait(pe, S("k_ready" if what[0] == "k" else "v_ready"), j + 1)
                wait(pe, S("t_free"), t_use(what, j))
                if what[1] == "0":
                    for t in range(NQ):
                        last = transpose(ps[:, 6, P * t:P * t + P], src[:, P * t:P * t + P])
                else:
                    last = transpose(ps[:, 6, 0:P], src[:, T - P:T])
                last.then_inc(S("t_full"), 1)

            def scores(p, s):
                g, hh, qt = p.times(8, s), s // 4, s % 4
                if s == 0:
                    wait(pe, S("q_ready"), p + 1)
                wait(pe, S("biased"), g + (-1 if s else 0))
                r = slice(64 * hh, 64 * hh + 64)
                nc.tensor.matmul(ps[:, 4 + s % 2, 0:P * (qt + 1)], q_sb[r, p.slot(2), P * qt:P * qt + P],
                                 k_sb[r, p.slot(2), 0:P * (qt + 1)], start=True, stop=True
                                 ).then_inc(S("sc_full"), 1)

            def prob_rows(p, s, j):
                g, qt = p.times(8, s), s % 4
                wait(pe, S("pr_norm"), g + 1)
                wait(pe, S("t_free"), t_use(f"T{s}", j))
                for kt in range(qt + 1):
                    last = transpose(ps[:, 6, P * kt:P * kt + P], pr[:, s % 2, P * kt:P * kt + P])
                last.then_inc(S("t_full"), 1)

            def values(p, hh, j):
                wait(pe, S("t_free"), t_use(f"T{4 * hh + 3}", j) + 1)
                if hh == 0:
                    wait(pe, S("o_lo_ready"), p)
                r = slice(64 * hh, 64 * hh + 64)
                for kt in range(NQ):
                    last = nc.tensor.matmul(ps[r, 7, P * kt:TP], v_tok[:, p.slot(2), kt, r], prT[:, kt, P * kt:TP],
                                            start=kt == 0, stop=kt == NQ - 1)
                last.then_inc(S("pv_done"), 1)

            qkv(At(0), 0, 6 * KD)
            pe.wait_ge(S("prm_in"), 16 * 13)
            for blk, n in enumerate((C_LAM + NR, 4 * NR + 2 * NF, 3 * NF, 3 * NF)):
                last = transpose(ps[:, 6, P * blk:P * blk + n], prow[0:n, blk, :])
            last.then_inc(S("prm_full"), 1)
            for F in range(16):
                last = transpose(ps[:, 7, 32 * F:32 * F + 32], frow[:, P * F:P * F + P])
            last.then_inc(S("prm_full"), 1)
            pe.wait_ge(S("prm_ready"), 1)
            for F in range(16, NF):
                last = transpose(ps[:, 6, 32 * F - 512:32 * F - 480], frow[:, P * F:P * F + P])
            last.then_inc(S("prm_full"), 1)
            pe.wait_ge(S("prm_ready"), 2)
            for j in range(NR):
                last = transpose(ps[:, 7, 32 * j:32 * j + 32], rrow[:, P * j:P * j + P])
            last.then_inc(S("prm_full"), 1)
            pe.wait_ge(S("prm_ready"), 4)
            pe.wait_ge(S("ncum_ready"), 1)
            for t in range(NQ):
                transpose(ps[:, 6, NH * t:NH * t + NH], fz[:, 6, P * t:P * t + P])
            for t in range(NQ + 1):
                w = min(P, T - P * t)
                last = transpose(ps[0:w, 6, 64 + NH * t:64 + NH * t + NH], fz[:, 5, P * t:P * t + w])
            last.then_inc(S("lf_full"), 1)
            pe.wait_ge(S("lf_tok_ready"), 1)
            for what in ("k0", "k1", "v0", "v1"):
                token_rows(At(0), what)

            def pair(j, p):
                scores(p, 0)
                qkv(j, 0, 3)
                if p.turn is not None or p.first:
                    values(p + (-1), 1, j + (-1))
                scores(p, 1)
                qkv(j, 3, 4)
                prob_rows(p, 0, j)
                scores(p, 2)
                qkv(j, 7, 5)
                prob_rows(p, 1, j)
                scores(p, 3)
                qkv(j, 12, 5)
                prob_rows(p, 2, j)
                scores(p, 4)
                qkv(j, 17, 4)
                token_rows(j, "k0")
                qkv(j, 21, 3)
                prob_rows(p, 3, j)
                scores(p, 5)
                qkv(j, 24, 4)
                token_rows(j, "k1")
                qkv(j, 28, 3)
                values(p, 0, j)
                prob_rows(p, 4, j)
                scores(p, 6)
                qkv(j, 31, 4)
                token_rows(j, "v0")
                qkv(j, 35, 3)
                prob_rows(p, 5, j)
                scores(p, 7)
                qkv(j, 38, 4)
                token_rows(j, "v1")
                qkv(j, 42, 3)
                prob_rows(p, 6, j)
                qkv(j, 45, 3)
                prob_rows(p, 7, j)

            pair(At(1), At(0))
            with pe.Fori(0, NPAIR // 2 - 1) as i:
                pair(At(2, 2, i), At(1, 2, i))
                pair(At(3, 2, i), At(2, 2, i))
            last_pair = At(NPAIR - 1)
            scores(last_pair, 0)
            values(last_pair + (-1), 1, last_pair)
            for s in range(1, 8):
                scores(last_pair, s)
                prob_rows(last_pair, s - 1, None)
                if s == 5:
                    values(last_pair, 0, None)
            prob_rows(last_pair, 7, None)
            values(last_pair, 1, None)

            pe.wait_ge(S("lf_pg_in"), 16 * NB * NPG)
            pe.wait_ge(S("t_free"), T_LAST + 8)
            for t in range(NPG):
                last = transpose(ps[:, 6, P * t:P * t + P], lf_pg[:, t, :, :].rearrange("p b h -> p (b h)"))
            last.then_inc(S("t_full"), 1)
            pe.wait_ge(S("cq_w_ready"), 1)
            pe.wait_ge(S("o_lo_ready"), NPAIR)
            nc.tensor.matmul(ps[:, 7, 0:NB], cq_w[:].rearrange("p h q -> p (h q)"), batch_of[:], start=True, stop=True
                             ).then_inc(S("cq_full"), 1)

            def s_scores(b, c=None):
                s = b.slot(2)
                bk = 2 * s
                wait(pe, S(f"k_pg{s}"), b.round(2).times(64, 64))
                wait(pe, S("qz_ready"), b.times(2, 2))
                wait(pe, S("e_b_ready"), b + 1)

                def k_columns(j):
                    ready = S("kT_even" if j % 2 == 0 else "kT_odd")
                    wait(pe, ready, b.times(4, j // 2))
                    for t in range(NPG):
                        last = transpose(ps[:, 4 + j % 2, P * t:P * t + P], k_pg[:, s, t, P * j:P * j + P])
                    last.then_inc(S("kT_full"), 1)

                def add(j):
                    wait(pe, S("kT_even" if j % 2 == 0 else "kT_odd"), b.times(4, j // 2 + 1))
                    if j == 0:
                        wait(pe, S("o_own_ready"), b + (-1))
                    q = qz[:, s, P * j:P * j + P]
                    nc.tensor.matmul(ps[:, bk, 0:PAST], q, kT[:, j % 2, :], start=j == 0, stop=False)
                    nc.tensor.matmul(ps[:, bk + 1, 0:TS], q, kT_s[:, j, :], start=j == 0, stop=False
                                     ).then_inc(S("kT_used"), 1)

                k_columns(0)
                for j in range(1, KD):
                    k_columns(j)
                    add(j - 1)
                    if j == 2 and c is not None:
                        s_outputs(c)
                add(KD - 1)
                nc.tensor.matmul(ps[:, bk, 0:PAST], e_b[:, s, :], nc_s[:, 0:PAST], start=False, stop=True)
                new = nc_s[:, PAST:PAST + TQ].rearrange("p (o k) -> p o k", o=1).broadcast_to([P, NB, TQ])
                nc.tensor.matmul(ps[:, bk + 1, 0:TS].rearrange("p (b k) -> p b k", b=NB), e_b[:, s, :], new,
                                 start=False, stop=True).then_inc(S("s_full"), 1)

            def s_values(b):
                s = b.slot(2)
                wait(pe, S("ps_norm"), b + 1)
                wait(pe, S("psT_ready"), b)
                wait(pe, S("os_lo"), NB - 2 if b.turn is None and b.first == NB - 1 else b)
                for t in range(NPG):
                    transpose(ps[:, 6, P * t:P * t + P], ss[:, s, P * t:P * t + P])
                transpose(ps[0:TS, 7, P:2 * P], ss[:, s, PAST:SW]).then_inc(S("psT_full"), 1)
                wait(pe, S("psT_ready"), b + 1)
                wait(pe, S(f"v_pg{s}"), b.round(2).times(64, 64))
                for half in range(2):
                    r = slice(512 * half, 512 * half + 512)
                    for t in range(NPG + 1):
                        v = v_pg[:, s, t, r] if t < NPG else v_new[:, r]
                        last = nc.tensor.matmul(ps[:, 2 * s + half, :], psT[:, t, :], v, start=t == 0, stop=t == NPG)
                last.then_inc(S("pv_s_done"), 1)

            def s_outputs(b):
                wait(pe, S("o_own_ready"), b + 1)
                wait(pe, S("os_lo"), b)
                for j in range(KD):
                    last = nc.tensor.matmul(ps[:, 7, TQ * j:TQ * j + TQ], o_own[:, P * j:P * j + P], q_of[:],
                                            start=True, stop=True)
                last.then_inc(S("os_full"), 1)

            pe.wait_ge(S("cq_s_ready"), 1)
            pe.wait_ge(S("psT_zero"), 1)
            pe.wait_ge(S("q_ready"), NPAIR)
            pe.wait_ge(S("k_ready"), NPAIR)
            pe.wait_ge(S("v_ready"), NPAIR)
            pe.wait_ge(S("qk_kept"), 2 * NPAIR)
            s_scores(At(0))
            s_scores(At(1))
            s_values(At(0))
            with pe.Fori(0, NB // 2 - 1) as i:
                s_scores(At(2, 2, i), At(0, 2, i))
                s_values(At(1, 2, i))
                s_scores(At(3, 2, i), At(1, 2, i))
                s_values(At(2, 2, i))
            s_values(At(NB - 1))
            s_outputs(At(NB - 2))
            s_outputs(At(NB - 1))

            pe.wait_ge(S("os_lo"), NB)
            pe.wait_ge(S("s_biased"), NB)
            for j in range(KD):
                n = At(N_AO + j)
                wait(pe, S("w_lo_ready"), n + 1)
                wait(pe, S("z_added"), Z_AO + j - 1)
                for half in range(2):
                    last = unit_half(pe, n, At(M_AO + j), half, [(k, o_hi[:, k, :], o_lo[:, k, :]) for k in range(KD)])
                last.then_inc(S("acc_full"), 1)

            def norm(k):
                b = LN_BANK[k]
                if k == 2:
                    pe.wait_ge(S("z_added"), Z_RO + 6)
                for j in range(KD):
                    pe.wait_ge(S("z_added"), Z_END[k] + j + 1)
                    for half in range(2):
                        last = nc.tensor.matmul(ps[:, b + half, 0:HT], over_d[:], x_f[:, j, HT * half:HT * half + HT],
                                                start=j == 0, stop=j == KD - 1)
                last.then_inc(S("ln_mean"), 1)
                sq_t = (ln_f, ln_f, ln_r, ln_f)[k][0]
                if k % 2:
                    pe.wait_ge(S("rows_ready"), ROWS_BEFORE[k] + 6)
                for j in range(KD):
                    pe.wait_ge(S("ln_sq_ready"), KD * k + j + 1)
                    for half in range(2):
                        last = nc.tensor.matmul(ps[:, b + 2 + half, 0:HT], over_d[:],
                                                sq_t[:, j % 2, HT * half:HT * half + HT],
                                                start=j == 0, stop=j == KD - 1)
                    last.then_inc(S("ln_sq_used"), 1)
                if k == 2:
                    pe.wait_ge(S("z_added"), Z_RO + KD)
                    pe.wait_ge(S("xr_kept"), NR)
                    pe.wait_ge(S("h_kept"), NR)
                    for i in range(3):
                        rows(k, i)

            def rows(k, i):
                src, n, w = (r_st, NR, 36) if k == 2 else (f_st, NF, 18)
                wait(pe, S("rows_ready"), ROWS_BEFORE[k] + max(i - 1, 0))
                for c in range(4 * i, min(4 * i + 4, n)):
                    last = transpose(ps[0:w, ROW_BANKS[k][i], P * (c % 4):P * (c % 4) + P], src[:, c, :])
                last.then_inc(S("rows_full"), 1)

            def opening(n, m, before):
                wait(pe, S("w_lo_ready"), n + 2)
                for k in range(KD):
                    wait(pe, S("x_lo_ready"), before + k + 1)
                    for c in range(2):
                        for half in range(2):
                            last = products(pe, n + c, ps[:, 2 * (m + c).slot(2) + half, 0:HT], x_terms()[k:k + 1], half,
                                            first=k == 0, last=k == KD - 1)
                        if k == KD - 1:
                            last.then_inc(S("acc_full"), 1)

            norm(0)

            def ffn(l, n0, m0, z0):
                def inner(F, n, m, n_waits=()):
                    Fg = F + NF * l
                    for c in range(2):
                        wait(pe, S("w_lo_ready"), n + c + 1)
                        wait(pe, S("gh_ready" if c == 0 else "h_ready"), Fg)
                        for sem, value in n_waits:
                            wait(pe, sem, value)
                        for half in range(2):
                            last = unit_half(pe, n + c, m + c, half, x_terms())
                        last.then_inc(S("acc_full"), 1)

                def outer(g, par, n, m):
                    wait(pe, S("h_lo_ready"), g.times(GF, NF * l + GF))
                    more = not (g.turn is None and g.first == NG - 1)
                    for c in range(4):
                        wait(pe, S("w_lo_ready"), n + c + 1)
                        for d in (2 * c, 2 * c + 1):
                            if d < 2:
                                nxt = g.times(GF, NF * l + GF)
                                wait(pe, S("gh_ready" if d == 0 else "h_ready"), nxt + (1 if more else 0))
                            else:
                                wait(pe, S("z_added"), g.times(KD, z0 + d - 1))
                            for half in range(2):
                                terms = [(2 * f + d % 2, h_hi[:, par, f, :], h_lo[:, par, f, :]) for f in range(GF)]
                                last = unit_half(pe, n + c, m + d, half, terms)
                            last.then_inc(S("acc_full"), 1)
                            if not more and d < 6:
                                if d == 0:
                                    pe.wait_ge(S("gh_kept"), NF * (l + 1))
                                rows(2 * l + 1, d)

                def group(g, par, more):
                    n, m = g.times(12, n0 + 2), g.times(16, m0 + 2)
                    for f in range(1, GF):
                        out_before = [(S("z_added"), g.times(KD, z0))] if f == 1 else []
                        inner(g.times(GF, f), n + 2 * (f - 1), m + 2 * (f - 1), out_before)
                    if more:
                        inner(g.times(GF, GF), n + 6, m + 6)
                    k = 8 if more else 6
                    outer(g, par, n + k, m + k)

                opening(At(n0), At(m0), KD * (1 if l == 0 else 3))
                with pe.Fori(0, NG // 2 - 1) as i:
                    group(At(0, 2, i), 0, True)
                    group(At(1, 2, i), 1, True)
                group(At(NG - 2), 0, True)
                group(At(NG - 1), 1, False)

            ffn(0, N_F0, M_F0, Z_F0)
            norm(1)

            def in_proj(j, c):
                n, m = j.times(2, N_RI + c), j.times(2, M_RI + c)
                wait(pe, S("w_lo_ready"), n + 1)
                wait(pe, S("gate_ready" if c == 0 else "xr_ready"), j)
                for half in range(2):
                    last = unit_half(pe, n, m, half, x_terms())
                last.then_inc(S("acc_full"), 1)

            def gates(j, sources, u):
                wait(pe, S("rgw_ready"), j + 1)
                wait(pe, S("cx_tap"), min(5 * (j.first + 2), 5 * NR) if j.turn is None else j.times(5, 10))
                wait(pe, S("rg_read"), j)
                for q in range(2):
                    for half in range(2):
                        for i in sources:
                            last = nc.tensor.matmul(ps[:, 4 + 2 * q + half, 0:HT], rgw[:, u, i + 1, q, :],
                                                    xc[:, (u + i) % 3, HT * half:HT * half + HT],
                                                    start=i == sources[0], stop=i == sources[-1])
                last.then_inc(S("rg_full"), 1)

            pe.wait_ge(S("xc_zero"), 1)
            opening(At(N_RI), At(M_RI), 2 * KD)
            in_proj(At(1), 0)
            in_proj(At(1), 1)
            with pe.Fori(0, 3) as i:
                for u in range(3):
                    j = At(2 + u, 3, i)
                    in_proj(j, 0)
                    in_proj(j, 1)
                    gates(At(u, 3, i), (-1, 0, 1), u)

            def out_proj(q, c):
                n = At(N_RO + 3 * q + c)
                tiles = range(4 * c, min(4 * c + 4, NR))
                wait(pe, S("w_lo_ready"), n + 1)
                wait(pe, S("r_lo_ready"), tiles[-1] + 1)
                for d in range(2):
                    for half in range(2):
                        terms = [(2 * (k - 4 * c) + d, r_hi[:, k, :], r_lo[:, k, :]) for k in tiles]
                        last = products(pe, n, ps[:, 4 * (q % 2) + 2 * d + half, 0:HT], terms, half,
                                        first=c == 0, last=c == 2)
                last.then_inc(S("ro_full"), 1)

            pe.wait_ge(S("gate_ready"), NR)
            pe.wait_ge(S("xr_ready"), NR)
            out_proj(0, 0)
            gates(At(NR - 2), (-1, 0, 1), (NR - 2) % 3)
            out_proj(0, 1)
            gates(At(NR - 1), (-1, 0), (NR - 1) % 3)
            out_proj(0, 2)
            pe.wait_ge(S("rg_read"), NR)
            for q in range(1, 4):
                wait(pe, S("z_added"), Z_RO + 2 * (q - 1) if q >= 2 else 0)
                for c in range(3):
                    out_proj(q, c)
            norm(2)
            ffn(1, N_F1, M_F1, Z_F1)
            norm(3)

            pe.wait_ge(S("x_f_ready"), 2 * KD)
            for t in range(NQ + 1):
                w = min(P, T - P * t)
                wait(pe, S("y_left"), t - 1)
                wait(pe, S("y_right"), t - 1)
                for j in range(KD):
                    last = transpose(ps[0:w, 2 * (t % 2) + j // 4, P * (j % 4):P * (j % 4) + P], x_f[:, j, P * t:P * t + w])
                last.then_inc(S("y_full"), 1)

        @block.scalar
        def _(act):
            def hi_next(n, done):
                if n.turn is not None or n.first + RING < N_END:
                    split_hi(act, n + RING, done, width_of(n + RING))

            for j in range(KD):
                act.wait_ge(S("x_f_ready"), j + 1)
                nc.scalar.copy(x_hi[:, j, :], x_f[:, j, :]).then_inc(S("x_hi_ready"), 1)
            for n in range(RING):
                split_hi(act, At(n), None)
            act.wait_ge(S("f_logits"), 1)
            nc.scalar.activation(fz[:, 0, :], fz[:, 1, :], ACT.Abs).then_inc(S("f_abs"), 1)
            act.wait_ge(S("f_abs"), 1)
            nc.scalar.activation(fz[:, 0, :], fz[:, 0, :], ACT.Exp, scale=-1.0).then_inc(S("f_exp"), 1)

            def q_out(j):
                wait(act, S("acc_full"), j.times(3, 3))
                wait(act, S("qk_kept"), j.times(2, -2))
                nc.scalar.mul(halves(q_sb[:, j.slot(2), :]), acc(j.times(3, 2)), HD ** -0.5).then_inc(S("q_ready"), 1)
                hi_next(j.times(3, 2), (S("acc_full"), j.times(3, 3)))

            def v_out(j):
                wait(act, S("acc_full"), j.times(3, 2))
                nc.scalar.copy(halves(v_sb[:]), acc(j.times(3, 1))).then_inc(S("v_ready"), 1)
                hi_next(j.times(3, 1), (S("acc_full"), j.times(3, 2)))

            def v_rows(j, part):
                wait(act, S("t_full"), t_use(f"v{part}", j) + 1)
                if part == 0:
                    wait(act, S("kv_stored"), j.times(64))
                    nc.scalar.copy(v_tok[:, j.slot(2)].rearrange("p t e -> p (t e)"), ps[:, 6, 0:TP]).then_inc(S("t_free"), 1)
                else:
                    nc.scalar.copy(v_new[0:TS, ds(j.times(P).v, P)], ps[P - TS:P, 6, 0:P]).then_inc(S("t_free"), 1)
                    wait(act, S("t_free"), t_use("v1", j) + 1)
                    nc.scalar.copy(cols[:, 5:6], cols[:, 0:1]).then_inc(S("v_new_ready"), 1)

            def exps(p, s):
                g, w = p.times(8, s), P * (s % 4 + 1)
                wait(act, S("row_max"), g + 1)
                nc.scalar.activation(pr[:, s % 2, 0:w], sc[:, s % 2, 0:w], ACT.Exp, bias=sm[:, 0, s % 2:s % 2 + 1],
                                     accum_out=sm[:, 1, s % 2:s % 2 + 1]).then_inc(S("probs"), 1)

            def prob_columns(p, s, j):
                qt = s % 4
                wait(act, S("t_full"), t_use(f"T{s}", j) + 1)
                wait(act, S("pv_done"), p.times(2, s // 4))
                nc.scalar.copy(prT[:, 0:qt + 1, P * qt:P * qt + P],
                               ps[:, 6, 0:P * (qt + 1)].rearrange("p (t k) -> p t k", k=P)).then_inc(S("t_free"), 1)

            def o_out(p):
                wait(act, S("pv_done"), p.times(2, 2))
                nc.scalar.copy(o_hi[:, ds(p.v, 1), 0:TP].rearrange("p o t -> p (o t)"), ps[:, 7, 0:TP]).then_inc(S("o_hi_ready"), 1)

            act.wait_ge(S("masks_ready"), 1)
            hi_next(At(0), (S("acc_full"), 1))
            v_out(At(0))
            q_out(At(0))
            for i, (dst, bank, w) in enumerate(((prm[:], 6, 512), (hist_f[:, 0:16, :], 7, 512),
                                                (hist_f[:, 16:NF, :], 6, 256), (hist_r[:], 7, 32 * NR))):
                act.wait_ge(S("prm_full"), i + 1)
                src = ps[:, bank, 0:w]
                if i == 0:
                    for blk, n in enumerate((C_LAM + NR, 4 * NR + 2 * NF, 3 * NF, 3 * NF)):
                        last = nc.scalar.copy(prm[:, P * blk:P * blk + n], ps[:, 6, P * blk:P * blk + n])
                    last.then_inc(S("prm_ready"), 1)
                else:
                    nc.scalar.copy(dst, src.rearrange("p (c w) -> p c w", w=32)).then_inc(S("prm_ready"), 1)
            lam = prm[:, C_LAM:C_LAM + NR]
            act.wait_ge(S("prm_ready"), 4)
            nc.scalar.activation(lru_c[:], lam, ACT.Abs).then_inc(S("lam_abs"), 1)
            act.wait_ge(S("lam_abs"), 1)
            nc.scalar.activation(lru_c[:], lru_c[:], ACT.Exp, scale=-1.0).then_inc(S("lam_exp"), 1)
            act.wait_ge(S("lf_full"), 1)
            nc.scalar.mul(cumq[:], ps[:, 6, 0:64].rearrange("p (t h) -> p t h", h=NH), -1.0)
            nc.scalar.copy(lf_tok[:, 0:NQ, :], ps[:, 6, 64:64 + NH * NQ].rearrange("p (t h) -> p t h", h=NH))
            nc.scalar.copy(lf_tok[0:TS, NQ, :], ps[0:TS, 6, 64 + NH * NQ:64 + NH * (NQ + 1)]).then_inc(S("lf_tok_ready"), 1)
            v_rows(At(0), 0)
            v_rows(At(0), 1)
            act.wait_ge(S("ncum_stored"), 16)
            act.wait_ge(S("lf_new_in"), 16 * NB)

            def pair(j, p):
                exps(p, 0)
                if p.turn is not None or p.first:
                    o_out(p + (-1))
                exps(p, 1)
                prob_columns(p, 0, j)
                exps(p, 2)
                prob_columns(p, 1, j)
                exps(p, 3)
                hi_next(j.times(3), (S("acc_full"), j.times(3, 1)))
                prob_columns(p, 2, j)
                exps(p, 4)
                prob_columns(p, 3, j)
                exps(p, 5)
                v_out(j)
                prob_columns(p, 4, j)
                exps(p, 6)
                v_rows(j, 0)
                prob_columns(p, 5, j)
                exps(p, 7)
                v_rows(j, 1)
                prob_columns(p, 6, j)
                q_out(j)
                prob_columns(p, 7, j)

            pair(At(1), At(0))
            with act.Fori(0, NPAIR // 2 - 1) as i:
                pair(At(2, 2, i), At(1, 2, i))
                pair(At(3, 2, i), At(2, 2, i))
            p = At(NPAIR - 1)
            exps(p, 0)
            o_out(p + (-1))
            for s in range(1, 8):
                exps(p, s)
                prob_columns(p, s - 1, None)
            prob_columns(p, 7, None)
            o_out(p)

            act.wait_ge(S("cq_full"), 1)
            nc.scalar.mul(cq_s[:], ps[:, 7, 0:NB], -1.0).then_inc(S("cq_s_ready"), 1)

            def kT_even(b):
                for j in range(0, KD, 2):
                    wait(act, S("kT_full"), b.times(KD, j + 1))
                    wait(act, S("kT_used"), b.times(KD, j - 1))
                    nc.scalar.copy(kT[:, 0, :], ps[:, 4, 0:PAST]).then_inc(S("kT_even"), 1)

            def s_exp(b):
                s = b.slot(2)
                wait(act, S("s_max"), b + 1)
                nc.scalar.activation(ss[:, s, :], ss[:, s, :], ACT.Exp, bias=sms[:, 0, s:s + 1],
                                     accum_out=sms[:, 1, s:s + 1]).then_inc(S("s_probs"), 1)

            def s_columns(b):
                wait(act, S("psT_full"), b + 1)
                nc.scalar.copy(psT[:, 0:NPG, :].rearrange("p t c -> p (t c)"), ps[:, 6, 0:PAST])
                nc.scalar.copy(psT[0:TS, NPG, :], ps[0:TS, 7, P:2 * P]).then_inc(S("psT_ready"), 1)

            def s_out(b):
                wait(act, S("os_full"), b + 1)
                nc.scalar.copy(o_hi[:, :, ds(b.times(TQ, TP).v, TQ)],
                               ps[:, 7, 0:KD * TQ].rearrange("p (j q) -> p j q", q=TQ)).then_inc(S("os_hi"), 1)

            act.wait_ge(S("psT_zero"), 1)
            kT_even(At(0))
            s_exp(At(0))

            def sample(b, c, o):
                kT_even(b)
                if o is not None:
                    s_out(o)
                s_columns(c)
                s_exp(b)

            sample(At(1), At(0), None)
            with act.Fori(0, NB // 2 - 1) as i:
                sample(At(2, 2, i), At(1, 2, i), At(0, 2, i))
                sample(At(3, 2, i), At(2, 2, i), At(1, 2, i))
            s_columns(At(NB - 1))
            s_out(At(NB - 2))
            s_out(At(NB - 1))
            for j in range(KD):
                hi_next(At(N_AO + j), (S("acc_full"), M_AO + j + 1))

            def norm(k):
                b = LN_BANK[k]
                sq_t, rs = (ln_f, ln_f, ln_r, ln_f)[k]
                for j in range(KD):
                    act.wait_ge(S("ln_centred"), KD * k + j + 1)
                    wait(act, S("ln_sq_used"), KD * k + j - 1)
                    nc.scalar.activation(sq_t[:, j % 2, :], x_f[:, j, :], ACT.Square).then_inc(S("ln_sq_ready"), 1)
                act.wait_ge(S("ln_sq_used"), KD * (k + 1))
                nc.scalar.activation(halves(rs[:, 0, :]), bank_pair(b + 2), ACT.Sqrt, bias=cols[:, 0:1]
                                     ).then_inc(S("ln_std"), 1)
                for j in range(KD):
                    h = prm[:, C_LNB + KD * k + j:C_LNB + KD * k + j + 1]
                    act.wait_ge(S("ln_scaled"), KD * k + j + 1)
                    if k < 3:
                        nc.scalar.activation(x_hi[:, j, :], x_f[:, j, :], ACT.Identity, bias=h).then_inc(S("x_hi_ready"), 1)
                    else:
                        nc.scalar.activation(x_f[:, j, :], x_f[:, j, :], ACT.Identity, bias=h).then_inc(S("x_f_ready"), 1)
                if k == 2:
                    for i in range(3):
                        rows(k, i)

            def rows(k, i):
                dst, w, n = (r_rows, 36, R) if k == 2 else (f_rows, 18, FF)
                act.wait_ge(S("rows_full"), ROWS_BEFORE[k] + i + 1)
                c0, c1 = 512 * i, min(512 * i + 512, n)
                nc.scalar.copy(dst[:, c0:c1], ps[0:w, ROW_BANKS[k][i], 0:c1 - c0]).then_inc(S("rows_ready"), 1)

            norm(0)

            def ffn(l, n0, m0):
                def tile(F, n, m, par, f):
                    Fg = F + NF * l
                    s = F.slot(2)
                    wait(act, S("acc_full"), m + 1)
                    wait(act, S("cv_tap"), Fg.times(3, -3))
                    wait(act, S("gh_kept"), Fg + (-1))
                    for src, t0, t1 in prompt_parts(2 * m.slot(2)):
                        nc.scalar.copy(gh[:, s, 2 + t0:2 + t1], src)
                    seq = gh[:, s, 2 + TP:GHW].rearrange("p (b c) -> p b c", c=2 + TQ)
                    src = ps[:, 2 * m.slot(2) + 1, TP - HT:HT].rearrange("p (b q) -> p b q", q=TQ)
                    nc.scalar.copy(seq[:, :, 2:2 + TQ], src).then_inc(S("gh_ready"), 1)
                    hi_next(n, (S("acc_full"), m + 1))
                    wait(act, S("cv_tap"), Fg.times(3, 3))
                    wait(act, S("h_ready"), Fg)
                    nc.scalar.activation(gl[:, 0:CVW], cv[:], ACT.Gelu_apprx_tanh).then_inc(S("gelu_ready"), 1)
                    wait(act, S("acc_full"), m + 2)
                    hi_next(n + 1, (S("acc_full"), m + 2))
                    wait(act, S("h_ready"), Fg + 1)
                    nc.scalar.copy(h_hi[:, par, f, :], hf[:]).then_inc(S("h_hi_ready"), 1)

                def group(g, par, more):
                    n, m = g.times(12, n0 + 2), g.times(16, m0 + 2)
                    for f in range(1, GF):
                        tile(g.times(GF, f), n + 2 * (f - 1), m + 2 * (f - 1), par, f)
                    if more:
                        tile(g.times(GF, GF), n + 6, m + 6, 1 - par, 0)
                    k = 8 if more else 6
                    for c in range(4):
                        hi_next(n + (k + c), (S("acc_full"), m + (k + 2 * c + 2)))
                        if not more and c < 3:
                            rows(2 * l + 1, 2 * c)
                            rows(2 * l + 1, 2 * c + 1)

                act.wait_ge(S("x_lo_ready"), KD * (2 if l == 0 else 4))
                tile(At(0), At(n0), At(m0), 0, 0)
                with act.Fori(0, NG // 2 - 1) as i:
                    group(At(0, 2, i), 0, True)
                    group(At(1, 2, i), 1, True)
                group(At(NG - 2), 0, True)
                group(At(NG - 1), 1, False)

            ffn(0, N_F0, M_F0)
            norm(1)

            def y_out(j, u):
                m = j.times(2, M_RI)
                wait(act, S("acc_full"), m + 1)
                wait(act, S("r_ready"), j + (-2))
                nc.scalar.activation(halves(gate[:, u, :]), acc(m), ACT.Gelu_apprx_tanh).then_inc(S("gate_ready"), 1)
                hi_next(j.times(2, N_RI), (S("acc_full"), m + 1))

            def x_out(j):
                m, s = j.times(2, M_RI + 1), j.slot(3)
                wait(act, S("acc_full"), m + 1)
                wait(act, S("cx_tap"), j.times(5, -10))
                wait(act, S("xr_kept"), j + (-2))
                for src, t0, t1 in prompt_parts(2 * m.slot(2)):
                    nc.scalar.copy(xr[:, s, 3 + t0:3 + t1], src)
                seq = xr[:, s, 3 + TP:XRW].rearrange("p (b c) -> p b c", c=3 + TQ)
                src = ps[:, 2 * m.slot(2) + 1, TP - HT:HT].rearrange("p (b q) -> p b q", q=TQ)
                nc.scalar.copy(seq[:, :, 3:3 + TQ], src).then_inc(S("xr_ready"), 1)
                hi_next(j.times(2, N_RI + 1), (S("acc_full"), m + 1))

            def gates(j):
                wait(act, S("rg_full"), j + 1)
                wait(act, S("r_ready"), j)
                col = lambda t, c: t[:, ds((j + c).v, 1)]
                nc.scalar.activation(halves(tr[:]), bank_pair(4), ACT.Tanh, bias=col(half_b, 0), scale=0.5
                                     ).then_inc(S("tr_half"), 1)
                nc.scalar.activation(halves(ti[:]), bank_pair(6), ACT.Tanh, bias=col(half_b, NR), scale=0.5
                                     ).then_inc(S("rg_read"), 1)
                wait(act, S("tr_half"), j + 1)
                nc.scalar.activation(tr[:], tr[:], ACT.Tanh, bias=col(lru_c, 0), scale=col(lru_c, 0)
                                     ).then_inc(S("tr_ready"), 1)
                wait(act, S("tr_ready"), j + 1)
                nc.scalar.activation(om[:], tr[:], ACT.Identity, bias=1.0, scale=-1.0).then_inc(S("om_ready"), 1)
                nc.scalar.activation(sq[:], tr[:], ACT.Sqrt, bias=cols[:, 1:2], scale=-1.0).then_inc(S("sq_ready"), 1)

            def r_out(j):
                wait(act, S("r_ready"), j + 1)
                nc.scalar.copy(r_hi[:, ds(j.v, 1), :].rearrange("p o t -> p (o t)"), uu[:]).then_inc(S("r_hi_ready"), 1)

            act.wait_ge(S("rows_stored"), 32)
            act.wait_ge(S("half_b_ready"), 1)
            for j in range(2):
                y_out(At(j), j)
                x_out(At(j))
            with act.Fori(0, 3) as i:
                for u in range(3):
                    j = At(2 + u, 3, i)
                    y_out(j, (2 + u) % 3)
                    x_out(j)
                    gates(At(u, 3, i))
                    r_out(At(u, 3, i))
            for c, j in enumerate((NR - 2, NR - 1)):
                gates(At(j))
                r_out(At(j))
                hi_next(At(N_RO + c), (S("ro_full"), c + 1))
            for c in range(2, 12):
                hi_next(At(N_RO + c), (S("ro_full"), c + 1))
            norm(2)
            act.wait_ge(S("rows_stored"), 16 * 6)
            ffn(1, N_F1, M_F1)
            norm(3)
            for t in range(NQ + 1):
                w = min(P, T - P * t)
                act.wait_ge(S("y_full"), t + 1)
                if t == 0:
                    act.wait_ge(S("rows_stored"), 16 * 8)
                wait(act, S(f"y_stored{t % 2}"), 16 * (t // 2))
                nc.scalar.copy(y_tok[0:w, t % 2, 0:512], ps[0:w, 2 * (t % 2), 0:512]).then_inc(S("y_left"), 1)

        @block.vector
        def _(dve):
            link_n = [0]

            def link(ins):
                link_n[0] += 1
                ins.then_inc(S("dve_step"), 1)
                dve.wait_ge(S("dve_step"), link_n[0])

            def lo_next(n):
                if n.turn is not None or n.first + RING < N_END:
                    split_lo(dve, n + RING, width_of(n + RING))

            V = nc.vector

            def x_lo_tile(j):
                dve.wait_ge(S("x_hi_ready"), j + 1)
                dve.wait_ge(S("x_f_ready"), j + 1)
                V.tensor_tensor(x_lo[:, j, :], x_f[:, j, :], x_hi[:, j, :].bitcast(f32), ALU.subtract
                                ).then_inc(S("x_lo_ready"), 1)

            for j in range(KD):
                b = 4 + 2 * (j % 2)
                dve.wait_ge(S("x_staged"), j + 1)
                V.tensor_copy(x_f[:, j, 0:TP], ps[:, b, 0:TP])
                V.tensor_copy(x_f[:, j, TP:T], ps[:, b + 1, 0:TS]).then_inc(S("x_f_ready"), 1)
                if j:
                    x_lo_tile(j - 1)
            x_lo_tile(KD - 1)
            for n in range(RING):
                split_lo(dve, At(n))

            def log1p_half(s, r, s2, e):
                link(V.tensor_scalar(r, e, 2.0, None, ALU.add))
                link(V.reciprocal(r, r))
                link(V.tensor_tensor(s, e, r, ALU.mult))
                link(V.tensor_tensor(s2, s, s, ALU.mult))
                link(V.tensor_scalar(r, s2, 1.0 / 17, None, ALU.mult))
                for k in (15, 13, 11, 9, 7, 5, 3):
                    link(V.scalar_tensor_tensor(out=r, in0=r, scalar=1.0 / k, in1=s2, op0=ALU.add, op1=ALU.mult))
                link(V.scalar_tensor_tensor(out=r, in0=r, scalar=1.0, in1=s, op0=ALU.add, op1=ALU.mult))

            dve.wait_ge(S("f_full"), 1)
            dve.wait_ge(S("wf_in"), 32)
            V.tensor_scalar(halves(fz[:, 1, :]), ps[0:NH, 4:6, 0:HT], bf_col[:], None, ALU.add
                            ).then_inc(S("f_logits"), 1)
            dve.wait_ge(S("f_exp"), 1)
            link(V.tensor_scalar(fz[:, 1, :], fz[:, 1, :], 0.0, None, ALU.min))
            log1p_half(fz[:, 3, :], fz[:, 2, :], fz[:, 4, :], fz[:, 0, :])
            link(V.scalar_tensor_tensor(out=fz[:, 5, :], in0=fz[:, 2, :], scalar=-2.0, in1=fz[:, 1, :],
                                        op0=ALU.mult, op1=ALU.add))
            dve.wait_ge(S("masks_ready"), 1)
            V.tensor_tensor_scan(out=fz[:, 6, 0:TP], data0=ones_s[0:NH, 0:TP], data1=fz[:, 5, 0:TP], initial=0.0,
                                 op0=ALU.mult, op1=ALU.subtract).then_inc(S("ncum_ready"), 1)

            def k_out(j):
                wait(dve, S("acc_full"), j.times(3, 1))
                wait(dve, S("qk_kept"), j.times(2, -2))
                V.tensor_copy(halves(k_sb[:, j.slot(2), :]), acc(j.times(3))).then_inc(S("k_ready"), 1)

            def k_rows(j, part):
                wait(dve, S("t_full"), t_use(f"k{part}", j) + 1)
                if part == 0:
                    wait(dve, S("kv_stored"), j.times(64))
                    V.tensor_copy(k_tok[:].rearrange("p t e -> p (t e)"), ps[:, 6, 0:TP]).then_inc(S("t_free"), 1)
                else:
                    V.tensor_copy(k_new[:], ps[P - TS:P, 6, 0:P]).then_inc(S("t_free"), 1)
                    wait(dve, S("t_free"), t_use("k1", j) + 1)
                    V.tensor_copy(cols[:, 6:7], cols[:, 0:1]).then_inc(S("k_new_ready"), 1)

            def bias(p, s):
                g, hh, qt = p.times(8, s), s // 4, s % 4
                q = cumq[:, qt, ds(p.times(2, hh).v, 1)]
                bank, off = ps[:, 4 + s % 2, :], P * qt
                wait(dve, S("sc_full"), g + 1)
                wait(dve, S("ncb_ready"), p.times(2, hh + 1))
                wait(dve, S("probs"), g + (-1 if s else 0))
                if qt:
                    V.scalar_tensor_tensor(out=sc[:, s % 2, 0:off], in0=bank[:, 0:off], scalar=q,
                                           in1=ncb[:, hh, 0:off], op0=ALU.add, op1=ALU.add)
                V.scalar_tensor_tensor(out=sc[:, s % 2, off:off + P], in0=bank[:, off:off + P], scalar=q,
                                       in1=ncbm[:, hh, off:off + P], op0=ALU.add, op1=ALU.add).then_inc(S("biased"), 1)
                wait(dve, S("biased"), g + 1)
                V.tensor_reduce(out=sm[:, 0, s % 2:s % 2 + 1], in_=sc[:, s % 2, 0:off + P], axis=AX.X, op=ALU.max,
                                negate=True).then_inc(S("row_max"), 1)

            def normalize(p, s):
                g, w = p.times(8, s), P * (s % 4 + 1)
                wait(dve, S("probs"), g + 1)
                V.reciprocal(sm[:, 2, s % 2:s % 2 + 1], sm[:, 1, s % 2:s % 2 + 1]).then_inc(S("row_inv"), 1)
                wait(dve, S("row_inv"), g + 1)
                V.tensor_scalar(pr[:, s % 2, 0:w], pr[:, s % 2, 0:w], sm[:, 2, s % 2:s % 2 + 1], None, ALU.mult
                                ).then_inc(S("pr_norm"), 1)

            def o_out(p):
                wait(dve, S("o_hi_ready"), p + 1)
                r = "p o t -> p (o t)"
                V.tensor_tensor(o_lo[:, ds(p.v, 1), 0:TP].rearrange(r), ps[:, 7, 0:TP],
                                o_hi[:, ds(p.v, 1), 0:TP].rearrange(r).bitcast(f32), ALU.subtract
                                ).then_inc(S("o_lo_ready"), 1)

            k_out(At(0))
            for n in range(3):
                lo_next(At(n))
            dve.wait_ge(S("lam_exp"), 1)
            w = [sc[:, 0, 64 * i:64 * i + NR] for i in range(3)]
            log1p_half(w[0], w[1], w[2], lru_c[:])
            lam = prm[:, C_LAM:C_LAM + NR]
            link(V.tensor_scalar(w[0], lam, -1.0, 0.0, ALU.mult, ALU.max))
            link(V.scalar_tensor_tensor(out=w[1], in0=w[1], scalar=2.0, in1=w[0], op0=ALU.mult, op1=ALU.add))
            link(V.tensor_scalar(lru_c[:], w[1], -2.0, None, ALU.mult))
            V.tensor_scalar(half_b[:], prm[:, C_RBA:C_RBA + 2 * NR], 0.5, None, ALU.mult).then_inc(S("half_b_ready"), 1)
            link(V.tensor_reduce(out=sc[:, 1, 0:TQ], in_=causal_w[:].rearrange("p h k -> p k h"), axis=AX.X, op=ALU.max))
            link(V.tensor_copy(new_mask[:].rearrange("p (b c) -> p b c", c=72)[:, :, 0:TQ],
                               sc[:, 1, 0:TQ].rearrange("p (o k) -> p o k", o=1).broadcast_to([P, NB, TQ])))
            k_rows(At(0), 0)
            k_rows(At(0), 1)

            def pair(j, p):
                bias(p, 0)
                if p.turn is not None or p.first:
                    o_out(p + (-1))
                bias(p, 1)
                normalize(p, 0)
                bias(p, 2)
                normalize(p, 1)
                bias(p, 3)
                k_out(j)
                normalize(p, 2)
                bias(p, 4)
                lo_next(j.times(3))
                normalize(p, 3)
                k_rows(j, 0)
                bias(p, 5)
                normalize(p, 4)
                k_rows(j, 1)
                bias(p, 6)
                normalize(p, 5)
                lo_next(j.times(3, 1))
                bias(p, 7)
                normalize(p, 6)
                normalize(p, 7)
                lo_next(j.times(3, 2))

            pair(At(1), At(0))
            with dve.Fori(0, NPAIR // 2 - 1) as i:
                pair(At(2, 2, i), At(1, 2, i))
                pair(At(3, 2, i), At(2, 2, i))
            p = At(NPAIR - 1)
            bias(p, 0)
            o_out(p + (-1))
            for s in range(1, 8):
                bias(p, s)
                normalize(p, s - 1)
            normalize(p, 7)
            o_out(p)

            dve.wait_ge(S("t_full"), T_LAST + 9)
            dve.wait_ge(S("lf_new_in"), 16 * NB)
            link(V.tensor_copy(lf_s[:, 0:PAST], ps[:, 6, 0:PAST]))
            link(V.tensor_tensor_scan(out=nc_s[:], data0=ones_s[:], data1=lf_s[:], initial=0.0,
                                      op0=ALU.mult, op1=ALU.subtract))
            V.tensor_tensor(cq_w[:], head_of[:],
                            nc_s[:, PAST:PAST + TQ].rearrange("p (o k) -> p o k", o=1).broadcast_to([P, NH, TQ]),
                            ALU.mult).then_inc(S("cq_w_ready"), 1)
            dve.wait_ge(S("cq_s_ready"), 1)

            def e_batch(b):
                wait(dve, S("s_full"), b + (-1))
                V.tensor_scalar(e_b[:, b.slot(2), :], head_of[:].rearrange("p h q -> p (h q)"),
                                batch_of[:, ds(b.v, 1)], None, ALU.mult).then_inc(S("e_b_ready"), 1)

            def kT_odd(b):
                for j in range(1, KD, 2):
                    wait(dve, S("kT_full"), b.times(KD, j + 1))
                    wait(dve, S("kT_used"), b.times(KD, j - 1))
                    V.tensor_copy(kT[:, 1, :], ps[:, 5, 0:PAST]).then_inc(S("kT_odd"), 1)

            def s_bias(b):
                s = b.slot(2)
                q = cq_s[:, ds(b.v, 1)]
                wait(dve, S("s_full"), b + 1)
                wait(dve, S("psT_full"), b + (-1))
                V.tensor_scalar(ss[:, s, 0:PAST], ps[:, 2 * s, 0:PAST], q, None, ALU.add)
                V.scalar_tensor_tensor(out=ss[:, s, PAST:SW], in0=ps[:, 2 * s + 1, 0:TS], scalar=q,
                                       in1=new_mask[:, ds(b.times(TS).v, TS)], op0=ALU.add, op1=ALU.add
                                       ).then_inc(S("s_biased"), 1)
                wait(dve, S("s_biased"), b + 1)
                V.tensor_reduce(out=sms[:, 0, s:s + 1], in_=ss[:, s, :], axis=AX.X, op=ALU.max, negate=True
                                ).then_inc(S("s_max"), 1)

            def s_normalize(b):
                s = b.slot(2)
                wait(dve, S("s_probs"), b + 1)
                V.reciprocal(sms[:, 2, s:s + 1], sms[:, 1, s:s + 1]).then_inc(S("s_inv"), 1)
                wait(dve, S("s_inv"), b + 1)
                V.tensor_scalar(ss[:, s, :], ss[:, s, :], sms[:, 2, s:s + 1], None, ALU.mult).then_inc(S("ps_norm"), 1)

            def s_own(b):
                wait(dve, S("pv_s_done"), b + 1)
                wait(dve, S("os_full"), b)
                own = own_head[:].rearrange("p (h o) -> p h o", o=1).broadcast_to([P, NH, HD])
                V.tensor_tensor(o_own[:].rearrange("p (h d) -> p h d", d=HD),
                                ps[:, 2 * b.slot(2):2 * b.slot(2) + 2, :].rearrange("p a (h d) -> p (a h) d", d=HD),
                                own, ALU.mult).then_inc(S("o_own_ready"), 1)

            def s_out(b):
                wait(dve, S("os_hi"), b + 1)
                o = ds(b.times(TQ, TP).v, TQ)
                V.tensor_tensor(o_lo[:, :, o], ps[:, 7, 0:KD * TQ].rearrange("p (j q) -> p j q", q=TQ),
                                o_hi[:, :, o].bitcast(f32), ALU.subtract).then_inc(S("os_lo"), 1)

            V.tensor_reduce(out=q_of[:], in_=ident[:].rearrange("p (h q) -> p q h", q=TQ), axis=AX.X, op=ALU.add)
            e_batch(At(0))
            kT_odd(At(0))
            s_bias(At(0))
            s_normalize(At(0))

            def sample(b, c, o):
                e_batch(b)
                kT_odd(b)
                if o is not None:
                    s_out(o)
                s_bias(b)
                s_normalize(b)
                s_own(c)

            sample(At(1), At(0), None)
            with dve.Fori(0, NB // 2 - 1) as i:
                sample(At(2, 2, i), At(1, 2, i), At(0, 2, i))
                sample(At(3, 2, i), At(2, 2, i), At(1, 2, i))
            s_own(At(NB - 1))
            s_out(At(NB - 2))
            s_out(At(NB - 1))

            def add_z(sem, full, src, j, z):
                wait(dve, sem, full)
                wait(dve, S("z_added"), z + (1 - KD))
                V.tensor_tensor(halves(x_f[:, j, :]), halves(x_f[:, j, :]), src, ALU.add).then_inc(S("z_added"), 1)

            dve.wait_ge(S("x_scaled"), KD)
            for j in range(KD):
                m = At(M_AO + j)
                add_z(S("acc_full"), m + 1, acc(m), j, At(Z_AO + j))
                lo_next(At(N_AO + j))

            def norm(k):
                b = LN_BANK[k]
                rs = (ln_f, ln_f, ln_r, ln_f)[k][1]
                dve.wait_ge(S("ln_mean"), k + 1)
                for j in range(KD):
                    V.tensor_tensor(halves(x_f[:, j, :]), halves(x_f[:, j, :]), bank_pair(b), ALU.subtract
                                    ).then_inc(S("ln_centred"), 1)
                dve.wait_ge(S("ln_std"), k + 1)
                V.reciprocal(rs[:, 1, :], rs[:, 0, :]).then_inc(S("ln_rstd"), 1)
                dve.wait_ge(S("ln_rstd"), k + 1)
                column = lambda c, j: prm[:, c + KD * k + j:c + KD * k + j + 1]

                def low(j):
                    dve.wait_ge(S("x_hi_ready"), KD * (k + 1) + j + 1)
                    V.scalar_tensor_tensor(out=x_lo[:, j, :], in0=x_f[:, j, :], scalar=column(C_LNB, j),
                                           in1=x_hi[:, j, :].bitcast(f32), op0=ALU.add, op1=ALU.subtract
                                           ).then_inc(S("x_lo_ready"), 1)

                for j in range(KD):
                    V.scalar_tensor_tensor(out=x_f[:, j, :], in0=x_f[:, j, :], scalar=column(C_LNG, j), in1=rs[:, 1, :],
                                           op0=ALU.mult, op1=ALU.mult).then_inc(S("ln_scaled"), 1)
                    if k < 3 and j:
                        low(j - 1)
                if k < 3:
                    low(KD - 1)

            norm(0)

            def ffn(l, n0, m0, z0):
                def tile(F, n, m, par, f):
                    Fg = F + NF * l
                    s = F.slot(2)
                    lo_next(n)
                    col = lambda c: prm[:, ds((F + c).v, 1)]
                    wait(dve, S("gh_ready"), Fg + 1)
                    wait(dve, S("gh_hist"), Fg + 1)
                    wait(dve, S("gelu_ready"), Fg)
                    V.tensor_scalar(cv[:], gh[:, s, 0:CVW], col(C_FCW[l]), col(C_FCB + NF * l), ALU.mult, ALU.add
                                    ).then_inc(S("cv_tap"), 1)
                    for t in (1, 2):
                        wait(dve, S("cv_tap"), Fg.times(3, t))
                        V.scalar_tensor_tensor(out=cv[:], in0=gh[:, s, t:t + CVW], scalar=col(C_FCW[l] + NF * t),
                                               in1=cv[:], op0=ALU.mult, op1=ALU.add).then_inc(S("cv_tap"), 1)
                    lo_next(n + 1)
                    wait(dve, S("acc_full"), m + 2)
                    wait(dve, S("gelu_ready"), Fg + 1)
                    wait(dve, S("h_hi_ready"), Fg)
                    for src, t0, t1 in prompt_parts(2 * (m + 1).slot(2)):
                        V.tensor_tensor(hf[:, t0:t1], gl[:, t0:t1], src, ALU.mult)
                    src = ps[:, 2 * (m + 1).slot(2) + 1, TP - HT:HT].rearrange("p (b q) -> p b q", q=TQ)
                    V.tensor_tensor(hf[:, TP:T].rearrange("p (b q) -> p b q", q=TQ), strided(gl, TP + 2, 2 + TQ), src,
                                    ALU.mult).then_inc(S("h_ready"), 1)
                    wait(dve, S("h_hi_ready"), Fg + 1)
                    V.tensor_tensor(h_lo[:, par, f, :], hf[:], h_hi[:, par, f, :].bitcast(f32), ALU.subtract
                                    ).then_inc(S("h_lo_ready"), 1)

                def group(g, par, more):
                    n, m = g.times(12, n0 + 2), g.times(16, m0 + 2)
                    for f in range(1, GF):
                        tile(g.times(GF, f), n + 2 * (f - 1), m + 2 * (f - 1), par, f)
                    if more:
                        tile(g.times(GF, GF), n + 6, m + 6, 1 - par, 0)
                    k = 8 if more else 6
                    for c in range(4):
                        for d in (2 * c, 2 * c + 1):
                            add_z(S("acc_full"), m + (k + d + 1), acc(m + (k + d)), d, g.times(KD, z0 + d))
                        lo_next(n + (k + c))

                dve.wait_ge(S("gh_zero"), l + 1)
                tile(At(0), At(n0), At(m0), 0, 0)
                dve.wait_ge(S("x_scaled"), KD * (2 if l == 0 else 4))
                with dve.Fori(0, NG // 2 - 1) as i:
                    group(At(0, 2, i), 0, True)
                    group(At(1, 2, i), 1, True)
                group(At(NG - 2), 0, True)
                group(At(NG - 1), 1, False)

            ffn(0, N_F0, M_F0, Z_F0)
            norm(1)

            def convolve(j):
                s, u = j.slot(3), j.slot(3)
                col = lambda c: prm[:, ds((j + c).v, 1)]
                wait(dve, S("xr_ready"), j + 1)
                wait(dve, S("xr_hist"), j + 1)
                wait(dve, S("cx_tap"), j.times(5))
                V.tensor_scalar(cx[:, 0:CXW], xr[:, s, 0:CXW], col(C_RCW), col(C_RCB), ALU.mult, ALU.add).then_inc(S("cx_tap"), 1)
                for t in (1, 2):
                    wait(dve, S("cx_tap"), j.times(5, t))
                    V.scalar_tensor_tensor(out=cx[:, 0:CXW], in0=xr[:, s, t:t + CXW], scalar=col(C_RCW + NR * t), in1=cx[:, 0:CXW],
                                           op0=ALU.mult, op1=ALU.add).then_inc(S("cx_tap"), 1)
                wait(dve, S("cx_tap"), j.times(5, 3))
                if j.turn is not None or j.first >= 2:
                    wait(dve, S("rg_full"), j + (-1))
                c3 = col(C_RCW + 3 * NR)
                V.scalar_tensor_tensor(out=xc[:, u, 0:TP], in0=xr[:, s, 3:3 + TP], scalar=c3, in1=cx[:, 0:TP],
                                       op0=ALU.mult, op1=ALU.add).then_inc(S("cx_tap"), 1)
                seq = xr[:, s, 3 + TP:XRW].rearrange("p (b c) -> p b c", c=3 + TQ)
                V.scalar_tensor_tensor(out=xc[:, u, TP:T].rearrange("p (b q) -> p b q", q=TQ), in0=seq[:, :, 3:3 + TQ],
                                       scalar=c3, in1=strided(cx, TP + 3, 3 + TQ), op0=ALU.mult, op1=ALU.add
                                       ).then_inc(S("cx_tap"), 1)

            STEPS = 9

            def recur(j, u):
                def step(k, ins):
                    ins.then_inc(S("r_step"), 1)
                    wait(dve, S("r_step"), j.times(STEPS, k))

                first = lambda x: x[:, TP:T].rearrange("p (b q) -> p b q", q=TQ)[:, :, 0]
                wait(dve, S("om_ready"), j + 1)
                step(1, V.reciprocal(om[:], om[:]))
                step(2, V.scalar_tensor_tensor(out=aa[:], in0=tr[:], scalar=1.0, in1=om[:], op0=ALU.add, op1=ALU.mult))
                wait(dve, S("r_lo_ready"), j)
                step(3, V.scalar_tensor_tensor(out=uu[:], in0=ti[:], scalar=1.0, in1=xc[:, u, :], op0=ALU.add, op1=ALU.mult))
                wait(dve, S("sq_ready"), j + 1)
                step(4, V.tensor_tensor(sq[:], sq[:], om[:], ALU.mult))
                step(5, V.tensor_tensor(uu[:], uu[:], sq[:], ALU.mult))
                h0 = hist_r[:, ds(j.v, 1), 24:32].rearrange("p o b -> p (o b)")
                step(6, V.tensor_tensor(sq[:, 0:NB], first(aa), h0, ALU.mult))
                step(7, V.tensor_tensor(first(uu), first(uu), sq[:, 0:NB], ALU.add))
                step(8, V.memset(first(aa), 0.0))
                step(9, V.tensor_tensor_scan(out=om[:], data0=aa[:], data1=uu[:], initial=0.0, op0=ALU.mult, op1=ALU.add))
                V.tensor_copy(r_st[:, ds(j.v, 1), 27:28].rearrange("p o c -> p (o c)"), om[:, TP - 1:TP])
                V.tensor_copy(r_st[:, ds(j.v, 1), 28:36].rearrange("p o c -> p (o c)"),
                              om[:, TP:T].rearrange("p (b q) -> p b q", q=TQ)[:, :, TQ - 1]).then_inc(S("h_kept"), 1)
                V.tensor_tensor(uu[:], om[:], gate[:, u, :], ALU.mult).then_inc(S("r_ready"), 1)

            def r_low(j):
                r = "p o t -> p (o t)"
                wait(dve, S("r_hi_ready"), j + 1)
                V.tensor_tensor(r_lo[:, ds(j.v, 1), :].rearrange(r), uu[:],
                                r_hi[:, ds(j.v, 1), :].rearrange(r).bitcast(f32), ALU.subtract).then_inc(S("r_lo_ready"), 1)

            dve.wait_ge(S("rows_stored"), 32)
            dve.wait_ge(S("xr_zero"), 1)
            for j in range(2):
                lo_next(At(N_RI + 2 * j))
                lo_next(At(N_RI + 2 * j + 1))
                convolve(At(j))
            with dve.Fori(0, 3) as i:
                for u in range(3):
                    j = At(2 + u, 3, i)
                    lo_next(j.times(2, N_RI))
                    lo_next(j.times(2, N_RI + 1))
                    convolve(j)
                    recur(At(u, 3, i), u)
                    r_low(At(u, 3, i))
            for c, j in enumerate((NR - 2, NR - 1)):
                recur(At(j), j % 3)
                r_low(At(j))
                lo_next(At(N_RO + c))
            dve.wait_ge(S("x_scaled"), 3 * KD)
            for q in range(4):
                for c in range(3):
                    if q or c == 2:
                        lo_next(At(N_RO + 3 * q + c))
                for d in range(2):
                    add_z(S("ro_full"), 3 * q + 3, bank_pair(4 * (q % 2) + 2 * d), 2 * q + d, At(Z_RO + 2 * q + d))
            norm(2)
            dve.wait_ge(S("rows_stored"), 16 * 6)
            ffn(1, N_F1, M_F1, Z_F1)
            norm(3)
            for t in range(NQ + 1):
                w = min(P, T - P * t)
                dve.wait_ge(S("y_full"), t + 1)
                if t == 0:
                    dve.wait_ge(S("rows_stored"), 16 * 8)
                wait(dve, S(f"y_stored{t % 2}"), 16 * (t // 2))
                V.tensor_copy(y_tok[0:w, t % 2, 512:D], ps[0:w, 2 * (t % 2) + 1, 0:512]).then_inc(S("y_right"), 1)


INPUTS = ["x_prompt", "x_sample", "cache_k", "cache_v", "cache_logf", "page_table", "state_rglru_h",
          "state_rglru_conv", "state_ffn_conv", "ln_g", "ln_b", "w_attn_in", "b_forget", "w_attn_out", "w_rnn_in",
          "rnn_conv_w", "rnn_conv_b", "w_rg_a", "b_rg_a", "w_rg_i", "b_rg_i", "rg_lambda", "w_rnn_out",
          "w_ffn_in", "ffn_conv_w", "ffn_conv_b", "w_ffn_out"]
OUTPUTS = [("y_prompt", (1, TP, D)), ("y_sample", (NB, TQ, D)), ("k_prompt", (1, TP, 1, NH, HD)),
           ("v_prompt", (1, TP, 1, NH, HD)), ("logf_prompt", (1, TP, 1, NH)), ("k_sample", (NB, TQ, 1, NH, HD)),
           ("v_sample", (NB, TQ, 1, NH, HD)), ("logf_sample", (NB, TQ, 1, NH)), ("h_prompt", (1, 1, R)),
           ("h_sample", (1, NB, R)), ("rconv_prompt", (1, 1, 3, R)), ("rconv_sample", (1, NB, 3, R)),
           ("fconv_prompt", (2, 1, 2, FF)), ("fconv_sample", (2, NB, 2, FF))]


def kernel(**inputs):
    import numpy as np
    import concourse.bacc as bacc
    from concourse.bass_utils import run_bass_kernel_spmd

    nc = bacc.Bacc("TRN2", target_bir_lowering=False, num_devices=1)
    arrays, args = {}, {}
    for name in INPUTS:
        arr = np.ascontiguousarray(inputs[name])
        arrays["in_" + name] = arr
        args[name] = nc.dram_tensor("in_" + name, arr.shape, mybir.dt.from_np(arr.dtype), kind="ExternalInput").ap()
    for name, shape in OUTPUTS:
        args[name] = nc.dram_tensor("out_" + name, shape, mybir.dt.float32, kind="ExternalOutput").ap()
    build(nc, args)
    r = run_bass_kernel_spmd(nc, [arrays], core_ids=[0])
    return tuple(r.results[0]["out_" + name] for name, _ in OUTPUTS)
```

```python
import concourse.bass as bass
from concourse import mybir
from contextlib import ExitStack

P = 128
D = 1024
KD = D // P
TP, NB, TQ = 512, 8, 8
TS = NB * TQ
T = TP + TS
HT = T // 2
NQ = TP // P
NH, HD = 16, 64
NPAIR = NH // 2
NPG = 4
PAST = NPG * P
FF = 3 * D
NF = FF // P
GF = 4
NG = NF // GF
R = 1408
NR = R // P
RB = 88
ALPHA = 4.0 ** 0.25
EPS = 1e-5
NEG = -3.0e38
SW = PAST + TS
GHW = 2 + TP + NB * (2 + TQ)
CVW = GHW - 2
XRW = 3 + TP + NB * (3 + TQ)
CXW = XRW - 3
RING = 3
SLOT = KD * P

N_QKV = 0
N_AO = N_QKV + 3 * NPAIR
N_F0 = N_AO + KD
N_RI = N_F0 + 12 * NG
N_RO = N_RI + 2 * NR
N_F1 = N_RO + 12
N_END = N_F1 + 12 * NG
M_AO = 3 * NPAIR
M_F0 = M_AO + KD
M_RI = M_F0 + 16 * NG
M_F1 = M_RI + 2 * NR
Z_AO = 0
Z_F0 = KD
Z_RO = Z_F0 + NG * KD
Z_F1 = Z_RO + KD

RO_ORDER = [(0, 0), (0, 1), (1, 0), (1, 1), (0, 2), (1, 2)] + [(q, c) for q in (2, 3) for c in range(3)]

C_LNG, C_LNB = 0, 32
C_RCB, C_RBA, C_RBI, C_LAM = 64, 75, 86, 97
C_RCW = 128
C_FCB = C_RCW + 4 * NR
C_FCW = (256, 384)


class At:

    def __init__(self, first, step=0, turn=None):
        self.first, self.step, self.turn = first, step, turn

    def __add__(self, k):
        return At(self.first + k, self.step, self.turn)

    def times(self, k, plus=0):
        return At(self.first * k + plus, self.step * k, self.turn)

    @property
    def v(self):
        return self.first if self.turn is None else self.turn * self.step + self.first

    def slot(self, r):
        assert self.turn is None or self.step % r == 0
        return self.first % r

    def round(self, r):
        return At(self.first // r, self.step // r, self.turn)


def wait(engine, sem, value):
    if isinstance(value, At):
        value = value.v
    if isinstance(value, int) and value <= 0:
        return
    engine.wait_ge(sem, value)


def build(nc, a):
    f32, f32r, i32 = mybir.dt.float32, mybir.dt.float32r, mybir.dt.int32
    ALU, ACT, AX = mybir.AluOpType, mybir.ActivationFunctionType, mybir.AxisListType
    ds = bass.ds
    ctx = ExitStack()
    with ctx:
        sems = {}

        def S(name):
            if name not in sems:
                sems[name] = ctx.enter_context(nc.semaphore(name))
            return sems[name]

        base = 16512
        top = [base]

        def sb(name, shape, dt=f32, at=None):
            size = 4
            for n in shape[1:]:
                size *= n
            size = (size + 31) // 32 * 32
            if at is None:
                off = top[0]
                top[0] += size
            else:
                off = at[0]
                at[0] += size
            assert off + size <= 229376, (name, off + size)
            return nc.alloc_sbuf_tensor_at(name, shape, dt, offset=off)

        ident = sb("ident", [P, P])
        over_d = sb("over_d", [P, P])
        prm = sb("prm", [P, 512])
        hist_f = sb("hist_f", [P, NF, 32])
        hist_r = sb("hist_r", [P, NR, 32])
        cols = sb("cols", [P, 8])
        lru_t = sb("lru_t", [P, NR])
        lru_a = sb("lru_a", [P, NR])
        lru_w = sb("lru_w", [P, 3, NR])
        x_f = sb("x_f", [P, KD, T])
        w_raw = sb("w_raw", [P, RING, SLOT])
        w_hi = sb("w_hi", [P, RING, SLOT], f32r)
        w_lo = sb("w_lo", [P, RING, SLOT], f32r)
        xhl_at = [top[0]]
        x_hi = sb("x_hi", [P, KD, T], f32r)
        x_lo = sb("x_lo", [P, KD, T], f32r)
        phase = top[0]

        at = [phase]
        o_hi = sb("o_hi", [P, KD, T], f32r, at)
        o_lo = sb("o_lo", [P, KD, T], f32r, at)
        v_new = sb("v_new", [P, D], f32, at)
        qT_s = sb("qT_s", [P, NPAIR, TS], f32, at)
        kT_s = sb("kT_s", [P, NPAIR, TS], f32, at)
        lf_pg = sb("lf_pg", [P, NPG, NB, NH], f32, at)
        lf_s = sb("lf_s", [P, PAST + TQ], f32, at)
        own_head = sb("own_head", [P, NH], f32, at)
        head_of = sb("head_of", [P, NH, TQ], f32, at)
        batch_of = sb("batch_of", [P, NB], f32, at)
        new_mask = sb("new_mask", [P, NB * 72], f32, at)
        causal_w = sb("causal_w", [P, NH, TQ], f32, at)
        ones_s = sb("ones_s", [P, PAST + TQ], f32, at)
        pages = sb("pages", [1, NB * NPG], i32, at)
        bf_col = sb("bf_col", [NH, 1], f32, at)
        pair_at = at[0]
        q_sb = sb("q_sb", [P, 2, T], f32, at)
        k_sb = sb("k_sb", [P, 2, T], f32, at)
        v_sb = sb("v_sb", [P, T], f32, at)
        v_tok = sb("v_tok", [P, 2, NQ, P], f32, at)
        k_tok = sb("k_tok", [P, NQ, P], f32, at)
        k_new = sb("k_new", [TS, P], f32, at)
        ncb = sb("ncb", [P, 2, TP], f32, at)
        ncbm = sb("ncbm", [P, 2, TP], f32, at)
        mask4 = sb("mask4", [P, NQ, P], f32, at)
        cumq = sb("cumq", [P, NQ, NH], f32, at)
        lf_tok = sb("lf_tok", [P, NQ + 1, NH], f32, at)
        sc = sb("sc", [P, 2, TP], f32, at)
        pr = sb("pr", [P, 2, TP], f32, at)
        prT = sb("prT", [P, NQ, TP], f32, at)
        sm = sb("sm", [P, 3, 2], f32, at)
        at0 = [pair_at]
        x_in = sb("x_in", [P, NQ + 1, D], f32, at0)
        assert at0[0] <= 229376
        at1 = [phase]
        prow = sb("prow", [P, 4, P], f32, at1)
        frow = sb("frow", [32, FF], f32, at1)
        rrow = sb("rrow", [32, R], f32, at1)
        wf = sb("wf", [P, KD, NH], f32, at1)
        fz = sb("fz", [NH, 3, T], f32, at1)
        ft = sb("ft", [P, 5, (NQ + 1) * NH], f32, at1)
        assert at1[0] <= phase + 2 * KD * T * 4
        k_pg = sb("k_pg", [P, 2, NPG, D], f32, xhl_at)
        at2 = [pair_at]
        v_pg = sb("v_pg", [P, 2, NPG, D], f32, at2)
        kT = sb("kT", [P, 2, PAST], f32, xhl_at)
        assert xhl_at[0] <= phase
        e_b = sb("e_b", [P, 2, P], f32, at2)
        nc_s = sb("nc_s", [P, PAST + TQ], f32, at2)
        cq_w = sb("cq_w", [P, NH, TQ], f32, at2)
        cq_s = sb("cq_s", [P, NB], f32, at2)
        ss = sb("ss", [P, 2, SW], f32, at2)
        sms = sb("sms", [P, 3, 2], f32, at2)
        o_own = sb("o_own", [P, D], f32, at2)
        q_of = sb("q_of", [P, TQ], f32, at2)
        at2 = [max(at[0], at2[0])]
        qz = sb("qz", [P, 2, KD * 144], f32, at2)
        psT = sb("psT", [P, NPG + 1, P], f32, at2)

        def norm_space(at, tag):
            return (sb("ln_sq" + tag, [P, 2, T], f32, at), sb("ln_rstd" + tag, [P, 2, T], f32, at),
                    sb("ln_sum" + tag, [P, T], f32, at))

        atf = [phase]
        gh = sb("gh", [P, 2, GHW], f32, atf)
        cv = sb("cv", [P, CVW], f32, atf)
        gl = sb("gl", [P, GHW], f32, atf)
        hf = sb("hf", [P, T], f32, atf)
        h_hi = sb("h_hi", [P, 2, GF, T], f32r, atf)
        h_lo = sb("h_lo", [P, 2, GF, T], f32r, atf)
        f_st = sb("f_st", [P, NF, 2 + 2 * NB], f32, atf)
        f_rows = sb("f_rows", [2 + 2 * NB, FF], f32, atf)
        ln_f = norm_space(atf, "f")

        atr = [phase]
        r_hi = sb("r_hi", [P, NR, T], f32r, atr)
        r_lo = sb("r_lo", [P, NR, T], f32r, atr)
        r_end = atr[0]
        gate = sb("gate", [P, 3, T], f32, atr)
        xr = sb("xr", [P, 3, XRW], f32, atr)
        cx = sb("cx", [P, XRW], f32, atr)
        xc = sb("xc", [P, 3, T], f32, atr)
        tr3 = sb("tr", [P, 3, T], f32, atr)
        ti3 = sb("ti", [P, 3, T], f32, atr)
        aa3 = sb("aa", [P, 3, T], f32, atr)
        uu = sb("uu", [P, T], f32, atr)
        rgw = sb("rgw", [P, 3, 3, 2, P], f32, atr)
        r_st = sb("r_st", [P, NR, 36], f32, atr)
        r_rows = sb("r_rows", [36, R], f32, [r_end])
        ln_r = norm_space([r_end + 8192], "r")
        y_tok = sb("y_tok", [P, NQ + 1, D], f32, [phase])

        ps = ctx.enter_context(nc.psum_tensor("ps", [P, 8, 512], f32))
        block = ctx.enter_context(nc.Block())

        def acc(m):
            b = 2 * m.slot(2)
            return ps[:, b:b + 2, 0:HT]

        def halves(x):
            return x.rearrange("p (a t) -> p a t", a=2)

        def bank_pair(b):
            return ps[:, b:b + 2, 0:HT]

        def prompt_parts(b):
            return [(ps[:, b, 0:HT], 0, HT), (ps[:, b + 1, 0:TP - HT], HT, TP)]

        def strided(x, first, step):
            return x[:, first:first + NB * step].rearrange("p (b c) -> p b c", c=step)[:, :, 0:TQ]

        xp = a["x_prompt"].rearrange("a (t p) d -> p (a t) d", p=P)
        xs = a["x_sample"].rearrange("a b d -> (a b) d")
        w_qkv = a["w_attn_in"].rearrange("a (k p) e -> p (a k) e", p=P)
        w_ao = a["w_attn_out"].rearrange("a (k p) e -> p (a k) e", p=P)
        w_ri = a["w_rnn_in"].rearrange("a (k p) e -> p (a k) e", p=P)
        w_ro = a["w_rnn_out"].rearrange("a (k p) e -> p (a k) e", p=P)
        w_fi = a["w_ffn_in"].rearrange("l (k p) e -> l p k e", p=P)
        w_fo = a["w_ffn_out"].rearrange("l (k p) e -> l p k e", p=P)
        ck = a["cache_k"].rearrange("n p a h d -> n p (a h d)")
        cvv = a["cache_v"].rearrange("n p a h d -> n p (a h d)")
        clf = a["cache_logf"].rearrange("n p a h -> n p (a h)")
        kp_o = a["k_prompt"].rearrange("a (t p) l h d -> p (a t) (l h d)", p=P)
        vp_o = a["v_prompt"].rearrange("a (t p) l h d -> p (a t) (l h d)", p=P)
        ks_o = a["k_sample"].rearrange("b q l h d -> (b q) (l h d)")
        vs_o = a["v_sample"].rearrange("b q l h d -> (b q) (l h d)")
        lp_o = a["logf_prompt"].rearrange("a (t p) l h -> p (a t) (l h)", p=P)
        ls_o = a["logf_sample"].rearrange("b q l h -> (b q) (l h)")
        yp_o = a["y_prompt"].rearrange("a (t p) d -> p (a t) d", p=P)
        ys_o = a["y_sample"].rearrange("a b d -> (a b) d")
        ncum_d = nc.dram_tensor("ncum_scratch", [NH, TP], f32, kind="Internal").ap()

        def load(sp, n, dst_cols, src):
            s = n.slot(RING)
            wait(sp, S("w_lo_ready"), n + (1 - RING))
            dst = w_raw[:, s, 0:dst_cols]
            k = src.shape[1]
            sp.dma_start(dst.rearrange("p (k e) -> p k e", k=k), src).then_inc(S(f"w_raw{s}"), 16)

        def split_hi(act, n, m_done, width=SLOT):
            s = n.slot(RING)
            wait(act, S(f"w_raw{s}"), n.round(RING).times(16, 16))
            if m_done is not None:
                wait(act, *m_done)
            nc.scalar.copy(w_hi[:, s, 0:width], w_raw[:, s, 0:width]).then_inc(S("w_hi_ready"), 1)

        def split_lo(dve, n, width=SLOT):
            s = n.slot(RING)
            wait(dve, S("w_hi_ready"), n + 1)
            nc.vector.tensor_tensor(w_lo[:, s, 0:width], w_raw[:, s, 0:width],
                                    w_hi[:, s, 0:width].bitcast(f32), ALU.subtract).then_inc(S("w_lo_ready"), 1)

        def width_of(n):
            return 3 * 2 * P if N_RO <= n.first < N_F1 and RO_ORDER[n.first - N_RO][1] == 2 else SLOT

        def products(pe, n, out, terms, half, first=True, last=True):
            s = n.slot(RING)
            for i, (t, hi, lo) in enumerate(terms):
                w_h, w_l = w_hi[:, s, t * P:(t + 1) * P], w_lo[:, s, t * P:(t + 1) * P]
                r = slice(half * HT, (half + 1) * HT)
                nc.tensor.matmul(out, w_h, hi[:, r], start=first and i == 0, stop=False)
                nc.tensor.matmul(out, w_h, lo[:, r], start=False, stop=False)
                done = nc.tensor.matmul(out, w_l, hi[:, r], start=False, stop=last and i == len(terms) - 1)
            return done

        def x_terms():
            return [(k, x_hi[:, k, :], x_lo[:, k, :]) for k in range(KD)]

        def unit_half(pe, n, m, half, terms):
            b = 2 * m.slot(2) + half
            return products(pe, n, ps[:, b, 0:HT], terms, half)

        T_ORDER = ["T0", "T1", "T2", "k0", "T3", "k1", "T4", "v0", "T5", "v1", "T6", "T7"]
        T_LAST = 4 + 12 * (NPAIR - 1)

        def t_use(what, j):
            if j is None:
                return At(T_LAST + int(what[1]))
            if j.turn is None and j.first == 0:
                return At(["k0", "k1", "v0", "v1"].index(what))
            return j.times(12, 4 - 12 + T_ORDER.index(what))

        def y_tile(engine, copy, half, t):
            w = min(P, T - P * t)
            engine.wait_ge(S("y_full"), 5 * half + t + 1)
            return copy(y_tok[0:w, t, 512 * half:512 * half + 512], ps[0:w, (t + 5 * half) % 8, :])

        @block.sync
        def _(sp):
            for half in range(2):
                e = slice(half * D // 2, (half + 1) * D // 2)
                sp.dma_start(x_in[:, 0:NQ, e], xp[:, :, e]).then_inc(S(f"x_in{half}"), 16)
                sp.dma_start(x_in[0:TS, NQ, e], xs[:, e]).then_inc(S(f"x_in{half}"), 16)
            sp.dma_start(wf[:], w_qkv[:, :, 3 * D:3 * D + NH]).then_inc(S("wf_in"), 16)
            sp.dma_start(bf_col[:], a["b_forget"].rearrange("a h -> h a")).then_inc(S("wf_in"), 16)

            def qkv(j, n):
                for c, first in enumerate((D, 2 * D, 0)):
                    load(sp, n + c, SLOT, w_qkv[:, :, ds(j.times(P, first).v, P)])

            qkv(At(0), At(N_QKV))

            def rows(blk, r0, n, src):
                sp.dma_start(prow[r0:r0 + n, blk, :], src).then_inc(S("prm_in"), 16)

            rows(0, C_LNG, 32, a["ln_g"].rearrange("l s (k p) -> (l s k) p", p=P))
            rows(0, C_LNB, 32, a["ln_b"].rearrange("l s (k p) -> (l s k) p", p=P))
            rows(0, C_RCB, NR, a["rnn_conv_b"].rearrange("l (k p) -> (l k) p", p=P))
            rows(0, C_RBA, NR, a["b_rg_a"].rearrange("l (k p) -> (l k) p", p=P))
            rows(0, C_RBI, NR, a["b_rg_i"].rearrange("l (k p) -> (l k) p", p=P))
            rows(0, C_LAM, NR, a["rg_lambda"].rearrange("l (k p) -> (l k) p", p=P))
            rows(1, 0, 4 * NR, a["rnn_conv_w"].rearrange("l w (k p) -> (l w k) p", p=P))
            rows(1, 4 * NR, 2 * NF, a["ffn_conv_b"].rearrange("l (k p) -> (l k) p", p=P))
            for l in range(2):
                rows(2 + l, 0, 3 * NF, a["ffn_conv_w"][l].rearrange("w (k p) -> (w k) p", p=P))
            sp.dma_start(frow[:], a["state_ffn_conv"].rearrange("l b w f -> (l b w) f")).then_inc(S("prm_in"), 16)
            sp.dma_start(rrow[0:24, :], a["state_rglru_conv"].rearrange("l b w f -> (l b w) f")).then_inc(S("prm_in"), 16)
            sp.dma_start(rrow[24:32, :], a["state_rglru_h"].rearrange("l b f -> (l b) f")).then_inc(S("prm_in"), 16)

            qkv(At(1), At(3))
            sp.wait_ge(S("ncum_ready"), 1)
            for b in range(NB):
                sp.dma_start(lf_s[NH * b:NH * (b + 1), PAST:PAST + TQ],
                             fz[:, 1, TP + TQ * b:TP + TQ * (b + 1)]).then_inc(S("lf_new_in"), 16)
            with sp.Fori(0, NPAIR - 2) as i:
                qkv(At(2, 1, i), At(6, 3, i))
            for j in range(RING):
                load(sp, At(N_AO + j), SLOT, w_ao[:, :, P * j:P * (j + 1)])

            sp.wait_ge(S("pages_in"), 16)

            def page_loads(b):
                k_loads(b)
                v_loads(b)

            def numbers(b):
                return [sp.value_load(pages[0:1, ds(b.times(NPG, t).v, 1)], min_val=0, max_val=39) for t in range(NPG)]

            def k_loads(b):
                s, pgs = b.slot(2), numbers(b)
                wait(sp, S("s_full"), b + (-1))
                for t, pg in enumerate(pgs):
                    sp.dma_start(k_pg[:, s, t, :], ck[ds(pg, 1)].rearrange("n p e -> (n p) e")).then_inc(S(f"k_pg{s}"), 16)

            def v_loads(b):
                s, pgs = b.slot(2), numbers(b)
                wait(sp, S("pv_s_done"), b + (-1))
                for t, pg in enumerate(pgs):
                    sp.dma_start(v_pg[:, s, t, :], cvv[ds(pg, 1)].rearrange("n p e -> (n p) e")).then_inc(S(f"v_pg{s}"), 16)

            sp.wait_ge(S("acc_full"), M_AO)
            for b in range(2):
                k_loads(At(b))
            sp.wait_ge(S("o_lo_ready"), NPAIR)
            sp.wait_ge(S("kv_stored"), 64 * NPAIR)
            sp.wait_ge(S("qk_kept"), 2 * NPAIR)
            for b in range(2):
                v_loads(At(b))
            with sp.Fori(0, NB // 2 - 1) as i:
                page_loads(At(2, 2, i))
                page_loads(At(3, 2, i))

            for j in range(RING, KD):
                load(sp, At(N_AO + j), SLOT, w_ao[:, :, P * j:P * (j + 1)])

            def ffn(l, n0):
                def pair(F, n):
                    load(sp, n, SLOT, w_fi[l, :, :, ds(F.times(P).v, P)])
                    load(sp, n + 1, SLOT, w_fi[l, :, :, ds(F.times(P, FF).v, P)])

                def group(g, more):
                    n = g.times(12, n0 + 2)
                    for f in range(1, GF):
                        pair(g.times(GF, f), n + 2 * (f - 1))
                    if more:
                        pair(g.times(GF, GF), n + 6)
                    for c in range(4):
                        load(sp, n + ((8 if more else 6) + c), SLOT,
                             w_fo[l, :, ds(g.times(GF).v, GF), 2 * P * c:2 * P * (c + 1)])

                pair(At(0), At(n0))
                with sp.Fori(0, NG - 1) as i:
                    group(At(0, 1, i), True)
                group(At(NG - 1), False)

            ffn(0, N_F0)

            def rnn_in(j, n):
                load(sp, n, SLOT, w_ri[:, :, ds(j.times(P).v, P)])
                load(sp, n + 1, SLOT, w_ri[:, :, ds(j.times(P, R).v, P)])

            rnn_in(At(0), At(N_RI))
            rnn_in(At(1), At(N_RI + 2))
            with sp.Fori(0, 3) as i:
                for u in range(3):
                    rnn_in(At(2 + u, 3, i), At(N_RI + 4 + 2 * u, 6, i))
            for i, (q, c) in enumerate(RO_ORDER):
                n = At(N_RO + i)
                load(sp, n, width_of(n), w_ro[:, 4 * c:min(4 * c + 4, NR), 2 * P * q:2 * P * (q + 1)])
            ffn(1, N_F1)

            for half in range(2):
                e = slice(half * D // 2, (half + 1) * D // 2)
                for t in range(NQ + 1):
                    if half and t % 2 == 0:
                        sp.wait_ge(S("y_dve"), t // 2 + 1)
                    else:
                        sp.wait_ge(S("y_act"), NQ + 1 + (t + 1) // 2 if half else t + 1)
                    if t < NQ:
                        sp.dma_start(yp_o[:, t, e], y_tok[:, t, e]).then_inc(S("y_stored"), 16)
                    else:
                        sp.dma_start(ys_o[:, e], y_tok[0:TS, t, e]).then_inc(S("y_stored"), 16)
            sp.wait_ge(S("y_stored"), 2 * 16 * (NQ + 1))

        Z_END = (Z_AO, Z_F0 + KD * (NG - 1), Z_RO, Z_F1 + KD * (NG - 1))

        def scale_residual(pool, k):
            for j in range(KD):
                pool.wait_ge(S("x_lo_ready"), KD * k + j + 1)
                if k == 0:
                    ins = nc.gpsimd.tensor_scalar(x_f[:, j, :], x_f[:, j, :], ALPHA, 1.0, ALU.mult, ALU.mult)
                else:
                    c = C_LNB + KD * (k - 1) + j
                    ins = nc.gpsimd.tensor_scalar(x_f[:, j, :], x_f[:, j, :], prm[:, c:c + 1], ALPHA, ALU.add, ALU.mult)
                ins.then_inc(S("x_scaled"), 1)

        def norm_sums(pool, k):
            total = (ln_f, ln_f, ln_r, ln_f)[k][2]
            for j in range(1, KD - 2):
                pool.wait_ge(S("z_added"), Z_END[k] + j + 1)
                if j > 1:
                    pool.wait_ge(S("ln_summed"), (KD - 3) * k + j - 1)
                nc.gpsimd.tensor_tensor(total[:], x_f[:, 0, :] if j == 1 else total[:], x_f[:, j, :], ALU.add
                                        ).then_inc(S("ln_summed"), 1)

        def ffn_pool(pool, l):
            nc.gpsimd.memset(gh[:, :, 0:2], 0.0).then_inc(S("gh_zero"), 1)

            def tile(F):
                Fg = F + NF * l
                s = F.slot(2)
                seq = gh[:, s, 2 + TP:GHW].rearrange("p (b c) -> p b c", c=2 + TQ)
                wait(pool, S("cv_tap"), Fg.times(3, -3))
                nc.gpsimd.tensor_copy(seq[:, :, 0:2],
                                      hist_f[:, ds(F.v, 1), 16 * l:16 * l + 16].rearrange("p o (b c) -> p (o b) c", c=2)
                                      ).then_inc(S("gh_hist"), 1)
                wait(pool, S("gh_ready"), Fg + 1)
                nc.gpsimd.tensor_copy(f_st[:, ds(F.v, 1), 0:2], gh[:, s, TP:TP + 2].rearrange("p (o c) -> p o c", o=1))
                nc.gpsimd.tensor_copy(f_st[:, ds(F.v, 1), 2:18].rearrange("p o (b c) -> p (o b) c", c=2),
                                      seq[:, :, TQ:TQ + 2]).then_inc(S("gh_kept"), 1)

            tile(At(0))
            tile(At(1))
            with pool.Fori(0, NF // 2 - 1) as i:
                tile(At(2, 2, i))
                tile(At(3, 2, i))
            norm_sums(pool, 1 + 2 * l)
            pool.wait_ge(S("rows_ready"), (6, 15)[l])
            pool.dma_start(a["fconv_prompt"][l].rearrange("b w f -> (b w) f"), f_rows[0:2, :]).then_inc(S("rows_stored"), 16)
            pool.dma_start(a["fconv_sample"][l].rearrange("b w f -> (b w) f"), f_rows[2:18, :]).then_inc(S("rows_stored"), 16)

        @block.gpsimd
        def _(pool):
            link_n = [0]

            def link(ins):
                link_n[0] += 1
                ins.then_inc(S("pool_step"), 1)
                pool.wait_ge(S("pool_step"), link_n[0])

            link(nc.gpsimd.memset(ident[:], 0.0))
            nc.gpsimd.affine_select(out=ident[:], in_=ident[:], compare_op=ALU.not_equal, fill=1.0, base=0,
                                    pattern=[[-1, P]], channel_multiplier=1).then_inc(S("ident_ready"), 1)
            pool.dma_start(pages[:], a["page_table"].rearrange("b (o t) -> o (b t)", o=1)).then_inc(S("pages_in"), 16)
            nc.gpsimd.memset(cols[:, 0:1], EPS)
            nc.gpsimd.memset(cols[:, 1:2], 2.0 ** -116)
            nc.gpsimd.memset(ones_s[:], 1.0)
            link(nc.gpsimd.memset(over_d[:], 1.0 / D))
            link(nc.gpsimd.memset(head_of[:], 0.0))
            for b in range(NB):
                link(nc.gpsimd.affine_select(out=head_of[:], in_=head_of[:], compare_op=ALU.not_equal, fill=1.0,
                                             base=-NH * b, pattern=[[-1, NH], [0, TQ]], channel_multiplier=1))
            link(nc.gpsimd.memset(batch_of[:], 1.0))
            link(nc.gpsimd.affine_select(out=batch_of[:], in_=batch_of[:], compare_op=ALU.is_ge, fill=0.0, base=0,
                                         pattern=[[-NH, NB]], channel_multiplier=1))
            link(nc.gpsimd.affine_select(out=batch_of[:], in_=batch_of[:], compare_op=ALU.is_ge, fill=0.0,
                                         base=NH - 1, pattern=[[NH, NB]], channel_multiplier=-1))
            link(nc.gpsimd.memset(causal_w[:], 0.0))
            link(nc.gpsimd.affine_select(out=causal_w[:], in_=causal_w[:], compare_op=ALU.is_ge, fill=NEG, base=0,
                                         pattern=[[-TQ, NH], [-1, TQ]], channel_multiplier=1))
            link(nc.gpsimd.affine_select(out=causal_w[:], in_=causal_w[:], compare_op=ALU.is_ge, fill=NEG,
                                         base=TQ - 1, pattern=[[TQ, NH], [0, TQ]], channel_multiplier=-1))
            link(nc.gpsimd.memset(own_head[:], 1.0))
            link(nc.gpsimd.affine_select(out=own_head[:], in_=own_head[:], compare_op=ALU.is_ge, fill=0.0, base=0,
                                         pattern=[[-TQ, NH]], channel_multiplier=1))
            link(nc.gpsimd.affine_select(out=own_head[:], in_=own_head[:], compare_op=ALU.is_ge, fill=0.0,
                                         base=TQ - 1, pattern=[[TQ, NH]], channel_multiplier=-1))
            nc.gpsimd.memset(ft[:, 0, :], 0.0)
            nc.gpsimd.memset(v_new[:], 0.0)
            nc.gpsimd.memset(new_mask[:], NEG).then_inc(S("masks_ready"), 1)
            pool.wait_ge(S("x_staged"), KD)
            link(nc.gpsimd.memset(mask4[:], 0.0))
            link(nc.gpsimd.affine_select(out=mask4[:], in_=mask4[:], compare_op=ALU.is_ge, fill=NEG, base=0,
                                         pattern=[[0, NQ], [-1, P]], channel_multiplier=1))
            pool.wait_ge(S("f_full"), 1)
            scale_residual(pool, 0)
            pool.wait_ge(S("ncum_ready"), 1)
            pool.dma_start(ncum_d, fz[:, 2, 0:TP]).then_inc(S("ncum_stored"), 16)
            pool.wait_ge(S("ncum_stored"), 16)
            pool.wait_ge(S("pages_in"), 16)

            def pair(j):
                s = j.slot(2)

                def decay_rows(hh):
                    wait(pool, S("biased"), j.times(8, 4 * hh + 4 - 8))
                    pool.dma_start(ncb[:, hh, :], ncum_d[ds(j.times(2, hh).v, 1), :].broadcast_to([P, TP])
                                   ).then_inc(S("ncb_in"), 16)
                    wait(pool, S("ncb_in"), j.times(32, 16 * hh + 16))
                    nc.gpsimd.tensor_tensor(ncbm[:, hh, :], ncb[:, hh, :],
                                            mask4[:].rearrange("p t k -> p (t k)"), ALU.add
                                            ).then_inc(S("ncb_ready"), 1)

                wait(pool, S("k_ready"), j + 1)
                nc.gpsimd.tensor_copy(kT_s[:, ds(j.v, 1), :], k_sb[:, s, TP:T]).then_inc(S("qk_kept"), 1)
                decay_rows(0)
                for t in range(NPG):
                    pg = pool.value_load(pages[0:1, ds(j.times(NPG, t).v, 1)], min_val=0, max_val=39)
                    pool.dma_start(lf_pg[:, t, ds(j.v, 1), :], clf[ds(pg, 1)].rearrange("n p h -> (n p) h")
                                   ).then_inc(S("lf_pg_in"), 16)
                wait(pool, S("t_free"), t_use("k1", j) + 1)
                pool.dma_start(kp_o[:, :, ds(j.times(P).v, P)], k_tok[:]).then_inc(S("kv_stored"), 16)
                pool.dma_start(ks_o[:, ds(j.times(P).v, P)], k_new[:]).then_inc(S("kv_stored"), 16)
                wait(pool, S("t_free"), t_use("v1", j) + 1)
                decay_rows(1)
                pool.dma_start(vp_o[:, :, ds(j.times(P).v, P)], v_tok[:, s]).then_inc(S("kv_stored"), 16)
                pool.dma_start(vs_o[:, ds(j.times(P).v, P)], v_new[0:TS, ds(j.times(P).v, P)]).then_inc(S("kv_stored"), 16)
                wait(pool, S("q_ready"), j + 1)
                nc.gpsimd.tensor_copy(qT_s[:, ds(j.v, 1), :], q_sb[:, s, TP:T]).then_inc(S("qk_kept"), 1)

            pair(At(0))
            nc.gpsimd.memset(psT[:], 0.0).then_inc(S("psT_zero"), 1)
            nc.gpsimd.memset(qz[:], 0.0).then_inc(S("qz_zero"), 1)
            pool.wait_ge(S("lf_tok_ready"), 1)
            pool.dma_start(lp_o, lf_tok[:, 0:NQ, :]).then_inc(S("lf_stored"), 16)
            pool.dma_start(ls_o, lf_tok[0:TS, NQ, :]).then_inc(S("lf_stored"), 16)
            pair(At(1))
            with pool.Fori(0, NPAIR // 2 - 1) as i:
                pair(At(2, 2, i))
                pair(At(3, 2, i))

            pool.wait_ge(S("qz_zero"), 1)
            pool.wait_ge(S("qk_kept"), 2 * NPAIR)

            def sample(b):
                s = b.slot(2)
                v = qz[:, s, :].rearrange("p (j c) -> p j c", c=144)
                wait(pool, S("s_full"), b + (-1))
                for hh in range(2):
                    nc.gpsimd.tensor_copy(v[64 * hh:64 * hh + 64, :, TQ * hh:TQ * hh + TQ],
                                          qT_s[64 * hh:64 * hh + 64, :, ds(b.times(TQ).v, TQ)]
                                          ).then_inc(S("qz_ready"), 1)

            sample(At(0))
            with pool.Fori(0, NB // 2 - 1) as i:
                sample(At(1, 2, i))
                sample(At(2, 2, i))
            sample(At(NB - 1))

            norm_sums(pool, 0)
            scale_residual(pool, 1)
            ffn_pool(pool, 0)
            scale_residual(pool, 2)

            pool.wait_ge(S("rows_stored"), 32)
            nc.gpsimd.memset(xr[:, :, 0:3], 0.0).then_inc(S("xr_zero"), 1)
            nc.gpsimd.memset(xc[:, 2, :], 0.0).then_inc(S("xc_zero"), 1)
            pieces = [0, 0, 0]

            def gate_weights(j):
                s = j % 3
                wait(pool, S("rg_full"), j - 2)
                nc.gpsimd.memset(rgw[:, s], 0.0).then_inc(S("rgw_zero"), 1)
                pool.wait_ge(S("rgw_zero"), j + 1)
                for i in range(max(j - 1, 0), min(j + 2, NR)):
                    for blk in range(NH):
                        r0, r1 = max(RB * blk, P * i), min(RB * blk + RB, P * i + P)
                        c0, c1 = max(RB * blk, P * j), min(RB * blk + RB, P * j + P)
                        if r0 >= r1 or c0 >= c1:
                            continue
                        for q, w in enumerate(("w_rg_a", "w_rg_i")):
                            pool.dma_start(rgw[r0 - P * i:r1 - P * i, s, i - j + 1, q, c0 - P * j:c1 - P * j],
                                           a[w][0, blk, r0 - RB * blk:r1 - RB * blk, c0 - RB * blk:c1 - RB * blk]
                                           ).then_inc(S(f"rgw_in{s}"), 16)
                            pieces[s] += 1

            def gate_weights_in(j):
                pool.wait_ge(S(f"rgw_in{j % 3}"), 16 * pieces[j % 3])
                nc.gpsimd.memset(cols[:, 2 + j % 3:3 + j % 3], 0.0).then_inc(S("rgw_ready"), 1)

            def conv_pool(j):
                s = j % 3
                hist = xr[:, s, 3 + TP:XRW].rearrange("p (b c) -> p b c", c=3 + TQ)
                wait(pool, S("cx_tap"), 5 * (j - 2))
                nc.gpsimd.tensor_copy(hist[:, :, 0:3], hist_r[:, j, 0:24].rearrange("p (b c) -> p b c", c=3)
                                      ).then_inc(S("xr_hist"), 1)
                pool.wait_ge(S("xr_ready"), j + 1)
                nc.gpsimd.tensor_copy(r_st[:, j, 0:3], xr[:, s, TP:TP + 3])
                nc.gpsimd.tensor_copy(r_st[:, j, 3:27].rearrange("p (b c) -> p b c", c=3),
                                      hist[:, :, TQ:TQ + 3]).then_inc(S("xr_kept"), 1)

            for j in range(NR):
                gate_weights(j)
                conv_pool(j)
                gate_weights_in(j)

            norm_sums(pool, 2)
            pool.wait_ge(S("rows_ready"), 9)
            pool.dma_start(a["rconv_prompt"].rearrange("l b w f -> (l b w) f"), r_rows[0:3, :]).then_inc(S("rows_stored"), 16)
            pool.dma_start(a["rconv_sample"].rearrange("l b w f -> (l b w) f"), r_rows[3:27, :]).then_inc(S("rows_stored"), 16)
            pool.dma_start(a["h_prompt"].rearrange("l b f -> (l b) f"), r_rows[27:28, :]).then_inc(S("rows_stored"), 16)
            pool.dma_start(a["h_sample"].rearrange("l b f -> (l b) f"), r_rows[28:36, :]).then_inc(S("rows_stored"), 16)
            scale_residual(pool, 3)
            pool.wait_ge(S("rows_stored"), 16 * 6)
            ffn_pool(pool, 1)

            for j in range(KD):
                c = C_LNB + 3 * KD + j
                pool.wait_ge(S("ln_scaled"), 3 * KD + j + 1)
                nc.gpsimd.tensor_scalar(x_f[:, j, :], x_f[:, j, :], prm[:, c:c + 1], 1.0, ALU.add, ALU.mult
                                        ).then_inc(S("x_f_ready"), 1)
            pool.wait_ge(S("rows_stored"), 16 * 8)
            pool.wait_ge(S("kv_stored"), 64 * NPAIR)
            pool.wait_ge(S("lf_stored"), 32)

        LN_BANK = (4, 4, 0, 4)
        ROW_BANKS = {1: (6, 7, 6, 7, 6, 7), 2: (4, 5, 6), 3: (6, 7, 6, 7, 6, 7)}
        ROWS_BEFORE = {1: 0, 2: 6, 3: 9}

        @block.tensor
        def _(pe):
            def transpose(out, in_):
                k = in_.shape[0]
                return nc.tensor.transpose(out, in_, ident[0:k, 0:k])

            pe.wait_ge(S("ident_ready"), 1)

            def f_logits(k):
                pe.wait_ge(S("x_f_ready"), k + 1)
                for half in range(2):
                    last = nc.tensor.matmul(ps[0:NH, 2 + half, 0:HT], wf[:, k, :], x_f[:, k, HT * half:HT * half + HT],
                                            start=k == 0, stop=k == KD - 1)
                return last

            for j in range(KD):
                if j % 4 == 0:
                    pe.wait_ge(S(f"x_in{j // 4}"), 32)
                b = 4 + 2 * (j % 2)
                wait(pe, S("x_f_ready"), j - 1)
                for t in range(NQ):
                    transpose(ps[:, b, P * t:P * t + P], x_in[:, t, P * j:P * j + P])
                transpose(ps[:, b + 1, 0:TS], x_in[0:TS, NQ, P * j:P * j + P]).then_inc(S("x_staged"), 1)
                if j == 1:
                    pe.wait_ge(S("wf_in"), 32)
                if j:
                    f_logits(j - 1)
            f_logits(KD - 1).then_inc(S("f_full"), 1)
            pe.wait_ge(S("x_lo_ready"), KD)

            def qkv(j, first, count):
                for term in range(first, first + count):
                    c, half, k = term // (2 * KD), term // KD % 2, term % KD
                    n = j.times(3, c)
                    if term % (2 * KD) == 0:
                        wait(pe, S("w_lo_ready"), n + 1)
                        wait(pe, *((S("v_ready"), j), (S("q_ready"), j), (S("k_ready"), j + 1))[c])
                    last = products(pe, n, ps[:, 2 * n.slot(2) + half, 0:HT], x_terms()[k:k + 1], half,
                                    first=k == 0, last=k == KD - 1)
                    if term % (2 * KD) == 2 * KD - 1:
                        last.then_inc(S("acc_full"), 1)

            def token_rows(j, what):
                src = (k_sb[:, j.slot(2), :] if what[0] == "k" else v_sb[:, :])
                wait(pe, S("k_ready" if what[0] == "k" else "v_ready"), j + 1)
                wait(pe, S("t_free"), t_use(what, j))
                if what[1] == "0":
                    for t in range(NQ):
                        last = transpose(ps[:, 6, P * t:P * t + P], src[:, P * t:P * t + P])
                else:
                    last = transpose(ps[:, 6, 0:P], src[:, T - P:T])
                last.then_inc(S("t_full"), 1)

            def scores(p, s):
                g, hh, qt = p.times(8, s), s // 4, s % 4
                if s == 0:
                    wait(pe, S("q_ready"), p + 1)
                wait(pe, S("biased"), g + (-1 if s else 0))
                r = slice(64 * hh, 64 * hh + 64)
                nc.tensor.matmul(ps[:, 4 + s % 2, 0:P * (qt + 1)], q_sb[r, p.slot(2), P * qt:P * qt + P],
                                 k_sb[r, p.slot(2), 0:P * (qt + 1)], start=True, stop=True
                                 ).then_inc(S("sc_full"), 1)

            def prob_rows(p, s, j):
                g, qt = p.times(8, s), s % 4
                wait(pe, S("pr_norm"), g + 1)
                wait(pe, S("t_free"), t_use(f"T{s}", j))
                for kt in range(qt + 1):
                    last = transpose(ps[:, 6, P * kt:P * kt + P], pr[:, s % 2, P * kt:P * kt + P])
                last.then_inc(S("t_full"), 1)

            def values(p, hh, j):
                wait(pe, S("t_free"), t_use(f"T{4 * hh + 3}", j) + 1)
                if hh == 0:
                    wait(pe, S("o_lo_ready"), p)
                r = slice(64 * hh, 64 * hh + 64)
                for kt in range(NQ):
                    last = nc.tensor.matmul(ps[r, 7, P * kt:TP], v_tok[:, p.slot(2), kt, r], prT[:, kt, P * kt:TP],
                                            start=kt == 0, stop=kt == NQ - 1)
                last.then_inc(S("pv_done"), 1)

            qkv(At(0), 0, KD)
            pe.wait_ge(S("f_logits"), 1)
            for t in range(NQ + 1):
                w = min(P, T - P * t)
                last = transpose(ps[0:w, 6, NH * t:NH * t + NH], fz[:, 0, P * t:P * t + w])
            last.then_inc(S("ft_full"), 1)
            qkv(At(0), KD, 2 * KD)
            pe.wait_ge(S("lf_tok_ready"), 1)
            for t in range(NQ + 1):
                w = min(P, T - P * t)
                out = ps[0:NH, 6, P * t:P * t + P] if t < NQ else ps[0:NH, 7, 0:w]
                last = transpose(out, lf_tok[0:w, t, :])
            last.then_inc(S("lf_full"), 1)
            qkv(At(0), 3 * KD, KD)
            pe.wait_ge(S("lf_ready"), 1)
            for i, what in enumerate(("k0", "k1", "v0", "v1")):
                token_rows(At(0), what)
                qkv(At(0), 4 * KD + i * KD // 2, KD // 2)
            pe.wait_ge(S("t_free"), 4)
            pe.wait_ge(S("prm_in"), 16 * 13)
            for blk, n in enumerate((C_LAM + NR, 4 * NR + 2 * NF, 3 * NF, 3 * NF)):
                last = transpose(ps[:, 6, P * blk:P * blk + n], prow[0:n, blk, :])
            last.then_inc(S("prm_full"), 1)
            for F in range(16):
                last = transpose(ps[:, 7, 32 * F:32 * F + 32], frow[:, P * F:P * F + P])
            last.then_inc(S("prm_full"), 1)
            pe.wait_ge(S("prm_ready"), 1)
            for F in range(16, NF):
                last = transpose(ps[:, 6, 32 * F - 512:32 * F - 480], frow[:, P * F:P * F + P])
            last.then_inc(S("prm_full"), 1)
            pe.wait_ge(S("prm_ready"), 2)
            for j in range(NR):
                last = transpose(ps[:, 7, 32 * j:32 * j + 32], rrow[:, P * j:P * j + P])
            last.then_inc(S("prm_full"), 1)
            pe.wait_ge(S("prm_ready"), 4)
            pe.wait_ge(S("ncum_ready"), 1)
            for t in range(NQ):
                last = transpose(ps[:, 6, NH * t:NH * t + NH], fz[:, 2, P * t:P * t + P])
            last.then_inc(S("cumq_full"), 1)
            pe.wait_ge(S("cumq_ready"), 1)

            def pair(j, p):
                scores(p, 0)
                qkv(j, 0, 3)
                scores(p, 1)
                if p.turn is not None or p.first:
                    values(p + (-1), 1, j + (-1))
                qkv(j, 3, 4)
                prob_rows(p, 0, j)
                scores(p, 2)
                qkv(j, 7, 5)
                prob_rows(p, 1, j)
                scores(p, 3)
                qkv(j, 12, 5)
                prob_rows(p, 2, j)
                scores(p, 4)
                qkv(j, 17, 4)
                token_rows(j, "k0")
                qkv(j, 21, 3)
                prob_rows(p, 3, j)
                scores(p, 5)
                qkv(j, 24, 4)
                token_rows(j, "k1")
                qkv(j, 28, 3)
                values(p, 0, j)
                prob_rows(p, 4, j)
                scores(p, 6)
                qkv(j, 31, 4)
                token_rows(j, "v0")
                qkv(j, 35, 3)
                prob_rows(p, 5, j)
                scores(p, 7)
                qkv(j, 38, 4)
                token_rows(j, "v1")
                qkv(j, 42, 3)
                prob_rows(p, 6, j)
                qkv(j, 45, 3)
                prob_rows(p, 7, j)

            pair(At(1), At(0))
            with pe.Fori(0, NPAIR // 2 - 1) as i:
                pair(At(2, 2, i), At(1, 2, i))
                pair(At(3, 2, i), At(2, 2, i))
            last_pair = At(NPAIR - 1)
            scores(last_pair, 0)
            scores(last_pair, 1)
            values(last_pair + (-1), 1, last_pair)
            for s in range(8):
                if s + 2 < 8:
                    scores(last_pair, s + 2)
                if s == 4:
                    values(last_pair, 0, None)
                prob_rows(last_pair, s, None)
            values(last_pair, 1, None)

            pe.wait_ge(S("lf_pg_in"), 16 * NB * NPG)
            pe.wait_ge(S("t_free"), T_LAST + 8)
            for t in range(NPG):
                last = transpose(ps[:, 6, P * t:P * t + P], lf_pg[:, t, :, :].rearrange("p b h -> p (b h)"))
            last.then_inc(S("t_full"), 1)

            def query_decay():
                pe.wait_ge(S("cq_w_ready"), 1)
                pe.wait_ge(S("o_lo_ready"), NPAIR)
                nc.tensor.matmul(ps[:, 7, 0:NB], cq_w[:].rearrange("p h q -> p (h q)"), batch_of[:], start=True,
                                 stop=True).then_inc(S("cq_full"), 1)

            def s_scores(b, c=None, o=None):
                s = b.slot(2)
                bk = 2 * s
                wait(pe, S(f"k_pg{s}"), b.round(2).times(64, 64))
                wait(pe, S("qz_ready"), b.times(2, 2))

                def k_columns(j):
                    ready = S("kT_even" if j % 2 == 0 else "kT_odd")
                    wait(pe, ready, b.times(4, j // 2))
                    for t in range(NPG):
                        last = transpose(ps[:, 4 + j % 2, P * t:P * t + P], k_pg[:, s, t, P * j:P * j + P])
                    last.then_inc(S("kT_full"), 1)

                def add(j):
                    wait(pe, S("kT_even" if j % 2 == 0 else "kT_odd"), b.times(4, j // 2 + 1))
                    if j == 0:
                        wait(pe, S("o_own_ready"), b + (-1))
                    q = qz[:, s, P * j:P * j + P]
                    nc.tensor.matmul(ps[:, bk, 0:PAST], q, kT[:, j % 2, :], start=j == 0, stop=False)
                    nc.tensor.matmul(ps[:, bk + 1, 0:TS], q, kT_s[:, j, :], start=j == 0, stop=False
                                     ).then_inc(S("kT_used"), 1)

                k_columns(0)
                for j in range(1, KD):
                    k_columns(j)
                    add(j - 1)
                    if j == 2 and o is not None:
                        s_outputs(o)
                if c is not None:
                    s_prob_rows(c)
                add(KD - 1)
                if c is None:
                    query_decay()
                wait(pe, S("e_b_ready"), b + 1)
                nc.tensor.matmul(ps[:, bk, 0:PAST], e_b[:, s, :], nc_s[:, 0:PAST], start=False, stop=True)
                new = nc_s[:, PAST:PAST + TQ].rearrange("p (o k) -> p o k", o=1).broadcast_to([P, NB, TQ])
                nc.tensor.matmul(ps[:, bk + 1, 0:TS].rearrange("p (b k) -> p b k", b=NB), e_b[:, s, :], new,
                                 start=False, stop=True).then_inc(S("s_full"), 1)

            def s_prob_rows(b):
                s = b.slot(2)
                wait(pe, S("ps_norm"), b + 1)
                wait(pe, S("psT_ready"), b)
                wait(pe, S("os_lo"), NB - 2 if b.turn is None and b.first == NB - 1 else b)
                for t in range(NPG):
                    transpose(ps[:, 6, P * t:P * t + P], ss[:, s, P * t:P * t + P])
                transpose(ps[0:TS, 7, P:2 * P], ss[:, s, PAST:SW]).then_inc(S("psT_full"), 1)

            def s_values(b):
                s = b.slot(2)
                wait(pe, S("psT_ready"), b + 1)
                wait(pe, S(f"v_pg{s}"), b.round(2).times(64, 64))
                for half in range(2):
                    r = slice(512 * half, 512 * half + 512)
                    for t in range(NPG + 1):
                        v = v_pg[:, s, t, r] if t < NPG else v_new[:, r]
                        last = nc.tensor.matmul(ps[:, 2 * s + half, :], psT[:, t, :], v, start=t == 0, stop=t == NPG)
                last.then_inc(S("pv_s_done"), 1)

            def s_outputs(b):
                wait(pe, S("o_own_ready"), b + 1)
                wait(pe, S("os_lo"), b)
                for j in range(KD):
                    last = nc.tensor.matmul(ps[:, 7, TQ * j:TQ * j + TQ], o_own[:, P * j:P * j + P], q_of[:],
                                            start=True, stop=True)
                last.then_inc(S("os_full"), 1)

            pe.wait_ge(S("q_ready"), NPAIR)
            pe.wait_ge(S("k_ready"), NPAIR)
            pe.wait_ge(S("v_ready"), NPAIR)
            pe.wait_ge(S("qk_kept"), 2 * NPAIR)
            s_scores(At(0))
            pe.wait_ge(S("cq_s_ready"), 1)
            pe.wait_ge(S("psT_zero"), 1)
            s_scores(At(1), At(0))
            s_values(At(0))
            with pe.Fori(0, NB // 2 - 1) as i:
                s_scores(At(2, 2, i), At(1, 2, i), At(0, 2, i))
                s_values(At(1, 2, i))
                s_scores(At(3, 2, i), At(2, 2, i), At(1, 2, i))
                s_values(At(2, 2, i))
            s_prob_rows(At(NB - 1))
            s_values(At(NB - 1))
            s_outputs(At(NB - 2))
            s_outputs(At(NB - 1))

            pe.wait_ge(S("os_lo"), NB)
            pe.wait_ge(S("s_biased"), NB)
            for j in range(KD):
                n = At(N_AO + j)
                wait(pe, S("w_lo_ready"), n + 1)
                wait(pe, S("z_added"), Z_AO + j - 1)
                for half in range(2):
                    last = unit_half(pe, n, At(M_AO + j), half, [(k, o_hi[:, k, :], o_lo[:, k, :]) for k in range(KD)])
                last.then_inc(S("acc_full"), 1)

            def norm(k):
                b = LN_BANK[k]
                if k == 2:
                    pe.wait_ge(S("z_added"), Z_RO + 6)
                for i in range(3):
                    if i == 0:
                        pe.wait_ge(S("ln_summed"), (KD - 3) * (k + 1))
                        src = (ln_f, ln_f, ln_r, ln_f)[k][2]
                    else:
                        pe.wait_ge(S("z_added"), Z_END[k] + KD - 2 + i)
                        src = x_f[:, KD - 3 + i, :]
                    for half in range(2):
                        last = nc.tensor.matmul(ps[:, b + half, 0:HT], over_d[:], src[:, HT * half:HT * half + HT],
                                                start=i == 0, stop=i == 2)
                last.then_inc(S("ln_mean"), 1)
                sq_t = (ln_f, ln_f, ln_r, ln_f)[k][0]
                if k % 2:
                    pe.wait_ge(S("rows_ready"), ROWS_BEFORE[k] + 6)
                for j in range(KD):
                    pe.wait_ge(S("ln_sq_ready"), KD * k + j + 1)
                    for half in range(2):
                        last = nc.tensor.matmul(ps[:, b + 2 + half, 0:HT], over_d[:],
                                                sq_t[:, j % 2, HT * half:HT * half + HT],
                                                start=j == 0, stop=j == KD - 1)
                    last.then_inc(S("ln_sq_used"), 1)
                if k == 2:
                    pe.wait_ge(S("z_added"), Z_RO + KD)
                    pe.wait_ge(S("xr_kept"), NR)
                    pe.wait_ge(S("h_kept"), NR)
                    for i in range(3):
                        rows(k, i)

            def rows(k, i):
                src, n, w = (r_st, NR, 36) if k == 2 else (f_st, NF, 18)
                wait(pe, S("rows_ready"), ROWS_BEFORE[k] + (max(i - 1, 0) if k % 2 else 0))
                for c in range(4 * i, min(4 * i + 4, n)):
                    last = transpose(ps[0:w, ROW_BANKS[k][i], P * (c % 4):P * (c % 4) + P], src[:, c, :])
                last.then_inc(S("rows_full"), 1)

            def opening(n, m, before):
                wait(pe, S("w_lo_ready"), n + 2)
                for k in range(KD):
                    wait(pe, S("x_lo_ready"), before + k + 1)
                    for c in range(2):
                        for half in range(2):
                            last = products(pe, n + c, ps[:, 2 * (m + c).slot(2) + half, 0:HT], x_terms()[k:k + 1], half,
                                            first=k == 0, last=k == KD - 1)
                        if k == KD - 1:
                            last.then_inc(S("acc_full"), 1)

            norm(0)

            def ffn(l, n0, m0, z0):
                def inner(F, n, m, added=None):
                    Fg = F + NF * l
                    for c in range(2):
                        wait(pe, S("w_lo_ready"), n + c + 1)
                        wait(pe, S("gh_ready" if c == 0 else "h_ready"), Fg)
                        if added is not None:
                            wait(pe, S("z_added"), added + (c - 1))
                        for half in range(2):
                            last = unit_half(pe, n + c, m + c, half, x_terms())
                        last.then_inc(S("acc_full"), 1)

                def outer(g, par, n, m):
                    more = not (g.turn is None and g.first == NG - 1)
                    for c in range(4):
                        wait(pe, S("w_lo_ready"), n + c + 1)
                        for d in (2 * c, 2 * c + 1):
                            if d < 2:
                                nxt = g.times(GF, NF * l + GF)
                                wait(pe, S("gh_ready" if d == 0 else "h_ready"), nxt + (1 if more else 0))
                            else:
                                wait(pe, S("z_added"), g.times(KD, z0 + d - 1))
                            terms = [(2 * f + d % 2, h_hi[:, par, f, :], h_lo[:, par, f, :]) for f in range(GF)]
                            early = 0
                            if d == 0 and not more:
                                early = GF - 1
                                wait(pe, S("h_lo_ready"), g.times(GF, NF * l + early))
                                for half in range(2):
                                    products(pe, n, ps[:, 2 * m.slot(2) + half, 0:HT], terms[:early], half, last=False)
                            if d == 0:
                                wait(pe, S("h_lo_ready"), g.times(GF, NF * l + GF))
                            for half in range(2):
                                last = products(pe, n + c, ps[:, 2 * (m + d).slot(2) + half, 0:HT], terms[early:], half,
                                                first=not early)
                            last.then_inc(S("acc_full"), 1)
                            if not more and d < 6:
                                if d == 0:
                                    pe.wait_ge(S("gh_kept"), NF * (l + 1))
                                rows(2 * l + 1, d)

                def group(g, par, more):
                    n, m = g.times(12, n0 + 2), g.times(16, m0 + 2)
                    for f in range(1, GF):
                        inner(g.times(GF, f), n + 2 * (f - 1), m + 2 * (f - 1), g.times(KD, z0) if f == 1 else None)
                    if more:
                        inner(g.times(GF, GF), n + 6, m + 6)
                    k = 8 if more else 6
                    outer(g, par, n + k, m + k)

                opening(At(n0), At(m0), KD * (1 if l == 0 else 3))
                with pe.Fori(0, NG // 2 - 1) as i:
                    group(At(0, 2, i), 0, True)
                    group(At(1, 2, i), 1, True)
                group(At(NG - 2), 0, True)
                group(At(NG - 1), 1, False)

            ffn(0, N_F0, M_F0, Z_F0)
            norm(1)

            def in_proj(j, c):
                n, m = j.times(2, N_RI + c), j.times(2, M_RI + c)
                wait(pe, S("w_lo_ready"), n + 1)
                wait(pe, S("gate_ready" if c == 0 else "xr_ready"), j)
                for half in range(2):
                    last = unit_half(pe, n, m, half, x_terms())
                last.then_inc(S("acc_full"), 1)

            def gates(j, sources, u):
                wait(pe, S("rgw_ready"), j + 1)
                wait(pe, S("cx_tap"), min(5 * (j.first + 2), 5 * NR) if j.turn is None else j.times(5, 10))
                wait(pe, S("rg_read"), j)
                for q in range(2):
                    for half in range(2):
                        for i in sources:
                            last = nc.tensor.matmul(ps[:, 4 + 2 * q + half, 0:HT], rgw[:, u, i + 1, q, :],
                                                    xc[:, (u + i) % 3, HT * half:HT * half + HT],
                                                    start=i == sources[0], stop=i == sources[-1])
                last.then_inc(S("rg_full"), 1)

            opening(At(N_RI), At(M_RI), 2 * KD)
            in_proj(At(1), 0)
            in_proj(At(1), 1)
            pe.wait_ge(S("xc_zero"), 1)
            with pe.Fori(0, 3) as i:
                for u in range(3):
                    j = At(2 + u, 3, i)
                    in_proj(j, 0)
                    in_proj(j, 1)
                    gates(At(u, 3, i), (-1, 0, 1), u)

            def out_proj(i):
                n, (q, c) = At(N_RO + i), RO_ORDER[i]
                tiles = range(4 * c, min(4 * c + 4, NR))
                wait(pe, S("w_lo_ready"), n + 1)
                wait(pe, S("r_lo_ready"), tiles[-1] + 1)
                for d in range(2):
                    for half in range(2):
                        terms = [(2 * (k - 4 * c) + d, r_hi[:, k, :], r_lo[:, k, :]) for k in tiles]
                        last = products(pe, n, ps[:, 4 * (q % 2) + 2 * d + half, 0:HT], terms, half,
                                        first=c == 0, last=c == 2)
                last.then_inc(S("ro_full"), 1)

            pe.wait_ge(S("gate_ready"), NR)
            pe.wait_ge(S("xr_ready"), NR)
            out_proj(0)
            gates(At(NR - 2), (-1, 0, 1), (NR - 2) % 3)
            out_proj(1)
            gates(At(NR - 1), (-1, 0), (NR - 1) % 3)
            pe.wait_ge(S("rg_read"), NR)
            for i in range(2, 12):
                if i in (6, 9):
                    pe.wait_ge(S("z_added"), Z_RO + (2 if i == 6 else 4))
                out_proj(i)
            norm(2)
            ffn(1, N_F1, M_F1, Z_F1)
            norm(3)

            for half in range(2):
                for j in range(4 * half, 4 * half + 4):
                    pe.wait_ge(S("x_f_ready"), KD + j + 1)
                    for t in range(NQ + 1):
                        w = min(P, T - P * t)
                        bank = (t + 5 * half) % 8
                        if half and bank < 2 and j == 4:
                            pe.wait_ge(S("y_act"), bank + 1)
                        last = transpose(ps[0:w, bank, P * (j % 4):P * (j % 4) + P], x_f[:, j, P * t:P * t + w])
                        if j % 4 == 3:
                            last.then_inc(S("y_full"), 1)

        @block.scalar
        def _(act):
            def hi_next(n, done):
                if n.turn is not None or n.first + RING < N_END:
                    split_hi(act, n + RING, done, width_of(n + RING))

            for j in range(KD):
                act.wait_ge(S("x_f_ready"), j + 1)
                nc.scalar.copy(x_hi[:, j, :], x_f[:, j, :]).then_inc(S("x_hi_ready"), 1)
            for n in range(RING):
                split_hi(act, At(n), None)
            act.wait_ge(S("ft_ready"), 1)
            nc.scalar.activation(ft[:, 1, :], ft[:, 0, :], ACT.Abs).then_inc(S("f_abs"), 1)
            act.wait_ge(S("f_abs"), 1)
            nc.scalar.activation(ft[:, 1, :], ft[:, 1, :], ACT.Exp, scale=-1.0).then_inc(S("f_exp"), 1)

            def q_out(j):
                wait(act, S("acc_full"), j.times(3, 3))
                wait(act, S("qk_kept"), j.times(2, -2))
                nc.scalar.mul(halves(q_sb[:, j.slot(2), :]), acc(j.times(3, 2)), HD ** -0.5).then_inc(S("q_ready"), 1)

            def v_out(j):
                wait(act, S("acc_full"), j.times(3, 2))
                nc.scalar.copy(halves(v_sb[:]), acc(j.times(3, 1))).then_inc(S("v_ready"), 1)

            def v_rows(j, part):
                wait(act, S("t_full"), t_use(f"v{part}", j) + 1)
                if part == 0:
                    wait(act, S("kv_stored"), j.times(64))
                    nc.scalar.copy(v_tok[:, j.slot(2)].rearrange("p t e -> p (t e)"), ps[:, 6, 0:TP]).then_inc(S("t_free"), 1)
                else:
                    nc.scalar.copy(v_new[0:TS, ds(j.times(P).v, P)], ps[P - TS:P, 6, 0:P]).then_inc(S("t_free"), 1)

            def exps(p, s):
                g, w = p.times(8, s), P * (s % 4 + 1)
                wait(act, S("row_max"), g + 1)
                nc.scalar.activation(pr[:, s % 2, 0:w], sc[:, s % 2, 0:w], ACT.Exp, bias=sm[:, 0, s % 2:s % 2 + 1],
                                     accum_out=sm[:, 1, s % 2:s % 2 + 1]).then_inc(S("probs"), 1)

            def prob_columns(p, s, j):
                qt = s % 4
                wait(act, S("t_full"), t_use(f"T{s}", j) + 1)
                wait(act, S("pv_done"), p.times(2, s // 4))
                nc.scalar.copy(prT[:, 0:qt + 1, P * qt:P * qt + P],
                               ps[:, 6, 0:P * (qt + 1)].rearrange("p (t k) -> p t k", k=P)).then_inc(S("t_free"), 1)

            def o_out(p):
                wait(act, S("pv_done"), p.times(2, 2))
                nc.scalar.copy(o_hi[:, ds(p.v, 1), 0:TP].rearrange("p o t -> p (o t)"), ps[:, 7, 0:TP]).then_inc(S("o_hi_ready"), 1)

            act.wait_ge(S("masks_ready"), 1)
            hi_next(At(0), (S("acc_full"), 1))
            v_out(At(0))
            hi_next(At(1), (S("acc_full"), 2))
            v_rows(At(0), 0)
            v_rows(At(0), 1)
            q_out(At(0))
            for i, (dst, bank, w) in enumerate(((prm[:], 6, 512), (hist_f[:, 0:16, :], 7, 512),
                                                (hist_f[:, 16:NF, :], 6, 256), (hist_r[:], 7, 32 * NR))):
                act.wait_ge(S("prm_full"), i + 1)
                src = ps[:, bank, 0:w]
                if i == 0:
                    for blk, n in enumerate((C_LAM + NR, 4 * NR + 2 * NF, 3 * NF, 3 * NF)):
                        last = nc.scalar.copy(prm[:, P * blk:P * blk + n], ps[:, 6, P * blk:P * blk + n])
                    last.then_inc(S("prm_ready"), 1)
                else:
                    nc.scalar.copy(dst, src.rearrange("p (c w) -> p c w", w=32)).then_inc(S("prm_ready"), 1)
            lam = prm[:, C_LAM:C_LAM + NR]
            act.wait_ge(S("prm_ready"), 4)
            nc.scalar.activation(lru_t[:], lam, ACT.Abs).then_inc(S("lam_abs"), 1)
            act.wait_ge(S("lam_abs"), 1)
            nc.scalar.activation(lru_t[:], lru_t[:], ACT.Exp, scale=-1.0).then_inc(S("lam_exp"), 1)
            act.wait_ge(S("cumq_full"), 1)
            nc.scalar.mul(cumq[:], ps[:, 6, 0:64].rearrange("p (t h) -> p t h", h=NH), -1.0).then_inc(S("cumq_ready"), 1)
            act.wait_ge(S("ncum_stored"), 16)
            act.wait_ge(S("lf_new_in"), 16 * NB)

            def pair(j, p):
                exps(p, 0)
                exps(p, 1)
                if p.turn is not None or p.first:
                    o_out(p + (-1))
                hi_next((j + (-1)).times(3, 2), (S("acc_full"), j.times(3)))
                prob_columns(p, 0, j)
                exps(p, 2)
                prob_columns(p, 1, j)
                exps(p, 3)
                prob_columns(p, 2, j)
                exps(p, 4)
                hi_next(j.times(3), (S("acc_full"), j.times(3, 1)))
                prob_columns(p, 3, j)
                exps(p, 5)
                v_out(j)
                prob_columns(p, 4, j)
                exps(p, 6)
                v_rows(j, 0)
                hi_next(j.times(3, 1), (S("acc_full"), j.times(3, 2)))
                prob_columns(p, 5, j)
                exps(p, 7)
                v_rows(j, 1)
                prob_columns(p, 6, j)
                q_out(j)
                prob_columns(p, 7, j)

            pair(At(1), At(0))
            with act.Fori(0, NPAIR // 2 - 1) as i:
                pair(At(2, 2, i), At(1, 2, i))
                pair(At(3, 2, i), At(2, 2, i))
            p = At(NPAIR - 1)
            exps(p, 0)
            exps(p, 1)
            o_out(p + (-1))
            for s in range(8):
                prob_columns(p, s, None)
                if s + 2 < 8:
                    exps(p, s + 2)
                if s == 0:
                    hi_next(At(3 * NPAIR - 1), (S("acc_full"), 3 * NPAIR))
            o_out(p)

            def kT_even(b, beside=None):
                for j in range(0, KD, 2):
                    if j == 2 and beside:
                        beside()
                    wait(act, S("kT_full"), b.times(KD, j + 1))
                    wait(act, S("kT_used"), b.times(KD, j - 1))
                    nc.scalar.copy(kT[:, 0, :], ps[:, 4, 0:PAST]).then_inc(S("kT_even"), 1)

            def s_exp(b):
                s = b.slot(2)
                wait(act, S("s_max"), b + 1)
                nc.scalar.activation(ss[:, s, :], ss[:, s, :], ACT.Exp, bias=sms[:, 0, s:s + 1],
                                     accum_out=sms[:, 1, s:s + 1]).then_inc(S("s_probs"), 1)

            def s_columns(b):
                wait(act, S("psT_full"), b + 1)
                nc.scalar.copy(psT[:, 0:NPG, :].rearrange("p t c -> p (t c)"), ps[:, 6, 0:PAST])
                nc.scalar.copy(psT[0:TS, NPG, :], ps[0:TS, 7, P:2 * P]).then_inc(S("psT_ready"), 1)

            def s_out(b):
                wait(act, S("os_full"), b + 1)
                nc.scalar.copy(o_hi[:, :, ds(b.times(TQ, TP).v, TQ)],
                               ps[:, 7, 0:KD * TQ].rearrange("p (j q) -> p j q", q=TQ)).then_inc(S("os_hi"), 1)

            kT_even(At(0))
            act.wait_ge(S("cq_full"), 1)
            nc.scalar.mul(cq_s[:], ps[:, 7, 0:NB], -1.0).then_inc(S("cq_s_ready"), 1)
            act.wait_ge(S("psT_zero"), 1)

            def sample(b, c, o, beside=None):
                kT_even(b, beside)
                if o is not None:
                    s_out(o)
                s_columns(c)
                s_exp(b)

            sample(At(1), At(0), None, lambda: s_exp(At(0)))
            with act.Fori(0, NB // 2 - 1) as i:
                sample(At(2, 2, i), At(1, 2, i), At(0, 2, i))
                sample(At(3, 2, i), At(2, 2, i), At(1, 2, i))
            s_columns(At(NB - 1))
            s_out(At(NB - 2))
            s_out(At(NB - 1))
            for j in range(KD):
                hi_next(At(N_AO + j), (S("acc_full"), M_AO + j + 1))

            def norm(k):
                b = LN_BANK[k]
                sq_t, rs, _ = (ln_f, ln_f, ln_r, ln_f)[k]
                for j in range(KD):
                    act.wait_ge(S("ln_centred"), KD * k + j + 1)
                    wait(act, S("ln_sq_used"), KD * k + j - 1)
                    nc.scalar.activation(sq_t[:, j % 2, :], x_f[:, j, :], ACT.Square).then_inc(S("ln_sq_ready"), 1)
                act.wait_ge(S("ln_sq_used"), KD * (k + 1))
                nc.scalar.activation(halves(rs[:, 0, :]), bank_pair(b + 2), ACT.Sqrt, bias=cols[:, 0:1]
                                     ).then_inc(S("ln_std"), 1)
                if k == 2:
                    for i in range(3):
                        rows(k, i)
                for j in range(KD if k < 3 else 0):
                    h = prm[:, C_LNB + KD * k + j:C_LNB + KD * k + j + 1]
                    act.wait_ge(S("ln_scaled"), KD * k + j + 1)
                    nc.scalar.activation(x_hi[:, j, :], x_f[:, j, :], ACT.Identity, bias=h).then_inc(S("x_hi_ready"), 1)

            def rows(k, i):
                dst, w, n = (r_rows, 36, R) if k == 2 else (f_rows, 18, FF)
                act.wait_ge(S("rows_full"), ROWS_BEFORE[k] + i + 1)
                c0, c1 = 512 * i, min(512 * i + 512, n)
                nc.scalar.copy(dst[:, c0:c1], ps[0:w, ROW_BANKS[k][i], 0:c1 - c0]).then_inc(S("rows_ready"), 1)

            norm(0)

            def ffn(l, n0, m0):
                def tile(F, n, m, par, f):
                    Fg = F + NF * l
                    s = F.slot(2)
                    wait(act, S("acc_full"), m + 1)
                    wait(act, S("cv_tap"), Fg.times(3, -3))
                    wait(act, S("gh_kept"), Fg + (-1))
                    for src, t0, t1 in prompt_parts(2 * m.slot(2)):
                        nc.scalar.copy(gh[:, s, 2 + t0:2 + t1], src)
                    seq = gh[:, s, 2 + TP:GHW].rearrange("p (b c) -> p b c", c=2 + TQ)
                    src = ps[:, 2 * m.slot(2) + 1, TP - HT:HT].rearrange("p (b q) -> p b q", q=TQ)
                    nc.scalar.copy(seq[:, :, 2:2 + TQ], src).then_inc(S("gh_ready"), 1)
                    hi_next(n, (S("acc_full"), m + 1))
                    wait(act, S("cv_tap"), Fg.times(3, 3))
                    wait(act, S("h_ready"), Fg)
                    nc.scalar.activation(gl[:, 0:CVW], cv[:], ACT.Gelu_apprx_tanh).then_inc(S("gelu_ready"), 1)
                    wait(act, S("acc_full"), m + 2)
                    hi_next(n + 1, (S("acc_full"), m + 2))
                    wait(act, S("h_ready"), Fg + 1)
                    nc.scalar.copy(h_hi[:, par, f, :], hf[:]).then_inc(S("h_hi_ready"), 1)

                def group(g, par, more):
                    n, m = g.times(12, n0 + 2), g.times(16, m0 + 2)
                    for f in range(1, GF):
                        tile(g.times(GF, f), n + 2 * (f - 1), m + 2 * (f - 1), par, f)
                    if more:
                        tile(g.times(GF, GF), n + 6, m + 6, 1 - par, 0)
                    k = 8 if more else 6
                    for c in range(4):
                        hi_next(n + (k + c), (S("acc_full"), m + (k + 2 * c + 2)))
                        if not more and c < 3:
                            rows(2 * l + 1, 2 * c)
                            rows(2 * l + 1, 2 * c + 1)

                act.wait_ge(S("x_lo_ready"), KD * (2 if l == 0 else 4))
                tile(At(0), At(n0), At(m0), 0, 0)
                with act.Fori(0, NG // 2 - 1) as i:
                    group(At(0, 2, i), 0, True)
                    group(At(1, 2, i), 1, True)
                group(At(NG - 2), 0, True)
                group(At(NG - 1), 1, False)

            ffn(0, N_F0, M_F0)
            norm(1)

            def y_out(j, u):
                m = j.times(2, M_RI)
                wait(act, S("acc_full"), m + 1)
                wait(act, S("r_ready"), j + (-2))
                nc.scalar.activation(halves(gate[:, u, :]), acc(m), ACT.Gelu_apprx_tanh).then_inc(S("gate_ready"), 1)
                hi_next(j.times(2, N_RI), (S("acc_full"), m + 1))

            def x_out(j):
                m, s = j.times(2, M_RI + 1), j.slot(3)
                wait(act, S("acc_full"), m + 1)
                wait(act, S("cx_tap"), j.times(5, -10))
                wait(act, S("xr_kept"), j + (-2))
                for src, t0, t1 in prompt_parts(2 * m.slot(2)):
                    nc.scalar.copy(xr[:, s, 3 + t0:3 + t1], src)
                seq = xr[:, s, 3 + TP:XRW].rearrange("p (b c) -> p b c", c=3 + TQ)
                src = ps[:, 2 * m.slot(2) + 1, TP - HT:HT].rearrange("p (b q) -> p b q", q=TQ)
                nc.scalar.copy(seq[:, :, 3:3 + TQ], src).then_inc(S("xr_ready"), 1)
                hi_next(j.times(2, N_RI + 1), (S("acc_full"), m + 1))

            def gates(j, u):
                tr, ti, aa = (w[:, u, :] for w in (tr3, ti3, aa3))
                wait(act, S("rg_full"), j + 1)
                col = lambda t, c: t[:, ds((j + c).v, 1)]
                nc.scalar.activation(halves(tr), bank_pair(4), ACT.Sigmoid, bias=col(prm, C_RBA)
                                     ).then_inc(S("gate_r_ready"), 1)
                nc.scalar.activation(halves(ti), bank_pair(6), ACT.Sigmoid, bias=col(prm, C_RBI)
                                     ).then_inc(S("rg_read"), 1)
                wait(act, S("gate_r_ready"), j + 1)
                nc.scalar.activation(aa, tr, ACT.Exp, scale=col(lru_a, 0))
                nc.scalar.activation(tr, tr, ACT.Tanh, scale=col(lru_t, 0)
                                     ).then_inc(S("tr_ready"), 1)
                wait(act, S("tr_ready"), j + 1)
                nc.scalar.activation(tr, tr, ACT.Sqrt, bias=cols[:, 1:2], scale=-1.0).then_inc(S("sq_ready"), 1)

            def r_out(j):
                wait(act, S("r_ready"), j + 1)
                nc.scalar.copy(r_hi[:, ds(j.v, 1), :].rearrange("p o t -> p (o t)"), uu[:]).then_inc(S("r_hi_ready"), 1)

            act.wait_ge(S("rows_stored"), 32)
            act.wait_ge(S("lru_ready"), 1)
            for j in range(2):
                y_out(At(j), j)
                x_out(At(j))
            with act.Fori(0, 3) as i:
                for u in range(3):
                    j = At(2 + u, 3, i)
                    y_out(j, (2 + u) % 3)
                    x_out(j)
                    gates(At(u, 3, i), u)
                    r_out(At(u, 3, i))
            hi_next(At(N_RO), (S("ro_full"), 1))
            gates(At(NR - 2), (NR - 2) % 3)
            gates(At(NR - 1), (NR - 1) % 3)
            hi_next(At(N_RO + 1), (S("ro_full"), 2))
            r_out(At(NR - 2))
            r_out(At(NR - 1))
            for c in range(2, 12):
                hi_next(At(N_RO + c), (S("ro_full"), c + 1))
            norm(2)
            act.wait_ge(S("rows_stored"), 16 * 6)
            ffn(1, N_F1, M_F1)
            norm(3)
            act.wait_ge(S("rows_stored"), 16 * 8)
            for half, t in [(0, t) for t in range(NQ + 1)] + [(1, t) for t in range(1, NQ + 1, 2)]:
                y_tile(act, nc.scalar.copy, half, t).then_inc(S("y_act"), 1)

        @block.vector
        def _(dve):
            link_n = [0]

            def link(ins):
                link_n[0] += 1
                ins.then_inc(S("dve_step"), 1)
                dve.wait_ge(S("dve_step"), link_n[0])

            def lo_next(n):
                if n.turn is not None or n.first + RING < N_END:
                    split_lo(dve, n + RING, width_of(n + RING))

            V = nc.vector

            def x_lo_tile(j):
                dve.wait_ge(S("x_hi_ready"), j + 1)
                dve.wait_ge(S("x_f_ready"), j + 1)
                V.tensor_tensor(x_lo[:, j, :], x_f[:, j, :], x_hi[:, j, :].bitcast(f32), ALU.subtract
                                ).then_inc(S("x_lo_ready"), 1)

            for j in range(KD):
                b = 4 + 2 * (j % 2)
                dve.wait_ge(S("x_staged"), j + 1)
                V.tensor_copy(x_f[:, j, 0:TP], ps[:, b, 0:TP])
                V.tensor_copy(x_f[:, j, TP:T], ps[:, b + 1, 0:TS]).then_inc(S("x_f_ready"), 1)
                if j:
                    x_lo_tile(j - 1)
            x_lo_tile(KD - 1)
            split_lo(dve, At(0))
            dve.wait_ge(S("f_full"), 1)
            dve.wait_ge(S("wf_in"), 32)
            V.tensor_scalar(halves(fz[:, 0, :]), ps[0:NH, 2:4, 0:HT], bf_col[:], None, ALU.add
                            ).then_inc(S("f_logits"), 1)
            for n in range(1, RING):
                split_lo(dve, At(n))

            def k_out(j):
                wait(dve, S("acc_full"), j.times(3, 1))
                wait(dve, S("qk_kept"), j.times(2, -2))
                V.tensor_copy(halves(k_sb[:, j.slot(2), :]), acc(j.times(3))).then_inc(S("k_ready"), 1)

            def log1p_half(s, r, s2, e):
                link(V.tensor_scalar(r, e, 2.0, None, ALU.add))
                link(V.reciprocal(r, r))
                link(V.tensor_tensor(s, e, r, ALU.mult))
                link(V.tensor_tensor(s2, s, s, ALU.mult))
                link(V.tensor_scalar(r, s2, 1.0 / 17, None, ALU.mult))
                for k in (15, 13, 11, 9, 7, 5, 3):
                    link(V.scalar_tensor_tensor(out=r, in0=r, scalar=1.0 / k, in1=s2, op0=ALU.add, op1=ALU.mult))
                link(V.scalar_tensor_tensor(out=r, in0=r, scalar=1.0, in1=s, op0=ALU.add, op1=ALU.mult))

            dve.wait_ge(S("masks_ready"), 1)
            dve.wait_ge(S("ft_full"), 1)
            V.tensor_copy(ft[:, 0, 0:NQ * NH], ps[:, 6, 0:NQ * NH])
            V.tensor_copy(ft[0:TS, 0, NQ * NH:], ps[0:TS, 6, NQ * NH:(NQ + 1) * NH]).then_inc(S("ft_ready"), 1)
            dve.wait_ge(S("f_exp"), 1)
            link(V.tensor_scalar(ft[:, 0, :], ft[:, 0, :], 0.0, None, ALU.min))
            log1p_half(ft[:, 3, :], ft[:, 2, :], ft[:, 4, :], ft[:, 1, :])
            V.scalar_tensor_tensor(out=lf_tok[:].rearrange("p t h -> p (t h)"), in0=ft[:, 2, :], scalar=-2.0,
                                   in1=ft[:, 0, :], op0=ALU.mult, op1=ALU.add).then_inc(S("lf_tok_ready"), 1)
            k_out(At(0))
            dve.wait_ge(S("lf_full"), 1)
            V.tensor_copy(fz[:, 1, 0:TP], ps[0:NH, 6, 0:TP])
            V.tensor_copy(fz[:, 1, TP:T], ps[0:NH, 7, 0:TS]).then_inc(S("lf_ready"), 1)
            dve.wait_ge(S("lf_ready"), 1)
            V.tensor_tensor_scan(out=fz[:, 2, 0:TP], data0=ones_s[0:NH, 0:TP], data1=fz[:, 1, 0:TP], initial=0.0,
                                 op0=ALU.mult, op1=ALU.subtract).then_inc(S("ncum_ready"), 1)

            def k_rows(j, part):
                wait(dve, S("t_full"), t_use(f"k{part}", j) + 1)
                if part == 0:
                    wait(dve, S("kv_stored"), j.times(64))
                    V.tensor_copy(k_tok[:].rearrange("p t e -> p (t e)"), ps[:, 6, 0:TP]).then_inc(S("t_free"), 1)
                else:
                    V.tensor_copy(k_new[:], ps[P - TS:P, 6, 0:P]).then_inc(S("t_free"), 1)

            def bias(p, s):
                g, hh, qt = p.times(8, s), s // 4, s % 4
                q = cumq[:, qt, ds(p.times(2, hh).v, 1)]
                bank, off = ps[:, 4 + s % 2, :], P * qt
                wait(dve, S("sc_full"), g + 1)
                wait(dve, S("ncb_ready"), p.times(2, hh + 1))
                wait(dve, S("probs"), g + (-1 if s else 0))
                if qt:
                    V.scalar_tensor_tensor(out=sc[:, s % 2, 0:off], in0=bank[:, 0:off], scalar=q,
                                           in1=ncb[:, hh, 0:off], op0=ALU.add, op1=ALU.add)
                V.scalar_tensor_tensor(out=sc[:, s % 2, off:off + P], in0=bank[:, off:off + P], scalar=q,
                                       in1=ncbm[:, hh, off:off + P], op0=ALU.add, op1=ALU.add).then_inc(S("biased"), 1)
                wait(dve, S("biased"), g + 1)
                V.tensor_reduce(out=sm[:, 0, s % 2:s % 2 + 1], in_=sc[:, s % 2, 0:off + P], axis=AX.X, op=ALU.max,
                                negate=True).then_inc(S("row_max"), 1)

            def normalize(p, s):
                g, w = p.times(8, s), P * (s % 4 + 1)
                wait(dve, S("probs"), g + 1)
                V.reciprocal(sm[:, 2, s % 2:s % 2 + 1], sm[:, 1, s % 2:s % 2 + 1]).then_inc(S("row_inv"), 1)
                wait(dve, S("row_inv"), g + 1)
                V.tensor_scalar(pr[:, s % 2, 0:w], pr[:, s % 2, 0:w], sm[:, 2, s % 2:s % 2 + 1], None, ALU.mult
                                ).then_inc(S("pr_norm"), 1)

            def o_out(p):
                wait(dve, S("o_hi_ready"), p + 1)
                r = "p o t -> p (o t)"
                V.tensor_tensor(o_lo[:, ds(p.v, 1), 0:TP].rearrange(r), ps[:, 7, 0:TP],
                                o_hi[:, ds(p.v, 1), 0:TP].rearrange(r).bitcast(f32), ALU.subtract
                                ).then_inc(S("o_lo_ready"), 1)

            lo_next(At(0))
            k_rows(At(0), 0)
            k_rows(At(0), 1)
            lo_next(At(1))
            link(V.tensor_reduce(out=sc[:, 1, 0:TQ], in_=causal_w[:].rearrange("p h k -> p k h"), axis=AX.X, op=ALU.max))
            link(V.tensor_copy(new_mask[:].rearrange("p (b c) -> p b c", c=72)[:, :, 0:TQ],
                               sc[:, 1, 0:TQ].rearrange("p (o k) -> p o k", o=1).broadcast_to([P, NB, TQ])))
            dve.wait_ge(S("cumq_ready"), 1)

            def pair(j, p):
                bias(p, 0)
                normalize(p, 0)
                bias(p, 1)
                if p.turn is not None or p.first:
                    o_out(p + (-1))
                normalize(p, 1)
                bias(p, 2)
                lo_next((j + (-1)).times(3, 2))
                normalize(p, 2)
                bias(p, 3)
                k_out(j)
                normalize(p, 3)
                bias(p, 4)
                k_rows(j, 0)
                normalize(p, 4)
                lo_next(j.times(3))
                bias(p, 5)
                k_rows(j, 1)
                normalize(p, 5)
                bias(p, 6)
                normalize(p, 6)
                bias(p, 7)
                lo_next(j.times(3, 1))
                normalize(p, 7)

            pair(At(1), At(0))
            with dve.Fori(0, NPAIR // 2 - 1) as i:
                pair(At(2, 2, i), At(1, 2, i))
                pair(At(3, 2, i), At(2, 2, i))
            p = At(NPAIR - 1)
            bias(p, 0)
            for s in range(8):
                if s < 7:
                    bias(p, s + 1)
                normalize(p, s)
                if s == 0:
                    o_out(p + (-1))
                if s == 2:
                    lo_next(At(3 * NPAIR - 1))
            o_out(p)

            dve.wait_ge(S("t_full"), T_LAST + 9)
            dve.wait_ge(S("lf_new_in"), 16 * NB)
            link(V.tensor_copy(lf_s[:, 0:PAST], ps[:, 6, 0:PAST]))
            link(V.tensor_tensor_scan(out=nc_s[:], data0=ones_s[:], data1=lf_s[:], initial=0.0,
                                      op0=ALU.mult, op1=ALU.subtract))
            V.tensor_tensor(cq_w[:], head_of[:],
                            nc_s[:, PAST:PAST + TQ].rearrange("p (o k) -> p o k", o=1).broadcast_to([P, NH, TQ]),
                            ALU.mult).then_inc(S("cq_w_ready"), 1)

            def e_batch(b):
                wait(dve, S("s_full"), b + (-1))
                V.tensor_scalar(e_b[:, b.slot(2), :], head_of[:].rearrange("p h q -> p (h q)"),
                                batch_of[:, ds(b.v, 1)], None, ALU.mult).then_inc(S("e_b_ready"), 1)

            def kT_odd(b, beside=None):
                for j in range(1, KD, 2):
                    if j == 3 and beside:
                        beside()
                    wait(dve, S("kT_full"), b.times(KD, j + 1))
                    wait(dve, S("kT_used"), b.times(KD, j - 1))
                    V.tensor_copy(kT[:, 1, :], ps[:, 5, 0:PAST]).then_inc(S("kT_odd"), 1)

            def s_bias(b):
                s = b.slot(2)
                q = cq_s[:, ds(b.v, 1)]
                wait(dve, S("s_full"), b + 1)
                wait(dve, S("psT_full"), b + (-1))
                V.tensor_scalar(ss[:, s, 0:PAST], ps[:, 2 * s, 0:PAST], q, None, ALU.add)
                V.scalar_tensor_tensor(out=ss[:, s, PAST:SW], in0=ps[:, 2 * s + 1, 0:TS], scalar=q,
                                       in1=new_mask[:, ds(b.times(TS).v, TS)], op0=ALU.add, op1=ALU.add
                                       ).then_inc(S("s_biased"), 1)
                wait(dve, S("s_biased"), b + 1)
                V.tensor_reduce(out=sms[:, 0, s:s + 1], in_=ss[:, s, :], axis=AX.X, op=ALU.max, negate=True
                                ).then_inc(S("s_max"), 1)

            def s_normalize(b):
                s = b.slot(2)
                wait(dve, S("s_probs"), b + 1)
                V.reciprocal(sms[:, 2, s:s + 1], sms[:, 1, s:s + 1]).then_inc(S("s_inv"), 1)
                wait(dve, S("s_inv"), b + 1)
                V.tensor_scalar(ss[:, s, :], ss[:, s, :], sms[:, 2, s:s + 1], None, ALU.mult).then_inc(S("ps_norm"), 1)

            def s_own(b):
                wait(dve, S("pv_s_done"), b + 1)
                wait(dve, S("os_full"), b)
                own = own_head[:].rearrange("p (h o) -> p h o", o=1).broadcast_to([P, NH, HD])
                V.tensor_tensor(o_own[:].rearrange("p (h d) -> p h d", d=HD),
                                ps[:, 2 * b.slot(2):2 * b.slot(2) + 2, :].rearrange("p a (h d) -> p (a h) d", d=HD),
                                own, ALU.mult).then_inc(S("o_own_ready"), 1)

            def s_out(b):
                wait(dve, S("os_hi"), b + 1)
                o = ds(b.times(TQ, TP).v, TQ)
                V.tensor_tensor(o_lo[:, :, o], ps[:, 7, 0:KD * TQ].rearrange("p (j q) -> p j q", q=TQ),
                                o_hi[:, :, o].bitcast(f32), ALU.subtract).then_inc(S("os_lo"), 1)

            V.tensor_reduce(out=q_of[:], in_=ident[:].rearrange("p (h q) -> p q h", q=TQ), axis=AX.X, op=ALU.add)
            e_batch(At(0))
            kT_odd(At(0))
            dve.wait_ge(S("cq_s_ready"), 1)
            s_bias(At(0))

            def sample(b, c, o, beside=None):
                e_batch(b)
                kT_odd(b, beside)
                if o is not None:
                    s_out(o)
                s_bias(b)
                s_normalize(b)
                s_own(c)

            sample(At(1), At(0), None, lambda: s_normalize(At(0)))
            with dve.Fori(0, NB // 2 - 1) as i:
                sample(At(2, 2, i), At(1, 2, i), At(0, 2, i))
                sample(At(3, 2, i), At(2, 2, i), At(1, 2, i))
            s_own(At(NB - 1))
            s_out(At(NB - 2))
            s_out(At(NB - 1))

            def add_z(sem, full, src, j, z):
                wait(dve, sem, full)
                wait(dve, S("z_added"), z + (1 - KD))
                V.tensor_tensor(halves(x_f[:, j, :]), halves(x_f[:, j, :]), src, ALU.add).then_inc(S("z_added"), 1)

            dve.wait_ge(S("x_scaled"), KD)
            for j in range(KD):
                m = At(M_AO + j)
                add_z(S("acc_full"), m + 1, acc(m), j, At(Z_AO + j))
                lo_next(At(N_AO + j))

            def norm(k):
                b = LN_BANK[k]
                rs = (ln_f, ln_f, ln_r, ln_f)[k][1]
                dve.wait_ge(S("ln_mean"), k + 1)
                for j in range(KD):
                    V.tensor_tensor(halves(x_f[:, j, :]), halves(x_f[:, j, :]), bank_pair(b), ALU.subtract
                                    ).then_inc(S("ln_centred"), 1)
                dve.wait_ge(S("ln_std"), k + 1)
                V.reciprocal(rs[:, 1, :], rs[:, 0, :]).then_inc(S("ln_rstd"), 1)
                dve.wait_ge(S("ln_rstd"), k + 1)
                column = lambda c, j: prm[:, c + KD * k + j:c + KD * k + j + 1]

                def low(j):
                    dve.wait_ge(S("x_hi_ready"), KD * (k + 1) + j + 1)
                    V.scalar_tensor_tensor(out=x_lo[:, j, :], in0=x_f[:, j, :], scalar=column(C_LNB, j),
                                           in1=x_hi[:, j, :].bitcast(f32), op0=ALU.add, op1=ALU.subtract
                                           ).then_inc(S("x_lo_ready"), 1)

                for j in range(KD):
                    V.scalar_tensor_tensor(out=x_f[:, j, :], in0=x_f[:, j, :], scalar=column(C_LNG, j), in1=rs[:, 1, :],
                                           op0=ALU.mult, op1=ALU.mult).then_inc(S("ln_scaled"), 1)
                    if k < 3 and j:
                        low(j - 1)
                if k < 3:
                    low(KD - 1)

            norm(0)

            def recurrence_constants():
                dve.wait_ge(S("lam_exp"), 1)
                w = [lru_w[:, i, :] for i in range(3)]
                log1p_half(w[0], w[1], w[2], lru_t[:])
                lam = prm[:, C_LAM:C_LAM + NR]
                link(V.tensor_scalar(w[0], lam, -1.0, 0.0, ALU.mult, ALU.max))
                link(V.scalar_tensor_tensor(out=w[1], in0=w[1], scalar=2.0, in1=w[0], op0=ALU.mult, op1=ALU.add))
                link(V.tensor_scalar(lru_t[:], w[1], -4.0, None, ALU.mult))
                V.tensor_scalar(lru_a[:], w[1], -8.0, None, ALU.mult).then_inc(S("lru_ready"), 1)

            def ffn(l, n0, m0, z0):
                def tile(F, n, m, par, f):
                    Fg = F + NF * l
                    s = F.slot(2)
                    lo_next(n)
                    col = lambda c: prm[:, ds((F + c).v, 1)]
                    wait(dve, S("gh_ready"), Fg + 1)
                    wait(dve, S("gh_hist"), Fg + 1)
                    wait(dve, S("gelu_ready"), Fg)
                    V.tensor_scalar(cv[:], gh[:, s, 0:CVW], col(C_FCW[l]), col(C_FCB + NF * l), ALU.mult, ALU.add
                                    ).then_inc(S("cv_tap"), 1)
                    for t in (1, 2):
                        wait(dve, S("cv_tap"), Fg.times(3, t))
                        V.scalar_tensor_tensor(out=cv[:], in0=gh[:, s, t:t + CVW], scalar=col(C_FCW[l] + NF * t),
                                               in1=cv[:], op0=ALU.mult, op1=ALU.add).then_inc(S("cv_tap"), 1)
                    wait(dve, S("acc_full"), m + 2)
                    wait(dve, S("gelu_ready"), Fg + 1)
                    wait(dve, S("h_hi_ready"), Fg)
                    for src, t0, t1 in prompt_parts(2 * (m + 1).slot(2)):
                        V.tensor_tensor(hf[:, t0:t1], gl[:, t0:t1], src, ALU.mult)
                    src = ps[:, 2 * (m + 1).slot(2) + 1, TP - HT:HT].rearrange("p (b q) -> p b q", q=TQ)
                    V.tensor_tensor(hf[:, TP:T].rearrange("p (b q) -> p b q", q=TQ), strided(gl, TP + 2, 2 + TQ), src,
                                    ALU.mult).then_inc(S("h_ready"), 1)
                    lo_next(n + 1)
                    wait(dve, S("h_hi_ready"), Fg + 1)
                    V.tensor_tensor(h_lo[:, par, f, :], hf[:], h_hi[:, par, f, :].bitcast(f32), ALU.subtract
                                    ).then_inc(S("h_lo_ready"), 1)

                def group(g, par, more):
                    n, m = g.times(12, n0 + 2), g.times(16, m0 + 2)
                    for f in range(1, GF):
                        tile(g.times(GF, f), n + 2 * (f - 1), m + 2 * (f - 1), par, f)
                    if more:
                        tile(g.times(GF, GF), n + 6, m + 6, 1 - par, 0)
                    k = 8 if more else 6
                    for c in range(4):
                        for d in (2 * c, 2 * c + 1):
                            add_z(S("acc_full"), m + (k + d + 1), acc(m + (k + d)), d, g.times(KD, z0 + d))
                        lo_next(n + (k + c))

                dve.wait_ge(S("gh_zero"), l + 1)
                tile(At(0), At(n0), At(m0), 0, 0)
                if l == 0:
                    recurrence_constants()
                dve.wait_ge(S("x_scaled"), KD * (2 if l == 0 else 4))
                with dve.Fori(0, NG // 2 - 1) as i:
                    group(At(0, 2, i), 0, True)
                    group(At(1, 2, i), 1, True)
                group(At(NG - 2), 0, True)
                group(At(NG - 1), 1, False)

            ffn(0, N_F0, M_F0, Z_F0)
            norm(1)

            def convolve(j):
                s, u = j.slot(3), j.slot(3)
                col = lambda c: prm[:, ds((j + c).v, 1)]
                wait(dve, S("xr_ready"), j + 1)
                wait(dve, S("xr_hist"), j + 1)
                wait(dve, S("cx_tap"), j.times(5))
                V.tensor_scalar(cx[:, 0:CXW], xr[:, s, 0:CXW], col(C_RCW), col(C_RCB), ALU.mult, ALU.add).then_inc(S("cx_tap"), 1)
                for t in (1, 2):
                    wait(dve, S("cx_tap"), j.times(5, t))
                    V.scalar_tensor_tensor(out=cx[:, 0:CXW], in0=xr[:, s, t:t + CXW], scalar=col(C_RCW + NR * t), in1=cx[:, 0:CXW],
                                           op0=ALU.mult, op1=ALU.add).then_inc(S("cx_tap"), 1)
                wait(dve, S("cx_tap"), j.times(5, 3))
                if j.turn is not None or j.first >= 2:
                    wait(dve, S("rg_full"), j + (-1))
                c3 = col(C_RCW + 3 * NR)
                V.scalar_tensor_tensor(out=xc[:, u, 0:TP], in0=xr[:, s, 3:3 + TP], scalar=c3, in1=cx[:, 0:TP],
                                       op0=ALU.mult, op1=ALU.add).then_inc(S("cx_tap"), 1)
                seq = xr[:, s, 3 + TP:XRW].rearrange("p (b c) -> p b c", c=3 + TQ)
                V.scalar_tensor_tensor(out=xc[:, u, TP:T].rearrange("p (b q) -> p b q", q=TQ), in0=seq[:, :, 3:3 + TQ],
                                       scalar=c3, in1=strided(cx, TP + 3, 3 + TQ), op0=ALU.mult, op1=ALU.add
                                       ).then_inc(S("cx_tap"), 1)

            STEPS = 7

            def recur(j, u):
                tr, ti, aa = (w[:, u, :] for w in (tr3, ti3, aa3))

                def step(k, ins):
                    ins.then_inc(S("r_step"), 1)
                    wait(dve, S("r_step"), j.times(STEPS, k))

                first = lambda x: x[:, TP:T].rearrange("p (b q) -> p b q", q=TQ)[:, :, 0]
                wait(dve, S("rg_read"), j + 1)
                wait(dve, S("r_lo_ready"), j)
                step(1, V.tensor_tensor(uu[:], ti, xc[:, u, :], ALU.mult))
                wait(dve, S("sq_ready"), j + 1)
                step(2, V.scalar_tensor_tensor(out=tr, in0=aa, scalar=1.0, in1=tr, op0=ALU.add, op1=ALU.mult))
                step(3, V.tensor_tensor(uu[:], uu[:], tr, ALU.mult))
                h0 = hist_r[:, ds(j.v, 1), 24:32].rearrange("p o b -> p (o b)")
                step(4, V.tensor_tensor(tr[:, 0:NB], first(aa), h0, ALU.mult))
                step(5, V.tensor_tensor(first(uu), first(uu), tr[:, 0:NB], ALU.add))
                step(6, V.memset(first(aa), 0.0))
                step(7, V.tensor_tensor_scan(out=ti, data0=aa, data1=uu[:], initial=0.0, op0=ALU.mult, op1=ALU.add))
                V.tensor_copy(r_st[:, ds(j.v, 1), 27:28].rearrange("p o c -> p (o c)"), ti[:, TP - 1:TP])
                V.tensor_copy(r_st[:, ds(j.v, 1), 28:36].rearrange("p o c -> p (o c)"),
                              ti[:, TP:T].rearrange("p (b q) -> p b q", q=TQ)[:, :, TQ - 1]).then_inc(S("h_kept"), 1)
                V.tensor_tensor(uu[:], ti, gate[:, u, :], ALU.mult).then_inc(S("r_ready"), 1)

            def r_low(j):
                r = "p o t -> p (o t)"
                wait(dve, S("r_hi_ready"), j + 1)
                V.tensor_tensor(r_lo[:, ds(j.v, 1), :].rearrange(r), uu[:],
                                r_hi[:, ds(j.v, 1), :].rearrange(r).bitcast(f32), ALU.subtract).then_inc(S("r_lo_ready"), 1)

            dve.wait_ge(S("rows_stored"), 32)
            dve.wait_ge(S("xr_zero"), 1)
            for j in range(2):
                lo_next(At(N_RI + 2 * j))
                lo_next(At(N_RI + 2 * j + 1))
                convolve(At(j))
            with dve.Fori(0, 3) as i:
                for u in range(3):
                    j = At(2 + u, 3, i)
                    lo_next(j.times(2, N_RI))
                    lo_next(j.times(2, N_RI + 1))
                    convolve(j)
                    recur(At(u, 3, i), u)
                    r_low(At(u, 3, i))
            lo_next(At(N_RO))
            for j in (NR - 2, NR - 1):
                recur(At(j), j % 3)
                r_low(At(j))
            dve.wait_ge(S("x_scaled"), 3 * KD)
            for i, (q, c) in enumerate(RO_ORDER):
                if c == 2:
                    for d in range(2):
                        add_z(S("ro_full"), i + 1, bank_pair(4 * (q % 2) + 2 * d), 2 * q + d, At(Z_RO + 2 * q + d))
                if i:
                    lo_next(At(N_RO + i))
            norm(2)
            dve.wait_ge(S("rows_stored"), 16 * 6)
            ffn(1, N_F1, M_F1, Z_F1)
            norm(3)
            dve.wait_ge(S("rows_stored"), 16 * 8)
            for t in range(0, NQ + 1, 2):
                y_tile(dve, V.tensor_copy, 1, t).then_inc(S("y_dve"), 1)


INPUTS = ["x_prompt", "x_sample", "cache_k", "cache_v", "cache_logf", "page_table", "state_rglru_h",
          "state_rglru_conv", "state_ffn_conv", "ln_g", "ln_b", "w_attn_in", "b_forget", "w_attn_out", "w_rnn_in",
          "rnn_conv_w", "rnn_conv_b", "w_rg_a", "b_rg_a", "w_rg_i", "b_rg_i", "rg_lambda", "w_rnn_out",
          "w_ffn_in", "ffn_conv_w", "ffn_conv_b", "w_ffn_out"]
OUTPUTS = [("y_prompt", (1, TP, D)), ("y_sample", (NB, TQ, D)), ("k_prompt", (1, TP, 1, NH, HD)),
           ("v_prompt", (1, TP, 1, NH, HD)), ("logf_prompt", (1, TP, 1, NH)), ("k_sample", (NB, TQ, 1, NH, HD)),
           ("v_sample", (NB, TQ, 1, NH, HD)), ("logf_sample", (NB, TQ, 1, NH)), ("h_prompt", (1, 1, R)),
           ("h_sample", (1, NB, R)), ("rconv_prompt", (1, 1, 3, R)), ("rconv_sample", (1, NB, 3, R)),
           ("fconv_prompt", (2, 1, 2, FF)), ("fconv_sample", (2, NB, 2, FF))]


def kernel(**inputs):
    import numpy as np
    import concourse.bacc as bacc
    from concourse.bass_utils import run_bass_kernel_spmd

    nc = bacc.Bacc("TRN2", target_bir_lowering=False, num_devices=1)
    arrays, args = {}, {}
    for name in INPUTS:
        arr = np.ascontiguousarray(inputs[name])
        arrays["in_" + name] = arr
        args[name] = nc.dram_tensor("in_" + name, arr.shape, mybir.dt.from_np(arr.dtype), kind="ExternalInput").ap()
    for name, shape in OUTPUTS:
        args[name] = nc.dram_tensor("out_" + name, shape, mybir.dt.float32, kind="ExternalOutput").ap()
    build(nc, args)
    r = run_bass_kernel_spmd(nc, [arrays], core_ids=[0])
    return tuple(r.results[0]["out_" + name] for name, _ in OUTPUTS)
```
